# Optimizing a Trainium2 kernel written in Bass

```python
import jax, jax.numpy as jnp
from jax import lax
import numpy as np

D_MODEL = 1024
BATCH = 1
SEQ = 256
DEPTH = 2

N_MEM = 256
D_MIX = D_MODEL
HGRN_DK = 128
HGRN_DV = 128
HGRN_WIDTH = D_MIX // 2
HGRN_HEADS = HGRN_WIDTH // HGRN_DV
HGRN_KW = HGRN_HEADS * HGRN_DK
FOX_DH = 64
FOX_WIDTH = D_MIX - HGRN_WIDTH
FOX_HEADS = FOX_WIDTH // FOX_DH
CHUNK = 64
Q_BLOCK = 128
D_FF = 2816
CROSS_HEADS = 4
CROSS_DH = D_MODEL // CROSS_HEADS
EPS = 1e-6
N_IN = 2 * HGRN_KW + 2 * HGRN_WIDTH + 3 * FOX_WIDTH + FOX_HEADS


def rms_norm(x, w):
    x32 = x.astype(jnp.float32)
    y = x32 * lax.rsqrt(jnp.mean(x32 * x32, axis=-1, keepdims=True) + EPS)
    return (y * w.astype(jnp.float32)).astype(x.dtype)

def swiglu(h, w_gate, w_up, w_down):
    return (jax.nn.silu(h @ w_gate) * (h @ w_up)) @ w_down

def hgrn2_chunk_scan(q, k, v, logf):
    B, H, S, DK = q.shape
    DV = v.shape[-1]
    nc = S // CHUNK

    def to_chunks(t):
        return t.reshape(B, H, nc, CHUNK, t.shape[-1]).transpose(2, 0, 1, 3, 4)

    qc, kc, vc = to_chunks(q), to_chunks(k), to_chunks(v)
    gc = jnp.cumsum(to_chunks(logf), axis=-2)
    mask = jnp.tril(jnp.ones((CHUNK, CHUNK), dtype=bool))[None, None, :, :, None]

    def step(state, inp):
        q_, k_, v_, g_ = inp
        o_inter = jnp.einsum('bhtk,bhkv->bhtv', q_ * jnp.exp(g_), state)
        diff = g_[:, :, :, None, :] - g_[:, :, None, :, :]
        decay = jnp.exp(jnp.where(mask, diff, -jnp.inf))
        a = jnp.einsum('bhtk,bhsk,bhtsk->bhts', q_, k_, decay)
        o = o_inter + jnp.einsum('bhts,bhsv->bhtv', a, v_)
        g_last = g_[:, :, -1:, :]
        new_state = jnp.exp(g_last[:, :, 0, :])[..., None] * state + jnp.einsum(
            'bhsk,bhsv->bhkv', k_ * jnp.exp(g_last - g_), v_)
        return new_state, o

    s0 = jnp.zeros((B, H, DK, DV), jnp.float32)
    _, oc = lax.scan(step, s0, (qc, kc, vc, gc))
    return oc.transpose(1, 2, 0, 3, 4).reshape(B, H, S, DV)

def forgetting_attention(q, k, v, logf):
    B, H, S, dh = q.shape
    nb = S // Q_BLOCK
    c = jnp.cumsum(logf, axis=-1)
    qb = q.reshape(B, H, nb, Q_BLOCK, dh).transpose(2, 0, 1, 3, 4)
    cb = c.reshape(B, H, nb, Q_BLOCK).transpose(2, 0, 1, 3)
    kpos = jnp.arange(S)
    scale = dh ** -0.5

    def block(args):
        q_blk, c_blk, i = args
        s = jnp.einsum('bhqd,bhkd->bhqk', q_blk, k).astype(jnp.float32) * scale
        s = s + (c_blk[..., :, None] - c[:, :, None, :])
        qpos = i * Q_BLOCK + jnp.arange(Q_BLOCK)
        s = jnp.where(kpos[None, :] <= qpos[:, None], s, -jnp.inf)
        p = jax.nn.softmax(s, axis=-1)
        return jnp.einsum('bhqk,bhkd->bhqd', p.astype(v.dtype), v)

    ob = lax.map(block, (qb, cb, jnp.arange(nb)))
    return ob.transpose(1, 2, 0, 3, 4).reshape(B, H, S, dh)

def hybrid_mixer(h, w_in, lb, out_norm_w, fox_bf, w_out):
    B, S, _ = h.shape
    sizes = [HGRN_KW, HGRN_KW, HGRN_WIDTH, HGRN_WIDTH, FOX_WIDTH, FOX_WIDTH, FOX_WIDTH]
    offsets = [int(o) for o in np.cumsum(sizes)]
    z = h @ w_in
    hq, hf, hi, hg, fq, fk, fv, ff = jnp.split(z, offsets, axis=-1)

    def heads(t, n):
        return t.reshape(B, S, n, -1).transpose(0, 2, 1, 3)

    zf = hf.astype(jnp.float32)
    lb32 = lb.astype(jnp.float32)
    logf_h = jnp.logaddexp(jnp.log(lb32), jnp.log1p(-lb32) + jax.nn.log_sigmoid(zf))
    k_h = (1.0 - lb32) * jax.nn.sigmoid(-zf)
    q_h = jax.nn.silu(hq.astype(jnp.float32))
    o_h = hgrn2_chunk_scan(heads(q_h, HGRN_HEADS), heads(k_h, HGRN_HEADS),
                           heads(hi.astype(jnp.float32), HGRN_HEADS),
                           heads(logf_h, HGRN_HEADS))
    o_h = rms_norm(o_h.transpose(0, 2, 1, 3), out_norm_w).reshape(B, S, HGRN_WIDTH)
    o_h = o_h * jax.nn.silu(hg.astype(jnp.float32))

    logf_f = jax.nn.log_sigmoid(ff.astype(jnp.float32) + fox_bf.astype(jnp.float32))
    o_f = forgetting_attention(heads(fq, FOX_HEADS), heads(fk, FOX_HEADS),
                               heads(fv, FOX_HEADS), logf_f.transpose(0, 2, 1))
    o_f = o_f.transpose(0, 2, 1, 3).reshape(B, S, FOX_WIDTH)

    o = jnp.concatenate([o_h.astype(h.dtype), o_f.astype(h.dtype)], axis=-1)
    return o @ w_out

def memory_cross_attention(h, m, wq, wk, wv, wo):
    B, S, _ = h.shape
    M = m.shape[1]
    q = (h @ wq).reshape(B, S, CROSS_HEADS, CROSS_DH)
    k = (m @ wk).reshape(B, M, CROSS_HEADS, CROSS_DH)
    v = (m @ wv).reshape(B, M, CROSS_HEADS, CROSS_DH)
    s = jnp.einsum('bshd,bmhd->bhsm', q, k).astype(jnp.float32) * (CROSS_DH ** -0.5)
    p = jax.nn.softmax(s, axis=-1).astype(h.dtype)
    o = jnp.einsum('bhsm,bmhd->bshd', p, v).reshape(B, S, D_MODEL)
    return o @ wo

def first_inputs(seed: int = 0) -> dict:
    key = jax.random.key(seed)
    ks = jax.random.split(key, 24)
    n = jax.random.normal
    f32 = jnp.float32

    def w(k, shape, fan_in):
        return n(k, shape, f32) * fan_in ** -0.5

    def gain(k, shape):
        return 1.0 + 0.05 * n(k, shape, f32)

    return {
        "x": n(ks[0], (BATCH, SEQ, D_MODEL), f32),
        "mem": n(ks[1], (BATCH, N_MEM, D_MODEL), f32),
        "ffn1_norm": gain(ks[2], (DEPTH, D_MODEL)),
        "ffn1_w_gate": w(ks[3], (DEPTH, D_MODEL, D_FF), D_MODEL),
        "ffn1_w_up": w(ks[4], (DEPTH, D_MODEL, D_FF), D_MODEL),
        "ffn1_w_down": w(ks[5], (DEPTH, D_FF, D_MODEL), D_FF),
        "mix_norm": gain(ks[6], (DEPTH, D_MODEL)),
        "w_in": w(ks[7], (DEPTH, D_MODEL, N_IN), D_MODEL),
        "hgrn_lb": n(ks[8], (DEPTH, HGRN_KW), f32),
        "hgrn_out_norm": gain(ks[9], (DEPTH, HGRN_DV)),
        "fox_f_bias": 2.0 + 0.5 * n(ks[10], (DEPTH, FOX_HEADS), f32),
        "w_out": w(ks[11], (DEPTH, D_MIX, D_MODEL), D_MIX),
        "cross_norm": gain(ks[12], (DEPTH, D_MODEL)),
        "mem_norm": gain(ks[13], (DEPTH, D_MODEL)),
        "cross_wq": w(ks[14], (DEPTH, D_MODEL, D_MODEL), D_MODEL),
        "cross_wk": w(ks[15], (DEPTH, D_MODEL, D_MODEL), D_MODEL),
        "cross_wv": w(ks[16], (DEPTH, D_MODEL, D_MODEL), D_MODEL),
        "cross_wo": w(ks[17], (DEPTH, D_MODEL, D_MODEL), D_MODEL),
        "ffn2_norm": gain(ks[18], (DEPTH, D_MODEL)),
        "ffn2_w_gate": w(ks[19], (DEPTH, D_MODEL, D_FF), D_MODEL),
        "ffn2_w_up": w(ks[20], (DEPTH, D_MODEL, D_FF), D_MODEL),
        "ffn2_w_down": w(ks[21], (DEPTH, D_FF, D_MODEL), D_FF),
        "final_norm": gain(ks[22], (D_MODEL,)),
    }

def first_block(x, mem, ffn1_norm, ffn1_w_gate, ffn1_w_up, ffn1_w_down, mix_norm, w_in,
              hgrn_lb, hgrn_out_norm, fox_f_bias, w_out, cross_norm, mem_norm,
              cross_wq, cross_wk, cross_wv, cross_wo, ffn2_norm, ffn2_w_gate,
              ffn2_w_up, ffn2_w_down, final_norm):
    lb_cum = jnp.cumsum(jax.nn.softmax(hgrn_lb.astype(jnp.float32), axis=0), axis=0)
    lb_all = lb_cum - lb_cum[0:1]
    for l in range(DEPTH):
        x = x + 0.5 * swiglu(rms_norm(x, ffn1_norm[l]), ffn1_w_gate[l], ffn1_w_up[l], ffn1_w_down[l])
        x = x + hybrid_mixer(rms_norm(x, mix_norm[l]), w_in[l], lb_all[l], hgrn_out_norm[l],
                             fox_f_bias[l], w_out[l])
        x = x + memory_cross_attention(rms_norm(x, cross_norm[l]), rms_norm(mem, mem_norm[l]),
                                       cross_wq[l], cross_wk[l], cross_wv[l], cross_wo[l])
        x = x + 0.5 * swiglu(rms_norm(x, ffn2_norm[l]), ffn2_w_gate[l], ffn2_w_up[l], ffn2_w_down[l])
    return rms_norm(x, final_norm)


SB_HEADS = 4
SB_HEAD_DIM = 64
RET_HEADS = 4
RET_QK_DIM = 64
RET_V_DIM = 128
RET_CHUNK = 128
ROPE_BASE = 10000.0
POOL_GROUPS = 4
POOL_GROUP_DIM = 64
POOL_WINDOWS = (2, 4, 8, 16)
N_BRANCHES = 3

SB_W = SB_HEADS * SB_HEAD_DIM
RET_QK_W = RET_HEADS * RET_QK_DIM
RET_V_W = RET_HEADS * RET_V_DIM
POOL_W = POOL_GROUPS * POOL_GROUP_DIM
SPLITS = (SB_W, SB_W, SB_W, RET_QK_W, RET_QK_W, RET_V_W, RET_V_W, POOL_W, N_BRANCHES * D_MODEL)
D_IN = SB_W * 3 + RET_QK_W * 2 + RET_V_W * 2 + POOL_W + N_BRANCHES * D_MODEL


def rmsnorm(x, g):
    xf = x.astype(jnp.float32)
    y = xf * lax.rsqrt(jnp.mean(xf * xf, axis=-1, keepdims=True) + EPS)
    return (y * g.astype(jnp.float32)).astype(x.dtype)

def swiglu_half(h, w1, w3, w2):
    return 0.5 * ((jax.nn.silu(h @ w1) * (h @ w3)) @ w2)

def stick_breaking_attention(q, k, v):
    B, S, H, dh = q.shape
    qf = (q.astype(jnp.float32) * (dh ** -0.5)).transpose(0, 2, 1, 3)
    kf = k.astype(jnp.float32).transpose(0, 2, 1, 3)
    vf = v.astype(jnp.float32).transpose(0, 2, 1, 3)
    nb = S // Q_BLOCK
    q_blocks = qf.reshape(B, H, nb, Q_BLOCK, dh).transpose(2, 0, 1, 3, 4)
    key_pos = jnp.arange(S)

    def block(args):
        qb, start = args
        z = jnp.einsum('bhqd,bhkd->bhqk', qb, kf)
        q_pos = start + jnp.arange(Q_BLOCK)
        mask = key_pos[None, :] < q_pos[:, None]
        log_beta = jax.nn.log_sigmoid(z)
        log_fail = jnp.where(mask, log_beta - z, 0.0)
        after = lax.cumsum(log_fail, axis=3, reverse=True) - log_fail
        w = jnp.where(mask, jnp.exp(log_beta + after), 0.0)
        return jnp.einsum('bhqk,bhkd->bhqd', w, vf)

    out = lax.map(block, (q_blocks, jnp.arange(nb) * Q_BLOCK))
    return out.transpose(1, 0, 3, 2, 4).reshape(B, S, H * dh)

def rotary(x, cos, sin):
    half = x.shape[-1] // 2
    x1, x2 = x[..., :half], x[..., half:]
    c = cos[None, :, None, :]
    s = sin[None, :, None, :]
    return jnp.concatenate([x1 * c - x2 * s, x2 * c + x1 * s], axis=-1)

def retention(q, k, v, g):
    B, S, H, dk = q.shape
    dv = v.shape[-1]
    half = dk // 2
    pos = jnp.arange(S, dtype=jnp.float32)
    inv_freq = ROPE_BASE ** (-jnp.arange(half, dtype=jnp.float32) / half)
    ang = pos[:, None] * inv_freq[None, :]
    cos, sin = jnp.cos(ang), jnp.sin(ang)
    qf = rotary(q.astype(jnp.float32), cos, sin)
    kf = rotary(k.astype(jnp.float32), cos, sin) * (dk ** -0.5)
    vf = v.astype(jnp.float32)
    log_gamma = jnp.log(1.0 - 2.0 ** (-5.0 - jnp.arange(H, dtype=jnp.float32)))

    C = RET_CHUNK
    N = S // C
    qc = qf.reshape(B, N, C, H, dk)
    kc = kf.reshape(B, N, C, H, dk)
    vc = vf.reshape(B, N, C, H, dv)
    idx = jnp.arange(C, dtype=jnp.float32)
    diff = idx[:, None] - idx[None, :]
    causal = diff >= 0
    decay = jnp.where(causal[None], jnp.exp(jnp.where(causal, diff, 0.0)[None] * log_gamma[:, None, None]), 0.0)
    scores = jnp.einsum('bnihd,bnjhd->bnhij', qc, kc) * decay
    intra = jnp.einsum('bnhij,bnjhe->bnihe', scores, vc)

    k_decay = jnp.exp((C - 1 - idx)[:, None] * log_gamma[None, :])
    kv = jnp.einsum('bnjhd,bnjhe->nbhde', kc * k_decay[:, :, None], vc)
    chunk_decay = jnp.exp(C * log_gamma)[None, :, None, None]

    def step(state, kv_n):
        return chunk_decay * state + kv_n, state

    _, states = lax.scan(step, jnp.zeros((B, H, dk, dv), jnp.float32), kv)
    q_decay = jnp.exp((idx + 1)[:, None] * log_gamma[None, :])
    cross = jnp.einsum('bnihd,nbhde->bnihe', qc * q_decay[:, :, None], states)

    y = (intra + cross).reshape(B, S, H, dv)
    y = y * lax.rsqrt(jnp.mean(y * y, axis=-1, keepdims=True) + EPS)
    return y.reshape(B, S, H * dv) * jax.nn.silu(g.astype(jnp.float32))

def pool_mixer(u, w_pool, pool_scale):
    B, S, _ = u.shape
    uf = u.astype(jnp.float32).reshape(B, S, POOL_GROUPS, POOL_GROUP_DIM)
    cs = jnp.concatenate([jnp.zeros((B, 1, POOL_GROUPS, POOL_GROUP_DIM), jnp.float32),
                          jnp.cumsum(uf, axis=1)], axis=1)
    t = jnp.arange(S)
    win = jnp.array(POOL_WINDOWS)
    lo = jnp.maximum(t[:, None] + 1 - win[None, :], 0)
    count = (t[:, None] + 1 - lo).astype(jnp.float32)
    cs_lo = cs[:, lo, jnp.arange(POOL_GROUPS)[None, :], :]
    mean = (cs[:, 1:] - cs_lo) / count[None, :, :, None]
    y = jnp.einsum('bsgc,gce->bsge', mean - uf, w_pool.astype(jnp.float32))
    return y.reshape(B, S, POOL_W) * pool_scale.astype(jnp.float32)

def second_inputs(seed: int = 0) -> dict:
    key = jax.random.key(seed)
    ks = jax.random.split(key, 20)

    def w(k, shape, fan_in):
        return jax.random.normal(k, shape, jnp.float32) * (fan_in ** -0.5)

    def gain(k, shape):
        return 1.0 + 0.02 * jax.random.normal(k, shape, jnp.float32)

    return {
        "x": jax.random.normal(ks[0], (BATCH, SEQ, D_MODEL), jnp.float32),
        "g_ffn1": gain(ks[1], (DEPTH, D_MODEL)),
        "w1_ffn1": w(ks[2], (DEPTH, D_MODEL, D_FF), D_MODEL),
        "w3_ffn1": w(ks[3], (DEPTH, D_MODEL, D_FF), D_MODEL),
        "w2_ffn1": w(ks[4], (DEPTH, D_FF, D_MODEL), D_FF),
        "g_mix": gain(ks[5], (DEPTH, D_MODEL)),
        "w_in": w(ks[6], (DEPTH, D_MODEL, D_IN), D_MODEL),
        "w_branch_sb": w(ks[7], (DEPTH, SB_W, D_MODEL), SB_W),
        "w_branch_ret": w(ks[8], (DEPTH, RET_V_W, D_MODEL), RET_V_W),
        "w_branch_pool": w(ks[9], (DEPTH, POOL_W, D_MODEL), POOL_W),
        "w_pool": w(ks[10], (DEPTH, POOL_GROUPS, POOL_GROUP_DIM, POOL_GROUP_DIM), POOL_GROUP_DIM),
        "pool_scale": gain(ks[11], (DEPTH, POOL_W)),
        "w_out": w(ks[12], (DEPTH, D_MODEL, D_MODEL), D_MODEL),
        "g_ffn2": gain(ks[13], (DEPTH, D_MODEL)),
        "w1_ffn2": w(ks[14], (DEPTH, D_MODEL, D_FF), D_MODEL),
        "w3_ffn2": w(ks[15], (DEPTH, D_MODEL, D_FF), D_MODEL),
        "w2_ffn2": w(ks[16], (DEPTH, D_FF, D_MODEL), D_FF),
        "g_final": gain(ks[17], (D_MODEL,)),
    }

def second_block(x, g_ffn1, w1_ffn1, w3_ffn1, w2_ffn1, g_mix, w_in, w_branch_sb, w_branch_ret,
              w_branch_pool, w_pool, pool_scale, w_out, g_ffn2, w1_ffn2, w3_ffn2, w2_ffn2, g_final):
    B, S, D = x.shape
    split_points = [int(p) for p in np.cumsum(SPLITS)[:-1]]
    for l in range(DEPTH):
        x = x + swiglu_half(rmsnorm(x, g_ffn1[l]), w1_ffn1[l], w3_ffn1[l], w2_ffn1[l])

        h = rmsnorm(x, g_mix[l])
        proj = h @ w_in[l]
        q_sb, k_sb, v_sb, q_r, k_r, v_r, g_r, u_p, gate = jnp.split(proj, split_points, axis=-1)
        y_sb = stick_breaking_attention(q_sb.reshape(B, S, SB_HEADS, SB_HEAD_DIM),
                                        k_sb.reshape(B, S, SB_HEADS, SB_HEAD_DIM),
                                        v_sb.reshape(B, S, SB_HEADS, SB_HEAD_DIM))
        y_ret = retention(q_r.reshape(B, S, RET_HEADS, RET_QK_DIM),
                          k_r.reshape(B, S, RET_HEADS, RET_QK_DIM),
                          v_r.reshape(B, S, RET_HEADS, RET_V_DIM), g_r)
        y_pool = pool_mixer(u_p, w_pool[l], pool_scale[l])

        gates = jax.nn.sigmoid(gate.astype(jnp.float32)).reshape(B, S, N_BRANCHES, D)
        merged = (gates[:, :, 0] * (y_sb @ w_branch_sb[l].astype(jnp.float32))
                  + gates[:, :, 1] * (y_ret @ w_branch_ret[l].astype(jnp.float32))
                  + gates[:, :, 2] * (y_pool @ w_branch_pool[l].astype(jnp.float32)))
        x = x + merged.astype(x.dtype) @ w_out[l]

        x = x + swiglu_half(rmsnorm(x, g_ffn2[l]), w1_ffn2[l], w3_ffn2[l], w2_ffn2[l])
    return rmsnorm(x, g_final)


def setup_inputs(seed=0):
    out = dict(first_inputs(seed))
    for name, value in second_inputs(seed + 1).items():
        if name != "x":
            out[name + "_2"] = value
    return out


def reference(
    x, mem, ffn1_norm, ffn1_w_gate, ffn1_w_up, ffn1_w_down, mix_norm, w_in, hgrn_lb,
    hgrn_out_norm, fox_f_bias, w_out, cross_norm, mem_norm, cross_wq, cross_wk, cross_wv,
    cross_wo, ffn2_norm, ffn2_w_gate, ffn2_w_up, ffn2_w_down, final_norm, g_ffn1_2, w1_ffn1_2,
    w3_ffn1_2, w2_ffn1_2, g_mix_2, w_in_2, w_branch_sb_2, w_branch_ret_2, w_branch_pool_2,
    w_pool_2, pool_scale_2, w_out_2, g_ffn2_2, w1_ffn2_2, w3_ffn2_2, w2_ffn2_2, g_final_2,
):
    x = first_block(
        x, mem, ffn1_norm, ffn1_w_gate, ffn1_w_up, ffn1_w_down, mix_norm, w_in, hgrn_lb,
        hgrn_out_norm, fox_f_bias, w_out, cross_norm, mem_norm, cross_wq, cross_wk, cross_wv,
        cross_wo, ffn2_norm, ffn2_w_gate, ffn2_w_up, ffn2_w_down, final_norm,
    )
    return second_block(
        x, g_ffn1_2, w1_ffn1_2, w3_ffn1_2, w2_ffn1_2, g_mix_2, w_in_2, w_branch_sb_2,
        w_branch_ret_2, w_branch_pool_2, w_pool_2, pool_scale_2, w_out_2, g_ffn2_2, w1_ffn2_2,
        w3_ffn2_2, w2_ffn2_2, g_final_2,
    )


_drawn_inputs = setup_inputs


def setup_inputs(seed=0):
    import zlib

    import numpy as np

    out = dict(_drawn_inputs(seed))
    spreads = {}
    factors = {'cross_norm': 6.251,
     'mem_norm': 3.914,
     'g_ffn1_2': 4.267,
     'pool_scale_2': 21.243,
     'g_ffn2_2': 35.432,
     'g_final_2': 23.091,
     'g_mix_2': 4.209}
    for name, (base, spread) in spreads.items():
        noise = np.random.default_rng([zlib.crc32(name.encode()), seed]).standard_normal(out[name].shape)
        drawn = base * np.exp(spread * noise) if base else spread * noise
        out[name] = __import__('jax').numpy.asarray(drawn.astype(out[name].dtype))
    for name, factor in factors.items():
        out[name] = (out[name] * factor).astype(out[name].dtype)
    return out
```

```python
from contextlib import ExitStack

import numpy as np
import concourse.bass as bass
from concourse import mybir

F32 = mybir.dt.float32
F32R = mybir.dt.float32r
I32 = mybir.dt.int32
ALU = mybir.AluOpType
ACT = mybir.ActivationFunctionType
AX = mybir.AxisListType.X

P = 128
SEQ, DM, DFF, DEPTH = 256, 1024, 2816, 2
TB = SEQ // P
KT = DM // P
EPS = 1e-6
FF_STEPS = DFF // 256
RING = 3
CREDIT = RING
FFN_UNITS = 3 * FF_STEPS
MASKED = -1e30
N_LOADS = 8
S_A, S_B = 3, 2
V_START, V_A, V_BETWEEN, V_B = 3, 47, 2, 14

A_FFN1 = 0
A_IN = FFN_UNITS
A_OUT = A_IN + 16
A_K = A_OUT + 4
A_V = A_K + 4
A_Q = A_V + 4
A_O = A_Q + 4
A_FFN2 = A_O + 4
A_UNITS = A_FFN2 + FFN_UNITS
B_FFN1 = 0
B_IN = FFN_UNITS
B_BR = B_IN + 22
B_OUT = B_BR + 4
B_FFN2 = B_OUT + 4
B_UNITS = B_FFN2 + FFN_UNITS
assert A_UNITS % RING == 0 and B_UNITS % RING == 0 and A_FFN2 % RING == 0 and B_FFN2 % RING == 0
LAYER_UNITS = (A_UNITS, B_UNITS)
FIRST_UNIT = (0, DEPTH * A_UNITS)

TURNS = (7, 4)
FIRST_TURN = (0, DEPTH * 7)
NORMS = (5, 3)
FIRST_NORM = (0, DEPTH * 5 + 1)
ADDS = (4, 3)
FIRST_ADD = (1, DEPTH * 4 + 2)

H_HEADS, H_D = 4, 128
X_HEADS, X_D = 8, 64
C_HEADS, C_D = 4, 256
HEAD_ORDER = (0, 2, 1, 3)
LEVELS = (64, 32, 16, 8, 4, 2, 1)
POOL_WINDOWS = (2, 4, 8, 16)

TABLES = (dict(level=128 * len(LEVELS), reset=256, zeros=128, causal=128, sel=1024, ones=256),
          dict(neg_later=128, neg_ones=128, strict=128, cos=64, sin=64, decay=1024, pool=1536))
CONST_AT = {name: (sum(list(t.values())[:n]), cols) for t in TABLES for n, (name, cols) in enumerate(t.items())}
N_CONST = max(sum(t.values()) for t in TABLES)


def constants():
    c = np.zeros((2, P, N_CONST), np.float32)

    def part(name):
        at, cols = CONST_AT[name]
        return c[0 if name in TABLES[0] else 1][:, at:at + cols]

    i = np.arange(P)
    s, t = i[:, None], i[None, :]
    for n, m in enumerate(LEVELS):
        part("level")[:, n * P:(n + 1) * P] = (s // (2 * m) == t // (2 * m)) & (s % (2 * m) < m) & (t % (2 * m) >= m)
    part("reset")[:] = (np.arange(SEQ) % P != 0)[None, :]
    part("causal")[:] = np.where(t <= s, 0.0, MASKED)
    for h in range(8):
        part("sel")[h, h * P:(h + 1) * P] = 1.0
    part("ones")[:] = 1.0
    part("neg_later")[:] = -(s > t).astype(np.float32)
    part("neg_ones")[:] = -1.0
    part("strict")[:] = s < t
    half = 32
    freq = np.float32(10000.0) ** (-np.arange(half, dtype=np.float32) / half)
    ang = np.arange(SEQ, dtype=np.float32)[:, None] * freq[None, :]
    for name, f in (("cos", np.cos), ("sin", np.sin)):
        part(name)[:] = f(ang).reshape(TB, P, half).transpose(1, 0, 2).reshape(P, TB * half)
    for h, head in enumerate(HEAD_ORDER):
        g = np.log(1.0 - 2.0 ** (-5.0 - head))
        for o in range(2):
            d = t + o * P - s
            w = np.where(d >= 0, np.exp(np.maximum(d, 0) * g), 0.0) * 64 ** -0.5
            part("decay")[:, (h * 2 + o) * P:(h * 2 + o + 1) * P] = w
    for n, win in enumerate(POOL_WINDOWS):
        for m, (sb, tb) in enumerate(((0, 0), (0, 1), (1, 1))):
            S, T = s + sb * P, t + tb * P
            count = np.minimum(T + 1, win)
            w = ((S <= T) & (S > T - win)) / count - (S == T)
            part("pool")[:, (n * 3 + m) * P:(n * 3 + m + 1) * P] = w
    return c[0], c[1], np.eye(P, dtype=np.float32)


def build(nc, x, mem, gains, table_a, table_b, eye, lb, out_norm, f_bias, w_pool, pool_scale, W, out):
    with ExitStack() as ctx:
        def sb(name, shape, dt=F32):
            return ctx.enter_context(nc.sbuf_tensor(name, shape, dt))

        def sem(name):
            return ctx.enter_context(nc.semaphore(name))

        raw = sb("raw", [P, RING, 4, 512])
        whi = sb("whi", [P, RING, 4, 512], F32R)
        wlo = sb("wlo", [P, RING, 4, 512], F32R)
        xres = sb("xres", [P, TB, DM])
        xn = sb("xn", [P, TB, DM])
        hT_hi = sb("hT_hi", [P, TB, KT, P], F32R)
        hT_lo = sb("hT_lo", [P, TB, KT, P], F32R)
        gain = sb("gain", [P, DM])
        silu_g = sb("silu_g", [P, TB, 256])
        prod = sb("prod", [P, TB, 256])
        aT_hi = sb("aT_hi", [P, 2, TB, P], F32R)
        aT_lo = sb("aT_lo", [P, 2, TB, P], F32R)
        ident = sb("ident", [P, P])
        cst = sb("cst", [P, N_CONST])
        stat = sb("stat", [P, 8])
        lbt = sb("lbt", [P, DEPTH, H_HEADS])
        lbw = sb("lbw", [P, 3, H_HEADS])
        lb_l = sb("lb_l", [P, 2, H_HEADS])
        onorm_l = sb("onorm_l", [P, H_D])
        pscale_l = sb("pscale_l", [P, 2])
        flog = sb("flog", [P, TB, 8])
        ln_lb = sb("ln_lb", [P, DEPTH, H_HEADS])
        ln_1mlb = sb("ln_1mlb", [P, DEPTH, H_HEADS])
        onorm = sb("onorm", [P, DEPTH, H_D])
        fbias = sb("fbias", [8, DEPTH])
        wpool = sb("wpool", [64, DEPTH, 4, 64])
        wpool_l = sb("wpool_l", [64, 4, 64])
        pscale = sb("pscale", [P, DEPTH, 2])
        sst = sb("sst", [P, 5, 16])
        hst = sb("hst", [P, 3, 8])
        arena = sb("arena", [P, 18432])

        def take(*spans):
            at, got = 0, []
            for n in spans:
                got.append(arena[:, at:at + n])
                at += n
            assert at <= 18432, at
            return got

        (memx_, zf, hq, hk, hv, hg, fq, fk, fv, cum, tmp1, tmp2, lev2, att, attx, fpT, fcs) = take(
            2048, *[1024] * 11, 2048, 1024, 512, 512, 1024)
        memx = memx_.rearrange("p (t d) -> p t d", t=TB)
        fsc, fp = lev2[:, 0:1024], lev2[:, 1024:2048]
        fcs_f, fcs_c, fcs_n, fcs_t = (fcs[0:8, 256 * n:256 * n + 256] for n in range(4))
        (qk_sb, qk_r, vu, v_r, g_r, pool_d, gates, st1, st2, st3, sc_r) = take(*[1024] * 6, 6144, *[1536] * 4)
        qk_rot = st2[:, 0:1024]
        qk_rT = qk_r
        br_tmp = arena[:, 12288:12288 + 2048]
        ps = ctx.enter_context(nc.psum_tensor("ps", [P, 8, 512], F32))
        ACC, G, TR = 0, 4, 6
        PAIRS = (4, 0, 2)

        def con(name, a=0, n=None, rows=P):
            at, cols = CONST_AT[name]
            return cst[0:rows, at + a:at + a + (cols if n is None else n)]

        loaded = sem("loaded")
        x_loaded = sem("x_loaded")
        gain_loaded = sem("gain_loaded")
        raw_loaded = [sem(f"raw_loaded{s}") for s in range(RING)]
        hi_ready = sem("hi_ready")
        lo_ready = sem("lo_ready")
        unit_done = sem("unit_done")
        x_ready = sem("x_ready")
        sq_sum = sem("sq_sum")
        sq_done = sem("sq_done")
        xn_ready = sem("xn_ready")
        turned = sem("turned")
        turn_hi = sem("turn_hi")
        turn_lo = sem("turn_lo")
        silu_done = sem("silu_done")
        prod_ready = sem("prod_ready")
        act_turned = sem("act_turned")
        act_hi = sem("act_hi")
        act_lo = sem("act_lo")
        chunk_out = sem("chunk_out")
        vstep = sem("vstep")
        sstep = sem("sstep")
        lb_abs, lb_sp, lb_done = sem("lb_abs"), sem("lb_sp"), sem("lb_done")
        h_abs, h_sp, h_gate, h_sp2 = sem("h_abs"), sem("h_sp"), sem("h_gate"), sem("h_sp2")
        h_key = sem("h_key")
        lev_diff, lev_exp, lev_ready, lev_prod, lev_kept = (sem(f"lev_{n}") for n in ("diff", "exp", "ready", "prod", "kept"))
        h_out, h_sq, h_sum, h_rms = sem("h_out"), sem("h_sq"), sem("h_sum"), sem("h_rms")
        f_abs, f_sp, f_cum, f_cumT, f_cumS = (sem(f"f_{n}") for n in ("abs", "sp", "cum", "cumT", "cumS"))
        f_tm, f_turn, f_logit = sem("f_tm"), sem("f_turn"), sem("f_logit")
        a_score, a_masked, a_max, a_prob, a_turn, a_pT, a_out = (
            sem(f"a_{n}") for n in ("score", "masked", "max", "prob", "turn", "pT", "out"))
        c_score, c_max, c_prob, c_turn, c_pT, c_out = (sem(f"c_{n}") for n in ("score", "max", "prob", "turn", "pT", "out"))
        r_rot, r_turn, r_kT, r_score, r_dec, r_out, r_sq, r_sum, r_rms, r_y, r_yT, r_hi, r_lo = (
            sem(f"r_{n}") for n in ("rot", "turn", "kT", "score", "dec", "out", "sq", "sum", "rms", "y", "yT", "hi", "lo"))
        s_score, s_sp, s_fail, s_after, s_sum, s_exp, s_w, s_out, s_hi, s_lo = (
            sem(f"s_{n}") for n in ("score", "sp", "fail", "after", "sum", "exp", "w", "out", "hi", "lo"))
        p_diff, p_dT, p_wl, p_out, p_hi, p_lo = (sem(f"p_{n}") for n in ("diff", "dT", "wl", "out", "hi", "lo"))
        br_done, br_used = sem("br_done"), sem("br_used")
        stored = sem("stored")

        def unit(b, l, off, c=0):
            return FIRST_UNIT[b] + l * LAYER_UNITS[b] + off + 3 * c

        def use(b, l, off, c=0):
            return FIRST_UNIT[b] // RING + l * (LAYER_UNITS[b] // RING) + off // RING + c + 1

        def turn_no(b, l, j):
            return FIRST_TURN[b] + l * TURNS[b] + j

        def norm_no(b, l, j):
            return FIRST_NORM[b] + l * NORMS[b] + j

        def add_no(b, l, j):
            return FIRST_ADD[b] + l * ADDS[b] + j

        def ffn_no(b, l, e):
            return 2 * DEPTH * b + 2 * l + e

        def chunk_no(b, l, i):
            return (0, DEPTH * 13)[b] + l * (13, 11)[b] + i

        def wait_unit(eng, b, l, off, c=0):
            eng.wait_ge(unit_done, unit(b, l, off, c) + 1 + CREDIT)

        def stepper(eng, done, base):
            count = [0]

            def step(ins):
                count[0] += 1
                ins.then_inc(done, 1)
                eng.wait_ge(done, base + count[0])

            return step, count

        block = ctx.enter_context(nc.Block())

        @block.sync
        def _(sp):
            sp.dma_start(xres[:, :, :], x[0].rearrange("(t p) d -> p t d", p=P)).then_inc(x_loaded, 16)

            def load(b, l, off, c, parts):
                s = off % RING
                sp.wait_ge(lo_ready, unit(b, l, off, c) + 1)
                for dst, src in reversed(parts(raw[:, s])):
                    sp.dma_start(dst, src).then_inc(raw_loaded[s], 16)

            def cols(a, b_):
                def parts(slot):
                    v = slot.rearrange("p k (t n) -> p k t n", t=2)
                    return [(v[:, :, t, :], src.rearrange("(k p) n -> p k n", p=P)) for t, src in enumerate((a, b_))]
                return parts

            def rows(w):
                def parts(slot):
                    v = slot.rearrange("p (k t) n -> p k (t n)", k=2)
                    return [(v[:, k, :], w[k * P:(k + 1) * P, :]) for k in range(2)]
                return parts

            def ffn(b, l, off, e):
                wg, wu, wd = W[b, e, "gate"], W[b, e, "up"], W[b, e, "down"]

                def gate_up(off, c, step):
                    for k in range(2):
                        load(b, l, off + k, c, cols(*(w[l, k * 512:(k + 1) * 512, bass.ds(step * 256, 256)] for w in (wg, wu))))

                def down(off, c, step):
                    load(b, l, off, c, rows(wd[l, bass.ds(step * 256, 256), :]))

                gate_up(off, 0, 0)
                with sp.Fori(0, FF_STEPS - 1) as c:
                    gate_up(off + 2, c, c + 1)
                    down(off + 4, c, c)
                down(off + FFN_UNITS - 1, 0, FF_STEPS - 1)

            def chunk(b, l, off, w, c0, c1):
                for k in range(2):
                    load(b, l, off + k, 0, cols(*(w[l, k * 512:(k + 1) * 512, a:a + 256] for a in (c0, c1))))

            def tall(b, l, off, n, w):
                for u in range(n):
                    load(b, l, off + u, 0, rows(w[l, u * 256:(u + 1) * 256, :]))

            with sp.Fori(0, DEPTH) as l:
                ffn(0, l, A_FFN1, 0)
                w = W["w_in"]
                for n, c0 in enumerate((512, 0, 1536, None, 2048, 2560, 3072, 1024)):
                    off = A_IN + 2 * n
                    if c0 is not None:
                        chunk(0, l, off, w, c0, c0 + 256)
                        continue
                    for k in range(2):
                        load(0, l, off + k, 0, lambda slot, k=k: [
                            (slot[:, 2 * i:2 * i + 2, 0:8],
                             w[l, k * 512 + i * 256:k * 512 + (i + 1) * 256, 3584:3592].rearrange("(k p) n -> p k n", p=P))
                            for i in range(2)])
                tall(0, l, A_OUT, 4, W["w_out"])
                for off, name in ((A_K, "cross_wk"), (A_V, "cross_wv"), (A_Q, "cross_wq")):
                    for i in range(2):
                        chunk(0, l, off + 2 * i, W[name], 512 * i, 512 * i + 256)
                tall(0, l, A_O, 4, W["cross_wo"])
                ffn(0, l, A_FFN2, 1)
            with sp.Fori(0, DEPTH) as l:
                ffn(1, l, B_FFN1, 0)
                for n, (c0, c1) in enumerate([(0, 256), (768, 1024), (512, 2304), (1280, 1536), (1792, 2048)]
                                             + [(2560 + 512 * i, 2816 + 512 * i) for i in range(6)]):
                    chunk(1, l, B_IN + 2 * n, W["w_in_2"], c0, c1)
                tall(1, l, B_BR, 1, W["w_branch_sb_2"])
                tall(1, l, B_BR + 1, 2, W["w_branch_ret_2"])
                tall(1, l, B_BR + 3, 1, W["w_branch_pool_2"])
                tall(1, l, B_OUT, 4, W["w_out_2"])
                ffn(1, l, B_FFN2, 1)
            o = out[0].rearrange("(t p) d -> p t d", p=P)
            for t in range(TB):
                sp.wait_ge(x_ready, 2 * add_no(1, DEPTH, 0) + t + 1)
                sp.dma_start(o[:, t, :], xres[:, t, :]).then_inc(stored, 16)
            sp.wait_ge(stored, 16 * TB)

        @block.gpsimd
        def _(pool):
            pool.sem_inc(lo_ready, CREDIT)

            def split_lo(n, s):
                pool.wait_ge(hi_ready, n + 1)
                pool.tensor_tensor(wlo[:, s], raw[:, s], whi[:, s].bitcast(F32), ALU.subtract).then_inc(lo_ready, 1)

            def forget_unit(n, s):
                pool.wait_ge(hi_ready, n + 1)
                pool.tensor_tensor(wlo[:, s, :, 0:8], raw[:, s, :, 0:8], whi[:, s, :, 0:8].bitcast(F32),
                                   ALU.subtract).then_inc(lo_ready, 1)

            FORGET = A_IN + 6
            with pool.Fori(0, DEPTH) as l:
                with pool.Fori(0, FORGET // RING) as c:
                    for s in range(RING):
                        split_lo(unit(0, l, s, c), s)
                for u in range(FORGET, FORGET + 3):
                    (forget_unit if u < FORGET + 2 else split_lo)(unit(0, l, u), u % RING)
                with pool.Fori(0, (A_UNITS - FORGET) // RING - 1) as c:
                    for s in range(RING):
                        split_lo(unit(0, l, FORGET + 3 + s, c), s)
            with pool.Fori(0, DEPTH) as l:
                with pool.Fori(0, B_UNITS // RING) as c:
                    for s in range(RING):
                        split_lo(unit(1, l, s, c), s)

        @block.scalar
        def _(act):
            for dst, src in ((cst[:, :], table_a), (ident[:, :], eye), (memx[:, :, :], mem[0].rearrange("(t p) d -> p t d", p=P)),
                             (lbt[:, :, :], lb), (onorm[:, :, :], out_norm.unsqueeze(0).broadcast_to([P, DEPTH, H_D])),
                             (fbias[:, :], f_bias), (wpool[:, :, :, :], w_pool), (pscale[:, :, :], pool_scale)):
                act.dma_start(dst, src).then_inc(loaded, 16)
            act.dma_start(gain[:, :], gains[0:1, :].broadcast_to([P, DM])).then_inc(gain_loaded, 16)

            act.wait_ge(loaded, N_LOADS * 16)
            act.wait_ge(lb_abs, 1)
            act.activation(lbw[:, 1, :], lbw[:, 1, :], ACT.Exp, scale=-1.0).then_inc(lb_sp, 1)
            act.wait_ge(lb_sp, 1)
            act.activation(lbw[:, 1, :], lbw[:, 1, :], ACT.Ln, bias=1.0).then_inc(lb_sp, 1)

            def split_hi(b, l, off, c=0, cols=512):
                s = off % RING
                act.wait_ge(raw_loaded[s], 32 * use(b, l, off, c))
                act.wait_ge(unit_done, unit(b, l, off, c) + 1)
                act.activation(whi[:, s, :, 0:cols], raw[:, s, :, 0:cols], ACT.Copy).then_inc(hi_ready, 1)

            def squares(src, n, add=None):
                for t in range(TB):
                    if add is not None:
                        act.wait_ge(x_ready, 2 * add + t + 1)
                    act.activation(xn[:, t, :], src[:, t, :], ACT.Square, accum_out=stat[:, t:t + 1]).then_inc(sq_sum, 1)
                    act.wait_ge(sq_sum, 2 * n + t + 1)
                    act.activation(stat[:, 2 + t:3 + t], stat[:, t:t + 1], ACT.Sqrt, scale=1.0 / DM, bias=EPS).then_inc(sq_done, 1)

            def next_gain(n):
                act.dma_start(gain[:, :], gains[bass.ds(n + 1, 1), :].broadcast_to([P, DM])).then_inc(gain_loaded, 16)

            def turn_out(T):
                for i in range(2 * TB):
                    t, h = divmod(i, 2)
                    act.wait_ge(turned, 4 * T + i + 1)
                    act.activation(hT_hi[:, t, 4 * h:4 * h + 4, :].rearrange("p k c -> p (k c)"), ps[:, TR + h, :],
                                   ACT.Copy).then_inc(turn_hi, 1)

            def ffn(b, l, off, e, T):
                f = ffn_no(b, l, e)

                def silu(u, cc, step):
                    for t in range(TB):
                        if t == 0:
                            wait_unit(act, b, l, u, cc)
                        act.activation(silu_g[:, t, :], ps[:, G + t, 0:256], ACT.Silu).then_inc(silu_done, 1)

                def evac(step):
                    act.wait_ge(act_turned, FF_STEPS * f + step + 1)
                    act.activation(aT_hi[:, :, :, :].rearrange("p k t c -> p (k t c)"), ps[:, TR, :],
                                   ACT.Copy).then_inc(act_hi, 1)

                turn_out(T)
                split_hi(b, l, off + 2)
                silu(off + 1, 0, 0)
                split_hi(b, l, off + 3)
                split_hi(b, l, off + 4)
                with act.Fori(0, FF_STEPS - 2) as c:
                    evac(c)
                    split_hi(b, l, off + 5, c)
                    silu(off + 3, c, c + 1)
                    split_hi(b, l, off + 6, c)
                    split_hi(b, l, off + 7, c)
                evac(FF_STEPS - 2)
                split_hi(b, l, off + FFN_UNITS - 1)
                silu(off + FFN_UNITS - 3, 0, FF_STEPS - 1)
                evac(FF_STEPS - 1)

            def chunk_out_(b, l, u, pair, dst, func, scale=1.0):
                wait_unit(act, b, l, u + 1)
                act.activation(dst, ps[:, pair:pair + 2, :].rearrange("p a c -> p (a c)"), func,
                               scale=scale).then_inc(chunk_out, 1)

            with act.Fori(0, DEPTH) as l:
                step, count = stepper(act, sstep, l * S_A)
                split_hi(0, l, A_FFN1)
                split_hi(0, l, A_FFN1 + 1)
                squares(xres, norm_no(0, l, 0), add_no(0, l, -1))
                ffn(0, l, A_FFN1, 0, turn_no(0, l, 0))
                U = A_IN
                split_hi(0, l, U)
                split_hi(0, l, U + 1)
                act.wait_ge(turn_lo, 4 * turn_no(0, l, 0) + 4)
                next_gain(norm_no(0, l, 0))
                squares(xres, norm_no(0, l, 1), add_no(0, l, 0))
                turn_out(turn_no(0, l, 1))
                split_hi(0, l, U + 2)
                plan = ((zf, ACT.Copy, 1.0), (hq, ACT.Silu, 1.0), (hg, ACT.Silu, 1.0), None, (fq, ACT.Copy, X_D ** -0.5),
                        (fk, ACT.Copy, 1.0), (fv, ACT.Copy, 1.0), (hv, ACT.Copy, 1.0))
                for i, what in enumerate(plan):
                    for u in (2 * i + 3, 2 * i + 4):
                        if u < 19:
                            split_hi(0, l, U + u, cols=8 if u in (6, 7) else 512)
                    if what:
                        dst, func, scale = what
                        chunk_out_(0, l, U + 2 * i, PAIRS[(i if i < 3 else i - 1) % 3], dst, func, scale)
                    else:
                        wait_unit(act, 0, l, U + 7)
                        act.activation(flog[:, :, :].rearrange("p t h -> p (t h)"), ps[:, TR, 0:16], ACT.Copy).then_inc(f_tm, 1)
                        act.wait_ge(f_turn, l + 1)
                        act.activation(fcs_f, ps[0:8, TR + 1, 0:256], ACT.Identity, bias=fbias[:, bass.ds(l, 1)]).then_inc(f_logit, 1)
                act.wait_ge(turn_lo, 4 * turn_no(0, l, 1) + 4)
                next_gain(norm_no(0, l, 1))
                act.wait_ge(h_abs, l + 1)
                step(act.activation(tmp1, tmp1, ACT.Exp, scale=-1.0))
                act.activation(tmp1, tmp1, ACT.Ln, bias=1.0).then_inc(h_sp, 1)
                act.wait_ge(f_abs, l + 1)
                step(act.activation(fcs_t, fcs_t, ACT.Exp, scale=-1.0))
                act.activation(fcs_t, fcs_t, ACT.Ln, bias=1.0).then_inc(f_sp, 1)
                act.wait_ge(h_gate, l + 1)
                step(act.activation(lev2[:, 0:1024], lev2[:, 0:1024], ACT.Exp, scale=-1.0))
                act.activation(lev2[:, 0:1024], lev2[:, 0:1024], ACT.Ln, bias=1.0).then_inc(h_sp2, 1)
                for h in range(H_HEADS):
                    act.activation(hk[:, h * SEQ:(h + 1) * SEQ], hk[:, h * SEQ:(h + 1) * SEQ], ACT.Exp, scale=-1.0,
                                   bias=lb_l[:, 1, h:h + 1]).then_inc(h_key, 1)
                NL = len(LEVELS) + 1
                for n in range(NL):
                    e = lev2[:, (n % 2) * 1024:(n % 2) * 1024 + 1024]
                    act.wait_ge(lev_diff, l * NL + n + 1)
                    act.activation(e, e, ACT.Exp).then_inc(lev_exp, 1)
                act.wait_ge(h_out, l + 1)
                o2 = ps[:, ACC + 2:ACC + 4, :].rearrange("p a c -> p (a c)")
                act.activation(tmp1, o2, ACT.Square).then_inc(h_sq, 1)
                act.activation(tmp2, o2, ACT.Copy)
                act.wait_ge(h_sum, l + 1)
                act.activation(hst[:, 1, :], hst[:, 0, :], ACT.Sqrt, scale=1.0 / H_D, bias=EPS).then_inc(h_rms, 1)
                act.wait_ge(f_cumT, l + 1)
                act.activation(sst[:, 3, :], ps[:, TR, 0:16], ACT.Copy).then_inc(f_cumS, 1)
                NA = X_HEADS * TB

                def fox_exp(i):
                    w = P * (i % 2 + 1)
                    act.wait_ge(a_max, l * NA + i + 1)
                    if i >= 4:
                        act.wait_ge(a_turn, l * NA + i - 3)
                    act.activation(fp[:, (i % 4) * 256:(i % 4) * 256 + w], fsc[:, (i % 4) * 256:(i % 4) * 256 + w], ACT.Exp,
                                   bias=sst[:, 1, i:i + 1], accum_out=sst[:, 2, i:i + 1]).then_inc(a_prob, 1)

                def fox_pT(i):
                    w = P * (i % 2 + 1)
                    act.wait_ge(a_turn, l * NA + i + 1)
                    if i >= 2:
                        act.wait_ge(a_out, l * NA + i - 1)
                    act.activation(fpT[:, (i % 2) * 256:(i % 2) * 256 + w], ps[:, G + i % 2, 0:w], ACT.Copy).then_inc(a_pT, 1)

                for i in range(NA + 1):
                    if i < NA:
                        fox_exp(i)
                    if i:
                        fox_pT(i - 1)
                turn_out(turn_no(0, l, 2))
                split_hi(0, l, A_OUT + 3)
                split_hi(0, l, A_K)
                split_hi(0, l, A_K + 1)
                squares(memx, norm_no(0, l, 2))
                turn_out(turn_no(0, l, 3))
                split_hi(0, l, A_K + 2)
                for i, (dst, scale) in enumerate(((zf, 1.0), (hq, 1.0), (hk, 1.0), (hv, 1.0))):
                    for u in (2 * i + 3, 2 * i + 4):
                        split_hi(0, l, A_K + u)
                    chunk_out_(0, l, A_K + 2 * i, PAIRS[i % 3], dst, ACT.Copy, scale)
                act.wait_ge(turn_lo, 4 * turn_no(0, l, 3) + 4)
                next_gain(norm_no(0, l, 2))
                squares(xres, norm_no(0, l, 3), add_no(0, l, 1))
                turn_out(turn_no(0, l, 4))
                for i, dst in enumerate((hg, fq)):
                    for u in (2 * i + 11, 2 * i + 12):
                        split_hi(0, l, A_K + u)
                    chunk_out_(0, l, A_Q + 2 * i, PAIRS[(4 + i) % 3], dst, ACT.Copy, C_D ** -0.5)
                act.wait_ge(turn_lo, 4 * turn_no(0, l, 4) + 4)
                next_gain(norm_no(0, l, 3))
                NC = C_HEADS * TB

                def cross_exp(i):
                    act.wait_ge(c_max, l * NC + i + 1)
                    if i >= 4:
                        act.wait_ge(c_turn, l * NC + i - 3)
                    act.activation(fp[:, (i % 4) * 256:(i % 4) * 256 + 256], ps[:, TR + i % 2, 0:256], ACT.Exp,
                                   bias=sst[:, 1, i:i + 1], accum_out=sst[:, 2, i:i + 1]).then_inc(c_prob, 1)

                def cross_pT(i):
                    act.wait_ge(c_turn, l * NC + i + 1)
                    if i >= 2:
                        act.wait_ge(c_out, l * NC + i - 1)
                    act.activation(fpT[:, (i % 2) * 256:(i % 2) * 256 + 256], ps[:, G + i % 2, 0:256], ACT.Copy).then_inc(c_pT, 1)

                for i in range(NC + 1):
                    if i < NC:
                        cross_exp(i)
                    if i:
                        cross_pT(i - 1)
                turn_out(turn_no(0, l, 5))
                split_hi(0, l, A_O + 3)
                split_hi(0, l, A_FFN2)
                split_hi(0, l, A_FFN2 + 1)
                squares(xres, norm_no(0, l, 4), add_no(0, l, 2))
                ffn(0, l, A_FFN2, 1, turn_no(0, l, 6))
                act.wait_ge(turn_lo, 4 * turn_no(0, l, 6) + 4)
                next_gain(norm_no(0, l, 4))
                assert count[0] == S_A, ("S_A", count[0])
            squares(xres, norm_no(0, DEPTH, 0), add_no(0, DEPTH, -1))
            act.wait_ge(x_ready, 2 * add_no(0, DEPTH, 0) + 2)
            act.dma_start(gain[:, :], gains[FIRST_NORM[1]:FIRST_NORM[1] + 1, :].broadcast_to([P, DM])).then_inc(gain_loaded, 16)
            act.dma_start(cst[:, :], table_b).then_inc(loaded, 16)
            with act.Fori(0, DEPTH) as l:
                step, count = stepper(act, sstep, DEPTH * S_A + l * S_B)
                split_hi(1, l, B_FFN1)
                split_hi(1, l, B_FFN1 + 1)
                squares(xres, norm_no(1, l, 0), add_no(1, l, -1))
                ffn(1, l, B_FFN1, 0, turn_no(1, l, 0))
                U = B_IN
                split_hi(1, l, U)
                split_hi(1, l, U + 1)
                act.wait_ge(turn_lo, 4 * turn_no(1, l, 0) + 4)
                next_gain(norm_no(1, l, 0))
                squares(xres, norm_no(1, l, 1), add_no(1, l, 0))
                turn_out(turn_no(1, l, 1))
                split_hi(1, l, U + 2)
                plan = [(qk_sb, ACT.Copy), (qk_r, ACT.Copy), (vu, ACT.Copy), (v_r, ACT.Copy), (g_r, ACT.Silu)] + [
                    (gates[:, 1024 * i:1024 * i + 1024], ACT.Sigmoid) for i in range(6)]
                for i, (dst, func) in enumerate(plan):
                    for u in (2 * i + 3, 2 * i + 4):
                        if u < 25:
                            split_hi(1, l, U + u)
                    if i == 0:
                        wait_unit(act, 1, l, U + 1)
                        act.activation(qk_sb[:, 0:512], ps[:, PAIRS[0], :], ACT.Copy, scale=64 ** -0.5)
                        act.activation(qk_sb[:, 512:1024], ps[:, PAIRS[0] + 1, :], ACT.Copy).then_inc(chunk_out, 1)
                        continue
                    chunk_out_(1, l, U + 2 * i, PAIRS[i % 3], dst, func)
                act.wait_ge(turn_lo, 4 * turn_no(1, l, 1) + 4)
                next_gain(norm_no(1, l, 1))
                for t in range(TB):
                    act.wait_ge(r_turn, l * TB + t + 1)
                    act.activation(qk_rT.rearrange("p (k t c) -> p k t c", k=4, t=TB)[:, :, t, :],
                                   ps[:, TR + t, :].rearrange("p (k c) -> p k c", k=4), ACT.Copy).then_inc(r_kT, 1)
                act.wait_ge(s_score, 2 * l + 2)
                step(act.activation(st1, ps[:, 3:6, :].rearrange("p a c -> p (a c)"), ACT.Abs))
                step(act.activation(st1, st1, ACT.Exp, scale=-1.0))
                act.activation(st1, st1, ACT.Ln, bias=1.0).then_inc(s_sp, 1)
                act.wait_ge(s_sum, l + 1)
                act.activation(st2, st2, ACT.Exp).then_inc(s_exp, 1)
                act.wait_ge(p_diff, l + 1)
                act.activation(pool_d[0:64, :], ps[0:64, G:G + 2, :].rearrange("p a c -> p (a c)"), ACT.Copy).then_inc(p_dT, 1)
                act.wait_ge(r_out, l + 1)
                o2 = ps[:, TR:TR + 2, :].rearrange("p a c -> p (a c)")
                act.activation(qk_sb, o2, ACT.Square).then_inc(r_sq, 1)
                act.activation(v_r, o2, ACT.Copy)
                act.wait_ge(r_sum, l + 1)
                act.activation(hst[:, 1, :], hst[:, 0, :], ACT.Sqrt, scale=1.0 / P, bias=EPS).then_inc(r_rms, 1)
                act.wait_ge(s_out, l + 1)
                act.activation(hT_hi[:, :, 0:2, :].rearrange("p t k c -> p k t c"),
                               ps[:, 3, :].rearrange("p (k t c) -> p k t c", k=2, t=TB), ACT.Copy).then_inc(s_hi, 1)
                act.wait_ge(p_out, l + 1)
                for k in range(2):
                    act.activation(hT_hi[:, :, 6 + k, :], ps[:, 4, k * 256:(k + 1) * 256].rearrange("p (t c) -> p t c", t=TB),
                                   ACT.Copy, scale=pscale_l[:, k:k + 1]).then_inc(p_hi, 1)
                for t in range(TB):
                    act.wait_ge(r_yT, l * TB + t + 1)
                    act.activation(hT_hi[:, t, 2:6, :].rearrange("p k c -> p (k c)"), ps[:, TR + t, :], ACT.Copy).then_inc(r_hi, 1)
                split_hi(1, l, B_BR + 3)
                split_hi(1, l, B_OUT)
                split_hi(1, l, B_OUT + 1)
                split_hi(1, l, B_OUT + 2)
                turn_out(turn_no(1, l, 2))
                split_hi(1, l, B_OUT + 3)
                split_hi(1, l, B_FFN2)
                split_hi(1, l, B_FFN2 + 1)
                squares(xres, norm_no(1, l, 2), add_no(1, l, 1))
                ffn(1, l, B_FFN2, 1, turn_no(1, l, 3))
                act.wait_ge(turn_lo, 4 * turn_no(1, l, 3) + 4)
                next_gain(norm_no(1, l, 2))
                assert count[0] == S_B, ("S_B", count[0])
            squares(xres, norm_no(1, DEPTH, 0), add_no(1, DEPTH, -1))

        @block.tensor
        def _(pe):
            pe.sem_inc(unit_done, CREDIT)
            pe.wait_ge(loaded, N_LOADS * 16)

            def split_product(out, l_hi, l_lo, r_hi, r_lo, first, last):
                pe.matmul(out, l_hi, r_hi, start=first, stop=False, skip_group_check=True)
                pe.matmul(out, l_hi, r_lo, start=False, stop=False, skip_group_check=True)
                return pe.matmul(out, l_lo, r_hi, start=False, stop=last, skip_group_check=True)

            def wait_weights(b, l, off, c=0):
                pe.wait_ge(lo_ready, unit(b, l, off, c) + 1 + CREDIT)

            def turn(T):
                for i in range(2 * TB):
                    t, h = divmod(i, 2)
                    if h == 0:
                        pe.wait_ge(xn_ready, 2 * T + t + 1)
                    if t:
                        pe.wait_ge(turn_lo, 4 * T + h + 1)
                    for k in range(4):
                        mm = pe.transpose(ps[:, TR + h, k * P:(k + 1) * P], xn[:, t, (4 * h + k) * P:(4 * h + k + 1) * P], ident[:, :])
                    mm.then_inc(turned, 1)
                pe.wait_ge(turn_lo, 4 * T + 4)

            def tokens_unit(b, l, off, c, k0, bank, first, last, ready=None):
                s = off % RING
                wait_weights(b, l, off, c)
                for t in range(TB):
                    if ready is not None:
                        pe.wait_ge(prod_ready, ready + t + 1)
                    for k in range(4):
                        mm = split_product(ps[:, bank + t, :], hT_hi[:, t, k0 + k, :], hT_lo[:, t, k0 + k, :],
                                           whi[:, s, k, :], wlo[:, s, k, :], first and k == 0, last and k == 3)
                mm.then_inc(unit_done, 1)

            def features_unit(b, l, off, k0, bank, first, last):
                s = off % RING
                wait_weights(b, l, off)
                for n in range(4):
                    cols = slice(n * P, (n + 1) * P)
                    for k in range(4):
                        mm = split_product(ps[:, bank + n // 2, n % 2 * SEQ:(n % 2 + 1) * SEQ],
                                           whi[:, s, k, cols], wlo[:, s, k, cols], hT_hi[:, :, k0 + k, :], hT_lo[:, :, k0 + k, :],
                                           first and k == 0 and n % 2 == 0, last and k == 3)
                mm.then_inc(unit_done, 1)

            def tall_unit(b, l, off, lhs, bank, first, last, c=0):
                s = off % RING
                wait_weights(b, l, off, c)
                for t in range(TB):
                    for half in range(2):
                        for k in range(2):
                            hi, lo = lhs(k)
                            mm = split_product(ps[:, bank + 2 * t + half, :], hi[:, t], lo[:, t],
                                               whi[:, s, 2 * k + half, :], wlo[:, s, 2 * k + half, :], first and k == 0, last and k == 1)
                mm.then_inc(unit_done, 1)

            def from_hT(k0):
                return lambda k: (hT_hi[:, :, k0 + k, :], hT_lo[:, :, k0 + k, :])

            def ffn(b, l, off, e, T):
                f = ffn_no(b, l, e)

                def half_up(off, c, step, k):
                    ready = 2 * FF_STEPS * f + 2 * (step - 1) if k == 0 and not (isinstance(step, int) and step == 0) else None
                    tokens_unit(b, l, off + k, c, 4 * k, G, k == 0, k == 1, ready)

                def turn_act(step):
                    pe.wait_ge(prod_ready, 2 * FF_STEPS * f + 2 * step + 2)
                    for k in range(2):
                        for t in range(TB):
                            mm = pe.transpose(ps[:, TR, (2 * k + t) * P:(2 * k + t + 1) * P], prod[:, t, k * P:(k + 1) * P], ident[:, :])
                    mm.then_inc(act_turned, 1)

                def down(off, c, step, first, last):
                    pe.wait_ge(act_lo, FF_STEPS * f + step + 1)
                    tall_unit(b, l, off, lambda k: (aT_hi[:, k], aT_lo[:, k]), ACC, first, last, c)

                def step_(off, c, step, first):
                    half_up(off, c, step, 0)
                    turn_act(step - 1)
                    half_up(off, c, step, 1)
                    down(off + 2, c, step - 1, first, False)

                turn(T)
                half_up(off, 0, 0, 0)
                half_up(off, 0, 0, 1)
                step_(off + 2, 0, 1, True)
                with pe.Fori(0, FF_STEPS - 2) as c:
                    step_(off + 5, c, c + 2, False)
                turn_act(FF_STEPS - 1)
                down(off + FFN_UNITS - 1, 0, FF_STEPS - 1, False, True)

            def chunk(b, l, off, pair, features, j=None):
                if j is not None:
                    pe.wait_ge(chunk_out, chunk_no(b, l, j) + 1)
                for k in range(2):
                    if features:
                        features_unit(b, l, off + k, 4 * k, pair, k == 0, k == 1)
                    else:
                        tokens_unit(b, l, off + k, 0, 4 * k, pair, k == 0, k == 1)

            with pe.Fori(0, DEPTH) as l:
                ffn(0, l, A_FFN1, 0, turn_no(0, l, 0))
                turn(turn_no(0, l, 1))
                for i, features in enumerate((True, True, False, None, True, True, False, False)):
                    off, j = A_IN + 2 * i, i if i < 3 else i - 1
                    if features is not None:
                        chunk(0, l, off, PAIRS[j % 3], features, j - 3 if j >= 3 else None)
                        continue
                    for k in range(2):
                        s = (off + k) % RING
                        wait_weights(0, l, off + k)
                        for t in range(TB):
                            for kk in range(4):
                                mm = split_product(ps[:, TR, 8 * t:8 * t + 8], hT_hi[:, t, 4 * k + kk, :], hT_lo[:, t, 4 * k + kk, :],
                                                   whi[:, s, kk, 0:8], wlo[:, s, kk, 0:8], k == 0 and kk == 0 and t == 0, k == 1 and kk == 3)
                        mm.then_inc(unit_done, 1)
                    pe.wait_ge(f_tm, l + 1)
                    for t in range(TB):
                        mm = pe.transpose(ps[0:8, TR + 1, t * P:(t + 1) * P], flog[:, t, :], ident[:, :])
                    mm.then_inc(f_turn, 1)
                pe.wait_ge(chunk_out, chunk_no(0, l, 7))
                NG = len(LEVELS) + 2
                for n in range(NG):
                    bank = ACC + 2 * (n % 2)
                    if n >= 2:
                        pe.wait_ge(lev_kept, l * NG + n - 1)
                    if n == 0:
                        pe.wait_ge(h_key, H_HEADS * (l + 1))
                        a, c = hk, hq
                    else:
                        pe.wait_ge(lev_ready, l * (NG - 1) + n)
                        a = c = lev2[:, (n - 1) % 2 * 1024:(n - 1) % 2 * 1024 + 1024]
                    if n < NG - 1:
                        for g in range(H_HEADS * TB):
                            mm = pe.matmul(ps[:, bank + g // 4, g % 4 * P:(g % 4 + 1) * P], a[:, g * P:(g + 1) * P],
                                           c[:, g * P:(g + 1) * P], start=True, stop=True)
                    else:
                        for h in range(H_HEADS):
                            mm = pe.matmul(ps[:, bank, h * P:(h + 1) * P], a[:, 2 * h * P:(2 * h + 1) * P],
                                           c[:, (2 * h + 1) * P:(2 * h + 2) * P], start=True, stop=True)
                    mm.then_inc(lev_prod, 1)
                pe.wait_ge(lev_kept, l * NG + NG)
                for h in range(H_HEADS):
                    v = [hv[:, t * 512 + h * P:t * 512 + (h + 1) * P] for t in range(TB)]
                    o = [ps[:, ACC + 2 + t, h * P:(h + 1) * P] for t in range(TB)]
                    pe.matmul(o[0], att[:, 2 * h * P:(2 * h + 1) * P], v[0], start=True, stop=True)
                    pe.matmul(o[1], attx[:, h * P:(h + 1) * P], v[0], start=True, stop=False)
                    mm = pe.matmul(o[1], att[:, (2 * h + 1) * P:(2 * h + 2) * P], v[1], start=False, stop=True)
                mm.then_inc(h_out, 1)
                pe.wait_ge(f_cum, l + 1)
                for t in range(TB):
                    mm = pe.matmul(ps[:, TR, 8 * t:8 * t + 8], fcs_c[:, t * P:(t + 1) * P], ident[0:8, 0:8], start=True, stop=True)
                mm.then_inc(f_cumT, 1)
                pe.wait_ge(f_cumS, l + 1)
                NA = X_HEADS * TB

                def fox_score(i):
                    h, t = divmod(i, 2)
                    w, r, j = P * (t + 1), h % 2 * 64, h // 2
                    if i >= 2:
                        pe.wait_ge(a_masked, l * NA + i - 1)
                    o = ps[:, TR + i % 2, 0:w]
                    pe.matmul(o, fq[r:r + 64, j * SEQ + t * P:j * SEQ + (t + 1) * P], fk[r:r + 64, j * SEQ:j * SEQ + w], start=True, stop=False)
                    pe.matmul(o, con("sel", h * P, P, 8), fcs_n[:, 0:w], start=False, stop=True).then_inc(a_score, 1)

                def fox_turn(i):
                    pe.wait_ge(a_prob, l * NA + i + 1)
                    if i >= 2:
                        pe.wait_ge(a_pT, l * NA + i - 1)
                    for k in range(i % 2 + 1):
                        mm = pe.transpose(ps[:, G + i % 2, k * P:(k + 1) * P], fp[:, i % 4 * 256 + k * P:i % 4 * 256 + (k + 1) * P], ident[:, :])
                    mm.then_inc(a_turn, 1)

                def fox_out(i):
                    h, t = divmod(i, 2)
                    pe.wait_ge(a_pT, l * NA + i + 1)
                    for k in range(t + 1):
                        mm = pe.matmul(ps[:, ACC + t, h * 64:(h + 1) * 64], fpT[:, i % 2 * 256 + k * P:i % 2 * 256 + (k + 1) * P],
                                       fv[:, k * 512 + h * 64:k * 512 + (h + 1) * 64], start=(k == 0), stop=(k == t))
                    mm.then_inc(a_out, 1)

                for i in range(NA + 3):
                    if i < NA:
                        fox_score(i)
                    if 2 <= i < NA + 2:
                        fox_turn(i - 2)
                    if i >= 3:
                        fox_out(i - 3)
                turn(turn_no(0, l, 2))
                for u in range(4):
                    tall_unit(0, l, A_OUT + u, from_hT(2 * u), ACC, u == 0, u == 3)
                turn(turn_no(0, l, 3))
                for i in range(6):
                    if i == 4:
                        turn(turn_no(0, l, 4))
                    chunk(0, l, A_K + 2 * i, PAIRS[i % 3], i not in (2, 3), 7 + i - 3 if i >= 3 else None)
                pe.wait_ge(chunk_out, chunk_no(0, l, 13))
                NC = C_HEADS * TB

                def cross_score(i):
                    h, t = divmod(i, 2)
                    if i >= 2:
                        pe.wait_ge(c_prob, l * NC + i - 1)
                    q, k_ = (hg, fq)[h // 2], (zf, hq)[h // 2]
                    for k in range(2):
                        at = (2 * (h % 2) + k) * SEQ
                        mm = pe.matmul(ps[:, TR + i % 2, 0:SEQ], q[:, at + t * P:at + (t + 1) * P], k_[:, at:at + SEQ], start=(k == 0), stop=(k == 1))
                    mm.then_inc(c_score, 1)

                def cross_turn(i):
                    pe.wait_ge(c_prob, l * NC + i + 1)
                    if i >= 2:
                        pe.wait_ge(c_pT, l * NC + i - 1)
                    for k in range(2):
                        mm = pe.transpose(ps[:, G + i % 2, k * P:(k + 1) * P], fp[:, i % 4 * 256 + k * P:i % 4 * 256 + (k + 1) * P], ident[:, :])
                    mm.then_inc(c_turn, 1)

                def cross_out(i):
                    h, t = divmod(i, 2)
                    v = (hk, hv)[h // 2]
                    pe.wait_ge(c_pT, l * NC + i + 1)
                    for k in range(2):
                        at = k * 512 + h % 2 * C_D
                        mm = pe.matmul(ps[:, ACC + 2 * t + h // 2, h % 2 * C_D:(h % 2 + 1) * C_D],
                                       fpT[:, i % 2 * 256 + k * P:i % 2 * 256 + (k + 1) * P], v[:, at:at + C_D], start=(k == 0), stop=(k == 1))
                    mm.then_inc(c_out, 1)

                for i in range(NC + 3):
                    if i < NC:
                        cross_score(i)
                    if 2 <= i < NC + 2:
                        cross_turn(i - 2)
                    if i >= 3:
                        cross_out(i - 3)
                turn(turn_no(0, l, 5))
                for u in range(4):
                    tall_unit(0, l, A_O + u, from_hT(2 * u), ACC, u == 0, u == 3)
                ffn(0, l, A_FFN2, 1, turn_no(0, l, 6))

            pe.wait_ge(loaded, N_LOADS * 16 + 16)
            with pe.Fori(0, DEPTH) as l:
                ffn(1, l, B_FFN1, 0, turn_no(1, l, 0))
                turn(turn_no(1, l, 1))
                for i in range(11):
                    chunk(1, l, B_IN + 2 * i, PAIRS[i % 3], i == 0, i - 3 if i >= 3 else None)
                pe.wait_ge(chunk_out, chunk_no(1, l, 11))
                for t in range(TB):
                    pe.wait_ge(r_rot, l * TB + t + 1)
                    for k in range(4):
                        mm = pe.transpose(ps[:, TR + t, k * P:(k + 1) * P], qk_rot[:, t * 512 + k * P:t * 512 + (k + 1) * P], ident[:, :])
                    mm.then_inc(r_turn, 1)

                def key_scores(qk, bank, done):
                    for n, h in enumerate(HEAD_ORDER):
                        r, j = h % 2 * 64, h // 2
                        if n == 2:
                            pe.wait_ge(done, 2 * l + 1)
                        q = qk[r:r + 64, j * SEQ:(j + 1) * SEQ]
                        k = qk[r:r + 64, (2 + j) * SEQ:(3 + j) * SEQ]
                        pe.matmul(ps[:, bank + n // 2, n % 2 * SEQ:(n % 2 + 1) * SEQ], k[:, 0:P], q, start=True, stop=True)
                        mm = pe.matmul(ps[:, bank + 2, n * P:(n + 1) * P], k[:, P:SEQ], q[:, P:SEQ], start=True, stop=True)
                        if n % 2:
                            mm.then_inc(done, 1)

                key_scores(qk_sb, 3, s_score)
                pe.wait_ge(r_kT, TB * (l + 1))
                key_scores(qk_rT, 0, r_score)
                pe.wait_ge(s_fail, l + 1)
                for g in range(4):
                    u = [vu[:, t * 512 + 256 + g * 64:t * 512 + 256 + (g + 1) * 64] for t in range(TB)]
                    o = ps[0:64, G + g // 2, g % 2 * SEQ:(g % 2 + 1) * SEQ]
                    m = [con("pool", (3 * g + n) * P, P) for n in range(3)]
                    pe.matmul(o[:, 0:P], u[0], m[0], start=True, stop=True)
                    pe.matmul(o[:, P:SEQ], u[0], m[1], start=True, stop=False)
                    mm = pe.matmul(o[:, P:SEQ], u[1], m[2], start=False, stop=True)
                mm.then_inc(p_diff, 1)
                pe.wait_ge(r_dec, l + 1)
                later, all_ = con("neg_later"), con("neg_ones")
                for n in range(2):
                    pe.matmul(ps[:, n, :], later, st3[:, n * 512:(n + 1) * 512], start=True, stop=False, skip_group_check=True)
                    pe.matmul(ps[:, n, :].rearrange("p (h b c) -> p h b c", h=2, b=2)[:, :, 1, :], all_,
                              st3[:, 1024 + n * 256:1024 + (n + 1) * 256], start=False, stop=True, skip_group_check=True)
                pe.matmul(ps[:, 2, :], later, st3[:, 1024:1536], start=True, stop=True).then_inc(s_after, 1)
                for n, h in enumerate(HEAD_ORDER):
                    v = [v_r[:, t * 512 + h * P:t * 512 + (h + 1) * P] for t in range(TB)]
                    o = [ps[:, TR + t, h * P:(h + 1) * P] for t in range(TB)]
                    pe.matmul(o[0], sc_r[:, 2 * n * P:(2 * n + 1) * P], v[0], start=True, stop=True)
                    pe.matmul(o[1], sc_r[:, (2 * n + 1) * P:(2 * n + 2) * P], v[0], start=True, stop=False)
                    mm = pe.matmul(o[1], sc_r[:, 1024 + n * P:1024 + (n + 1) * P], v[1], start=False, stop=True)
                mm.then_inc(r_out, 1)
                pe.wait_ge(p_dT, l + 1)
                pe.wait_ge(p_wl, l + 1)
                pe.wait_ge(s_w, l + 1)
                for n, h in enumerate(HEAD_ORDER):
                    r = h % 2 * 64
                    v = [vu[:, t * 512 + h * 64:t * 512 + (h + 1) * 64] for t in range(TB)]
                    o = ps[r:r + 64, 3, h // 2 * SEQ:(h // 2 + 1) * SEQ]
                    pe.matmul(o[:, 0:P], v[0], st2[:, 2 * n * P:(2 * n + 1) * P], start=True, stop=True)
                    pe.matmul(o[:, P:SEQ], v[0], st2[:, (2 * n + 1) * P:(2 * n + 2) * P], start=True, stop=False)
                    mm = pe.matmul(o[:, P:SEQ], v[1], st2[:, 1024 + n * P:1024 + (n + 1) * P], start=False, stop=True)
                mm.then_inc(s_out, 1)
                for g in range(4):
                    r = g % 2 * 64
                    mm = pe.matmul(ps[r:r + 64, 4, g // 2 * SEQ:(g // 2 + 1) * SEQ], wpool_l[:, g, :], pool_d[0:64, g * SEQ:(g + 1) * SEQ],
                                   start=True, stop=True)
                mm.then_inc(p_out, 1)
                for t in range(TB):
                    pe.wait_ge(r_y, l + 1)
                    for k in range(4):
                        mm = pe.transpose(ps[:, TR + t, k * P:(k + 1) * P], v_r[:, t * 512 + k * P:t * 512 + (k + 1) * P], ident[:, :])
                    mm.then_inc(r_yT, 1)
                pe.wait_ge(s_lo, l + 1)
                pe.wait_ge(p_lo, l + 1)
                tall_unit(1, l, B_BR, from_hT(0), 0, True, True)
                pe.wait_ge(r_lo, TB * (l + 1))
                tall_unit(1, l, B_BR + 1, from_hT(2), 4, True, False)
                tall_unit(1, l, B_BR + 2, from_hT(4), 4, False, True)
                pe.wait_ge(br_used, 2 * l + 1)
                tall_unit(1, l, B_BR + 3, from_hT(6), 0, True, True)
                turn(turn_no(1, l, 2))
                for u in range(4):
                    tall_unit(1, l, B_OUT + u, from_hT(2 * u), ACC, u == 0, u == 3)
                ffn(1, l, B_FFN2, 1, turn_no(1, l, 3))

        @block.vector
        def _(dve):
            dve.wait_ge(x_loaded, 16)
            dve.sem_inc(x_ready, 2)
            dve.wait_ge(loaded, N_LOADS * 16)
            step, count = stepper(dve, vstep, 0)

            def absolute(o, z):
                return dve.scalar_tensor_tensor(out=o, in0=z, scalar=-1.0, in1=z, op0=ALU.mult, op1=ALU.max)

            dve.memset(ln_lb[:, 0, :], MASKED)
            dve.memset(ln_1mlb[:, 0, :], 0.0)
            step(dve.tensor_tensor(lbw[:, 0, :], lbt[:, 1, :], lbt[:, 0, :], ALU.subtract))
            absolute(lbw[:, 1, :], lbw[:, 0, :]).then_inc(lb_abs, 1)
            dve.wait_ge(lb_sp, 2)
            dve.scalar_tensor_tensor(out=ln_lb[:, 1, :], in0=lbw[:, 0, :], scalar=0.0, in1=lbw[:, 1, :], op0=ALU.min, op1=ALU.subtract)
            step(dve.scalar_tensor_tensor(out=lbw[:, 2, :], in0=lbw[:, 0, :], scalar=0.0, in1=lbw[:, 1, :], op0=ALU.max, op1=ALU.add))
            step(dve.tensor_scalar(ln_1mlb[:, 1, :], lbw[:, 2, :], -1.0, None, ALU.mult))
            assert count[0] == V_START, ("V_START", count[0])

            def norm(n, src, out, ready):
                for t in range(TB):
                    dve.wait_ge(sq_done, 2 * n + t + 1)
                    step(dve.reciprocal(stat[:, 4 + t:5 + t], stat[:, 2 + t:3 + t]))
                    if t == 0:
                        dve.wait_ge(gain_loaded, 16 * n + 16)
                    dve.scalar_tensor_tensor(out=out[:, t, :], in0=src[:, t, :], scalar=stat[:, 4 + t:5 + t], in1=gain[:, :],
                                             op0=ALU.mult, op1=ALU.mult).then_inc(ready, 1)

            def turn_out(T):
                for i in range(2 * TB):
                    t, h = divmod(i, 2)
                    dve.wait_ge(turn_hi, 4 * T + i + 1)
                    at = lambda m: m[:, t, 4 * h:4 * h + 4, :].rearrange("p k c -> p (k c)")
                    dve.tensor_tensor(at(hT_lo), ps[:, TR + h, :], at(hT_hi).bitcast(F32), ALU.subtract).then_inc(turn_lo, 1)

            def add(b, l, off, factor):
                wait_unit(dve, b, l, off)
                for t in range(TB):
                    dve.scalar_tensor_tensor(out=xres[:, t, :], in0=ps[:, ACC + 2 * t:ACC + 2 * t + 2, :].rearrange("p a c -> p (a c)"),
                                             scalar=factor, in1=xres[:, t, :], op0=ALU.mult, op1=ALU.add).then_inc(x_ready, 1)

            def ffn(b, l, off, e, T, n):
                f = ffn_no(b, l, e)

                def product(stp):
                    for t in range(TB):
                        dve.wait_ge(silu_done, 2 * FF_STEPS * f + 2 * stp + t + 1)
                        dve.tensor_tensor(prod[:, t, :], silu_g[:, t, :], ps[:, G + t, 256:512], ALU.mult).then_inc(prod_ready, 1)

                def rest(stp):
                    dve.wait_ge(act_hi, FF_STEPS * f + stp + 1)
                    flat = lambda m: m[:, :, :, :].rearrange("p k t c -> p (k t c)")
                    dve.tensor_tensor(flat(aT_lo), ps[:, TR, :], flat(aT_hi).bitcast(F32), ALU.subtract).then_inc(act_lo, 1)

                norm(n, xres, xn, xn_ready)
                turn_out(T)
                product(0)
                with dve.Fori(0, FF_STEPS - 1) as c:
                    rest(c)
                    product(c + 1)
                rest(FF_STEPS - 1)
                add(b, l, off + FFN_UNITS - 1, 0.5)

            def head_norm(squares, o, summed, rooted):
                dve.tensor_reduce(hst[:, 0, :], squares.rearrange("p (g c) -> p g c", g=8), AX, ALU.add).then_inc(summed, 1)
                dve.wait_ge(*rooted)
                step(dve.reciprocal(hst[:, 2, :], hst[:, 1, :]))
                o3 = o.rearrange("p (g c) -> p g c", g=8)
                step(dve.tensor_tensor(o3, o3, hst[:, 2, :].unsqueeze(2).broadcast_to([P, 8, P]), ALU.mult))

            with dve.Fori(0, DEPTH) as l:
                step, count = stepper(dve, vstep, V_START + l * V_A)
                dve.tensor_copy(lb_l[:, 0, :], ln_lb[:, bass.ds(l, 1), :].rearrange("p a h -> p (a h)"))
                dve.tensor_copy(lb_l[:, 1, :], ln_1mlb[:, bass.ds(l, 1), :].rearrange("p a h -> p (a h)"))
                step(dve.tensor_copy(onorm_l[:, :], onorm[:, bass.ds(l, 1), :].rearrange("p a h -> p (a h)")))
                ffn(0, l, A_FFN1, 0, turn_no(0, l, 0), norm_no(0, l, 0))
                norm(norm_no(0, l, 1), xres, xn, xn_ready)
                turn_out(turn_no(0, l, 1))
                dve.wait_ge(chunk_out, chunk_no(0, l, 0) + 1)
                absolute(tmp1, zf).then_inc(h_abs, 1)
                dve.wait_ge(f_logit, l + 1)
                absolute(fcs_t, fcs_f).then_inc(f_abs, 1)
                dve.wait_ge(h_sp, l + 1)
                dve.scalar_tensor_tensor(out=hk, in0=zf, scalar=0.0, in1=tmp1, op0=ALU.max, op1=ALU.add)
                step(dve.scalar_tensor_tensor(out=tmp2, in0=zf, scalar=0.0, in1=tmp1, op0=ALU.min, op1=ALU.subtract))

                def head(m, h):
                    return m[:, h * SEQ:(h + 1) * SEQ]

                for h in range(H_HEADS):
                    last = dve.tensor_scalar(head(tmp1, h), head(tmp2, h), lb_l[:, 1, h:h + 1], None, ALU.add)
                step(last)
                for h in range(H_HEADS):
                    dve.tensor_scalar(head(zf, h), head(tmp1, h), lb_l[:, 0, h:h + 1], None, ALU.max)
                    last = dve.tensor_scalar(head(lev2, h), head(tmp1, h), lb_l[:, 0, h:h + 1], None, ALU.subtract)
                step(last)
                absolute(lev2[:, 0:1024], lev2[:, 0:1024]).then_inc(h_gate, 1)
                dve.wait_ge(f_sp, l + 1)
                step(dve.scalar_tensor_tensor(out=fcs_f, in0=fcs_f, scalar=0.0, in1=fcs_t, op0=ALU.min, op1=ALU.subtract))
                step(dve.tensor_tensor_scan(fcs_c, con("ones", rows=8), fcs_f, 0.0, ALU.mult, ALU.add))
                dve.tensor_scalar(fcs_n, fcs_c, -1.0, None, ALU.mult).then_inc(f_cum, 1)
                dve.memset(att, 0.0)
                dve.wait_ge(h_sp2, l + 1)
                step(dve.tensor_tensor(zf, zf, lev2[:, 0:1024], ALU.add))
                for h in range(H_HEADS):
                    last = dve.tensor_tensor_scan(head(cum, h), con("reset"), head(zf, h), 0.0, ALU.mult, ALU.add)
                step(last)
                NL = len(LEVELS) + 1
                NG = NL + 1

                def level(n, m_):
                    m = LEVELS[n] if n < NL - 1 else P
                    return m, m_.rearrange("p (b c) -> p b c", c=2 * m)

                def lev(n):
                    return lev2[:, n % 2 * 1024:n % 2 * 1024 + 1024]

                def diff(n):
                    m, e = level(n, lev(n))
                    g = level(n, cum)[1]
                    B = 1024 // (2 * m)
                    end = g[:, :, m - 1:m].broadcast_to([P, B, m])
                    dve.tensor_tensor(e[:, :, 0:m], end, g[:, :, 0:m], ALU.subtract)
                    if n < NL - 1:
                        last = dve.tensor_tensor(e[:, :, m:2 * m], g[:, :, m:2 * m], end, ALU.subtract)
                    else:
                        last = dve.tensor_copy(e[:, :, m:2 * m], g[:, :, m:2 * m])
                    last.then_inc(lev_diff, 1)

                def decayed(n):
                    m, e = level(n, lev(n))
                    dve.wait_ge(lev_exp, l * NL + n + 1)
                    dve.tensor_tensor(e[:, :, 0:m], e[:, :, 0:m], level(n, hk)[1][:, :, 0:m], ALU.mult)
                    dve.tensor_tensor(e[:, :, m:2 * m], e[:, :, m:2 * m], level(n, hq)[1][:, :, m:2 * m], ALU.mult).then_inc(lev_ready, 1)

                def keep(n):
                    bank = ACC + 2 * (n % 2)
                    mask = ident[:, :] if n == 0 else con("level", (n - 1) * P, P)
                    dve.copy_predicated(att.rearrange("p (g c) -> p g c", c=P),
                                        mask.bitcast(I32).unsqueeze(1).broadcast_to([P, 8, P]),
                                        ps[:, bank:bank + 2, :].rearrange("p a (g c) -> p (a g) c", c=P)).then_inc(lev_kept, 1)

                diff(0)
                dve.wait_ge(h_key, H_HEADS * (l + 1))
                for n in range(NL):
                    decayed(n)
                    if n + 1 < NL:
                        dve.wait_ge(lev_prod, l * NG + n + 1)
                        if n:
                            dve.wait_ge(lev_kept, l * NG + n)
                        diff(n + 1)
                        keep(n)
                dve.wait_ge(lev_prod, l * NG + NG)
                dve.wait_ge(lev_kept, l * NG + NL - 1)
                dve.tensor_copy(attx, ps[:, ACC + 2 * ((NG - 1) % 2), :]).then_inc(lev_kept, 1)
                keep(NL - 1)
                dve.wait_ge(h_sq, l + 1)
                head_norm(tmp1, tmp2, h_sum, (h_rms, l + 1))
                o3 = tmp2.rearrange("p (g c) -> p g c", g=8)
                step(dve.tensor_tensor(o3, o3, onorm_l[:, :].unsqueeze(1).broadcast_to([P, 8, P]), ALU.mult))
                dve.tensor_tensor(xn[:, :, 0:512], tmp2.rearrange("p (t c) -> p t c", t=TB), hg.rearrange("p (t c) -> p t c", t=TB), ALU.mult)
                dve.wait_ge(f_cumS, l + 1)
                NA = X_HEADS * TB
                for i in range(NA):
                    h, t = divmod(i, 2)
                    w, at = P * (t + 1), i % 4 * 256
                    dve.wait_ge(a_score, l * NA + i + 1)
                    if i >= 4:
                        dve.wait_ge(a_prob, l * NA + i - 3)
                    dve.scalar_tensor_tensor(out=fsc[:, at:at + w], in0=ps[:, TR + i % 2, 0:w], scalar=sst[:, 3, 8 * t + h:8 * t + h + 1],
                                             in1=con("zeros", P - t * P, w), op0=ALU.add, op1=ALU.add).then_inc(a_masked, 1)
                    dve.wait_ge(a_masked, l * NA + i + 1)
                    step(dve.tensor_reduce(sst[:, 0, i:i + 1], fsc[:, at:at + w], AX, ALU.max))
                    dve.tensor_scalar(sst[:, 1, i:i + 1], sst[:, 0, i:i + 1], -1.0, None, ALU.mult).then_inc(a_max, 1)
                dve.wait_ge(a_out, l * NA + NA)
                step(dve.reciprocal(sst[:, 4, :], sst[:, 2, :]))
                for t in range(TB):
                    dve.tensor_tensor(xn[:, t, 512:1024].rearrange("p (h d) -> p h d", h=X_HEADS),
                                      ps[:, ACC + t, :].rearrange("p (h d) -> p h d", h=X_HEADS),
                                      sst[:, 4, :].rearrange("p (h t) -> p t h", t=TB)[:, t, :].unsqueeze(2).broadcast_to([P, X_HEADS, X_D]),
                                      ALU.mult).then_inc(xn_ready, 1)
                turn_out(turn_no(0, l, 2))
                add(0, l, A_OUT + 3, 1.0)
                norm(norm_no(0, l, 2), memx, xn, xn_ready)
                turn_out(turn_no(0, l, 3))
                norm(norm_no(0, l, 3), xres, xn, xn_ready)
                turn_out(turn_no(0, l, 4))
                NC = C_HEADS * TB
                for i in range(NC):
                    dve.wait_ge(c_score, l * NC + i + 1)
                    step(dve.tensor_reduce(sst[:, 0, i:i + 1], ps[:, TR + i % 2, 0:256], AX, ALU.max))
                    dve.tensor_scalar(sst[:, 1, i:i + 1], sst[:, 0, i:i + 1], -1.0, None, ALU.mult).then_inc(c_max, 1)
                dve.wait_ge(c_out, l * NC + NC)
                step(dve.reciprocal(sst[:, 4, 0:NC], sst[:, 2, 0:NC]))
                for t in range(TB):
                    dve.tensor_tensor(xn[:, t, :].rearrange("p (h d) -> p h d", h=C_HEADS),
                                      ps[:, ACC + 2 * t:ACC + 2 * t + 2, :].rearrange("p a (h d) -> p (a h) d", d=C_D),
                                      sst[:, 4, 0:NC].rearrange("p (h t) -> p t h", t=TB)[:, t, :].unsqueeze(2).broadcast_to([P, C_HEADS, C_D]),
                                      ALU.mult).then_inc(xn_ready, 1)
                turn_out(turn_no(0, l, 5))
                add(0, l, A_O + 3, 1.0)
                ffn(0, l, A_FFN2, 1, turn_no(0, l, 6), norm_no(0, l, 4))
                assert count[0] == V_A, ("V_A", count[0])
            step, count = stepper(dve, vstep, V_START + DEPTH * V_A)
            norm(norm_no(0, DEPTH, 0), xres, xres, x_ready)
            assert count[0] == V_BETWEEN, ("V_BETWEEN", count[0])
            dve.wait_ge(loaded, N_LOADS * 16 + 16)
            with dve.Fori(0, DEPTH) as l:
                step, count = stepper(dve, vstep, V_START + DEPTH * V_A + V_BETWEEN + l * V_B)
                dve.tensor_copy(wpool_l[:, :, :].rearrange("p g c -> p (g c)"), wpool[:, bass.ds(l, 1), :, :].rearrange("p a g c -> p (a g c)"))
                step(dve.tensor_copy(pscale_l[:, :], pscale[:, bass.ds(l, 1), :].rearrange("p a k -> p (a k)")))
                dve.sem_inc(p_wl, 1)
                ffn(1, l, B_FFN1, 0, turn_no(1, l, 0), norm_no(1, l, 0))
                norm(norm_no(1, l, 1), xres, xn, xn_ready)
                turn_out(turn_no(1, l, 1))
                dve.wait_ge(chunk_out, chunk_no(1, l, 1) + 1)
                parts = []
                for t, tmp in enumerate((st1, st3)):
                    xx = qk_r[:, t * 512:(t + 1) * 512].rearrange("p (h d) -> p h d", h=8)
                    x1, x2 = xx[:, :, 0:32], xx[:, :, 32:64]
                    cos, sin = (con(n, t * 32, 32).unsqueeze(1).broadcast_to([P, 8, 32]) for n in ("cos", "sin"))
                    q = [tmp[:, n * 256:(n + 1) * 256].rearrange("p (h d) -> p h d", h=8) for n in range(4)]
                    for o, a, c in zip(q, (x1, x2, x2, x1), (cos, sin, cos, sin)):
                        last = dve.tensor_tensor(o, a, c, ALU.mult)
                    parts.append(q)
                step(last)
                for t, q in enumerate(parts):
                    rot = qk_rot[:, t * 512:(t + 1) * 512].rearrange("p (h d) -> p h d", h=8)
                    dve.tensor_tensor(rot[:, :, 0:32], q[0], q[1], ALU.subtract)
                    dve.tensor_tensor(rot[:, :, 32:64], q[2], q[3], ALU.add).then_inc(r_rot, 1)
                zs = ps[:, 3:6, :].rearrange("p a c -> p (a c)")
                dve.wait_ge(r_score, 2 * l + 2)
                dve.tensor_tensor(sc_r[:, 0:1024], ps[:, 0:2, :].rearrange("p a c -> p (a c)"), con("decay"), ALU.mult)
                dve.tensor_tensor(sc_r[:, 1024:1536].rearrange("p (h c) -> p h c", h=4), ps[:, 2, :].rearrange("p (h c) -> p h c", h=4),
                                  con("decay").rearrange("p (h o c) -> p h o c", h=4, o=2)[:, :, 0, :], ALU.mult).then_inc(r_dec, 1)
                dve.wait_ge(r_turn, TB * (l + 1))
                dve.wait_ge(s_sp, l + 1)
                dve.scalar_tensor_tensor(out=st2, in0=zs, scalar=0.0, in1=st1, op0=ALU.min, op1=ALU.subtract)
                step(dve.scalar_tensor_tensor(out=st3, in0=zs, scalar=0.0, in1=st1, op0=ALU.max, op1=ALU.add))

                def masked(m):
                    strict = con("strict").unsqueeze(1).broadcast_to([P, 4, P])
                    a = m[:, 0:1024].rearrange("p (h o c) -> p h o c", h=4, o=2)[:, :, 0, :]
                    c = m[:, 1024:1536].rearrange("p (h c) -> p h c", h=4)
                    dve.tensor_tensor(a, a, strict, ALU.mult)
                    return dve.tensor_tensor(c, c, strict, ALU.mult)

                masked(st3).then_inc(s_fail, 1)
                dve.wait_ge(s_after, l + 1)
                dve.tensor_tensor(st2, st2, ps[:, 0:3, :].rearrange("p a c -> p (a c)"), ALU.add).then_inc(s_sum, 1)
                dve.wait_ge(s_exp, l + 1)
                masked(st2).then_inc(s_w, 1)
                dve.wait_ge(r_sq, l + 1)
                head_norm(qk_sb, v_r, r_sum, (r_rms, l + 1))
                dve.tensor_tensor(v_r, v_r, g_r, ALU.mult).then_inc(r_y, 1)
                dve.wait_ge(s_hi, l + 1)
                dve.tensor_tensor(hT_lo[:, :, 0:2, :].rearrange("p t k c -> p k t c"), ps[:, 3, :].rearrange("p (k t c) -> p k t c", k=2, t=TB),
                                  hT_hi[:, :, 0:2, :].rearrange("p t k c -> p k t c").bitcast(F32), ALU.subtract).then_inc(s_lo, 1)
                dve.wait_ge(p_hi, 2 * l + 2)
                for k in range(2):
                    last = dve.scalar_tensor_tensor(out=hT_lo[:, :, 6 + k, :], in0=ps[:, 4, k * 256:(k + 1) * 256].rearrange("p (t c) -> p t c", t=TB),
                                                    scalar=pscale_l[:, k:k + 1], in1=hT_hi[:, :, 6 + k, :].bitcast(F32),
                                                    op0=ALU.mult, op1=ALU.subtract)
                last.then_inc(p_lo, 1)
                for t in range(TB):
                    dve.wait_ge(r_hi, l * TB + t + 1)
                    dve.tensor_tensor(hT_lo[:, t, 2:6, :].rearrange("p k c -> p (k c)"), ps[:, TR + t, :],
                                      hT_hi[:, t, 2:6, :].rearrange("p k c -> p (k c)").bitcast(F32), ALU.subtract).then_inc(r_lo, 1)

                def gated(out, n, bank, t):
                    return dve.tensor_tensor(out.rearrange("p (h c) -> p h c", h=2), ps[:, bank + 2 * t:bank + 2 * t + 2, :],
                                             gates[:, n * 2048:(n + 1) * 2048].rearrange("p (h t c) -> p t h c", h=2, t=TB)[:, t], ALU.mult)

                def tmp(t):
                    return br_tmp[:, t * DM:(t + 1) * DM]

                wait_unit(dve, 1, l, B_BR)
                for t in range(TB):
                    last = gated(xn[:, t, :], 0, 0, t)
                last.then_inc(br_used, 1)
                wait_unit(dve, 1, l, B_BR + 2)
                for t in range(TB):
                    last = gated(tmp(t), 1, 4, t)
                step(last)
                dve.wait_ge(br_used, 2 * l + 1)
                for t in range(TB):
                    last = dve.tensor_tensor(xn[:, t, :], xn[:, t, :], tmp(t), ALU.add)
                last.then_inc(br_used, 1)
                dve.wait_ge(br_used, 2 * l + 2)
                wait_unit(dve, 1, l, B_BR + 3)
                for t in range(TB):
                    step(gated(tmp(t), 2, 0, t))
                    dve.tensor_tensor(xn[:, t, :], xn[:, t, :], tmp(t), ALU.add).then_inc(xn_ready, 1)
                turn_out(turn_no(1, l, 2))
                add(1, l, B_OUT + 3, 1.0)
                ffn(1, l, B_FFN2, 1, turn_no(1, l, 3), norm_no(1, l, 2))
                assert count[0] == V_B, ("V_B", count[0])
            step, count = stepper(dve, vstep, V_START + DEPTH * V_A + V_BETWEEN + DEPTH * V_B)
            norm(norm_no(1, DEPTH, 0), xres, xres, x_ready)


FFN_NAMES = {(0, 0): ("ffn1_w_gate", "ffn1_w_up", "ffn1_w_down"), (0, 1): ("ffn2_w_gate", "ffn2_w_up", "ffn2_w_down"),
             (1, 0): ("w1_ffn1_2", "w3_ffn1_2", "w2_ffn1_2"), (1, 1): ("w1_ffn2_2", "w3_ffn2_2", "w2_ffn2_2")}
WEIGHTS = ("w_in", "w_out", "cross_wq", "cross_wk", "cross_wv", "cross_wo", "w_in_2", "w_branch_sb_2", "w_branch_ret_2",
           "w_branch_pool_2", "w_out_2")
NORM_ORDER = (("ffn1_norm", "mix_norm", "mem_norm", "cross_norm", "ffn2_norm"), ("g_ffn1_2", "g_mix_2", "g_ffn2_2"))


def kernel(**inputs):
    import concourse.bacc as bacc
    from concourse.bass_utils import run_bass_kernel_spmd

    a = {k: np.asarray(v) for k, v in inputs.items()}
    gains = []
    for names, last in zip(NORM_ORDER, ("final_norm", "g_final_2")):
        gains += [a[n][l] for l in range(DEPTH) for n in names] + [a[last]]
    table_a, table_b, eye = constants()
    small = dict(
        x=a["x"], mem=a["mem"], gains=np.stack(gains), table_a=table_a, table_b=table_b, eye=eye,
        lb=a["hgrn_lb"].reshape(DEPTH, H_HEADS, P).transpose(2, 0, 1), out_norm=a["hgrn_out_norm"],
        f_bias=a["fox_f_bias"].T, w_pool=a["w_pool_2"].transpose(2, 0, 1, 3),
        pool_scale=a["pool_scale_2"].reshape(DEPTH, 2, P).transpose(2, 0, 1))
    big = {n: a[n] for n in WEIGHTS} | {n: a[n] for names in FFN_NAMES.values() for n in names}
    nc = bacc.Bacc("TRN2", target_bir_lowering=False, num_devices=1)
    arrays, aps = {}, {}
    for name, v in (small | big).items():
        arrays["in_" + name] = np.ascontiguousarray(v)
        aps[name] = nc.dram_tensor("in_" + name, v.shape, mybir.dt.from_np(v.dtype), kind="ExternalInput").ap()
    out = nc.dram_tensor("out_0", (1, SEQ, DM), F32, kind="ExternalOutput").ap()
    W = {n: aps[n] for n in WEIGHTS}
    for (b, e), names in FFN_NAMES.items():
        for what, n in zip(("gate", "up", "down"), names):
            W[b, e, what] = aps[n]
    build(nc, *(aps[n] for n in small), W, out)
    r = run_bass_kernel_spmd(nc, [arrays], core_ids=[0])
    return r.results[0]["out_0"]
```

```python
from contextlib import ExitStack

import numpy as np
import concourse.bass as bass
from concourse import mybir

F32 = mybir.dt.float32
F32R = mybir.dt.float32r
I32 = mybir.dt.int32
ALU = mybir.AluOpType
ACT = mybir.ActivationFunctionType
AX = mybir.AxisListType.X

P = 128
SEQ, DM, DFF, DEPTH = 256, 1024, 2816, 2
TB = SEQ // P
KT = DM // P
EPS = 1e-6
FF_STEPS = DFF // 256
RING = 3
CREDIT = RING
FFN_UNITS = 3 * FF_STEPS
MASKED = -1e30
N_LOADS = 6
S_A, S_B = 3, 2
V_START, V_A, V_B = 3, 38, 10

A_FFN1 = 0
A_IN = FFN_UNITS
A_OUT = A_IN + 16
A_K = A_OUT + 4
A_V = A_K + 4
A_Q = A_V + 4
A_O = A_Q + 4
A_FFN2 = A_O + 4
A_UNITS = A_FFN2 + FFN_UNITS
B_FFN1 = 0
B_IN = FFN_UNITS
B_BR = B_IN + 22
B_OUT = B_BR + 4
B_FFN2 = B_OUT + 4
B_UNITS = B_FFN2 + FFN_UNITS
assert A_UNITS % RING == 0 and B_UNITS % RING == 0 and A_FFN2 % RING == 0 and B_FFN2 % RING == 0
LAYER_UNITS = (A_UNITS, B_UNITS)
FIRST_UNIT = (0, DEPTH * A_UNITS)

TURNS = (7, 4)
FIRST_TURN = (0, DEPTH * 7)
ROWS = (2, 1)
NORMS = (5, 3)
FIRST_NORM = (0, DEPTH * 5 + 1)
ADDS = (4, 3)
FIRST_ADD = (1, DEPTH * 4 + 2)

H_HEADS, H_D = 4, 128
X_HEADS, X_D = 8, 64
C_HEADS, C_D = 4, 256
PIECES = 2 * TB
HEAD_ORDER = (0, 2, 1, 3)
TAKEN = ("SVVVVSS" "SSSSVV", "SVSSSSSSSSS")
LEVELS = (64, 32, 16, 8, 4, 2, 1)
POOL_WINDOWS = (2, 4, 8, 16)

TABLES = (dict(level=128 * len(LEVELS), reset=256, zeros=128, causal=128, sel=1024, ones=256),
          dict(neg_later=128, neg_ones=128, strict=128, cos=64, sin=64, decay=1024, pool=1536))
CONST_AT = {name: (sum(list(t.values())[:n]), cols) for t in TABLES for n, (name, cols) in enumerate(t.items())}
N_CONST = max(sum(t.values()) for t in TABLES)


def constants():
    c = np.zeros((2, P, N_CONST), np.float32)

    def part(name):
        at, cols = CONST_AT[name]
        return c[0 if name in TABLES[0] else 1][:, at:at + cols]

    i = np.arange(P)
    s, t = i[:, None], i[None, :]
    for n, m in enumerate(LEVELS):
        part("level")[:, n * P:(n + 1) * P] = (s // (2 * m) == t // (2 * m)) & (s % (2 * m) < m) & (t % (2 * m) >= m)
    part("reset")[:] = (np.arange(SEQ) % P != 0)[None, :]
    part("causal")[:] = np.where(t <= s, 0.0, MASKED)
    for h in range(8):
        part("sel")[h, h * P:(h + 1) * P] = 1.0
    part("ones")[:] = 1.0
    part("neg_later")[:] = -(s > t).astype(np.float32)
    part("neg_ones")[:] = -1.0
    part("strict")[:] = s < t
    half = 32
    freq = np.float32(10000.0) ** (-np.arange(half, dtype=np.float32) / half)
    ang = np.arange(SEQ, dtype=np.float32)[:, None] * freq[None, :]
    for name, f in (("cos", np.cos), ("sin", np.sin)):
        part(name)[:] = f(ang).reshape(TB, P, half).transpose(1, 0, 2).reshape(P, TB * half)
    for h, head in enumerate(HEAD_ORDER):
        g = np.log(1.0 - 2.0 ** (-5.0 - head))
        for o in range(2):
            d = t + o * P - s
            w = np.where(d >= 0, np.exp(np.maximum(d, 0) * g), 0.0) * 64 ** -0.5
            part("decay")[:, (h * 2 + o) * P:(h * 2 + o + 1) * P] = w
    for n, win in enumerate(POOL_WINDOWS):
        for m, (sb, tb) in enumerate(((0, 0), (0, 1), (1, 1))):
            S, T = s + sb * P, t + tb * P
            count = np.minimum(T + 1, win)
            w = ((S <= T) & (S > T - win)) / count - (S == T)
            part("pool")[:, (n * 3 + m) * P:(n * 3 + m + 1) * P] = w
    return c[0], c[1], np.eye(P, dtype=np.float32)


def build(nc, x, mem, gains, table_a, table_b, eye, lb, out_norm, f_bias, w_pool, pool_scale, W, out):
    with ExitStack() as ctx:
        def sb(name, shape, dt=F32):
            return ctx.enter_context(nc.sbuf_tensor(name, shape, dt))

        def sem(name):
            return ctx.enter_context(nc.semaphore(name))

        raw = sb("raw", [P, RING, 4, 512])
        whi = sb("whi", [P, RING, 4, 512], F32R)
        wlo = sb("wlo", [P, RING, 4, 512], F32R)
        xres = sb("xres", [P, TB, DM])
        xn = sb("xn", [P, TB, DM])
        hT_hi = sb("hT_hi", [P, TB, KT, P], F32R)
        hT_lo = sb("hT_lo", [P, TB, KT, P], F32R)
        gain = sb("gain", [P, DM])
        silu_g = sb("silu_g", [P, TB, 256])
        prod = sb("prod", [P, TB, 256])
        aT_hi = sb("aT_hi", [P, 2, TB, P], F32R)
        aT_lo = sb("aT_lo", [P, 2, TB, P], F32R)
        ident = sb("ident", [P, P])
        cst = sb("cst", [P, N_CONST])
        stat = sb("stat", [P, 2, 3, TB])
        lbt = sb("lbt", [P, DEPTH, H_HEADS])
        lbw = sb("lbw", [P, 3, H_HEADS])
        lb_l = sb("lb_l", [P, 2, H_HEADS])
        onorm_l = sb("onorm_l", [P, H_D])
        pscale_l = sb("pscale_l", [P, 2])
        flog = sb("flog", [P, TB, 8])
        ln_lb = sb("ln_lb", [P, DEPTH, H_HEADS])
        ln_1mlb = sb("ln_1mlb", [P, DEPTH, H_HEADS])
        onorm = sb("onorm", [P, DEPTH, H_D])
        fbias = sb("fbias", [8, DEPTH])
        wpool = sb("wpool", [64, DEPTH, 4, 64])
        wpool_l = sb("wpool_l", [64, 4, 64])
        pscale = sb("pscale", [P, DEPTH, 2])
        sst = sb("sst", [P, 5, 16])
        hst = sb("hst", [P, 3, 8])
        arena = sb("arena", [P, 18432])

        def take(*spans):
            at, got = 0, []
            for n in spans:
                got.append(arena[:, at:at + n])
                at += n
            assert at <= 18432, at
            return got

        (memx_, zf, hq, hk, hv, hg, fq, fk, fv, cum, tmp1, tmp2, lev2, att, attx, fpT, fcs) = take(
            2048, *[1024] * 11, 2048, 1024, 512, 512, 1024)
        memx = memx_.rearrange("p (t d) -> p t d", t=TB)
        fsc, fp = lev2[:, 0:1024], lev2[:, 1024:2048]
        norm_diag, rms_row = fpT[:, 0:256], fpT[:, 256:512]
        sq_junk = lev2
        fcs_f, fcs_c, fcs_n, fcs_t = (fcs[0:8, 256 * n:256 * n + 256] for n in range(4))
        (qk_sb, qk_r, vu, v_r, g_r, pool_d, gates, st1, st2, st3, sc_r) = take(*[1024] * 6, 6144, *[1536] * 4)
        qk_rot = st2[:, 0:1024]
        qk_rT = qk_r
        br_tmp = arena[:, 12288:12288 + 2048]
        ps = ctx.enter_context(nc.psum_tensor("ps", [P, 8, 512], F32))
        ACC, G, TR = 0, 4, 6
        PAIRS = (4, 0, 2)

        def con(name, a=0, n=None, rows=P):
            at, cols = CONST_AT[name]
            return cst[0:rows, at + a:at + a + (cols if n is None else n)]

        loaded = sem("loaded")
        ident_loaded = sem("ident_loaded")
        lb_loaded = sem("lb_loaded")
        x_loaded = sem("x_loaded")
        gain_loaded = sem("gain_loaded")
        raw_loaded = [sem(f"raw_loaded{s}") for s in range(RING)]
        hi_ready = sem("hi_ready")
        lo_ready = sem("lo_ready")
        unit_done = sem("unit_done")
        acc_done = sem("acc_done")
        x_ready = sem("x_ready")
        sq_sum = sem("sq_sum")
        sq_done = sem("sq_done")
        inv_ready = sem("inv_ready")
        row_diag = sem("row_diag")
        row_made = sem("row_made")
        row_ready = sem("row_ready")
        xn_ready = sem("xn_ready")
        turned = sem("turned")
        turn_hi = sem("turn_hi")
        turn_lo = sem("turn_lo")
        silu_done = sem("silu_done")
        prod_ready = sem("prod_ready")
        act_turned = sem("act_turned")
        act_hi = sem("act_hi")
        act_lo = sem("act_lo")
        chunk_out = sem("chunk_out")
        feat_out = sem("feat_out")
        vstep = sem("vstep")
        sstep = sem("sstep")
        lb_abs, lb_sp, lb_done = sem("lb_abs"), sem("lb_sp"), sem("lb_done")
        h_abs, h_sp, h_gate, h_sp2 = sem("h_abs"), sem("h_sp"), sem("h_gate"), sem("h_sp2")
        h_key = sem("h_key")
        lev_diff, lev_exp, lev_ready, lev_prod, lev_kept = (sem(f"lev_{n}") for n in ("diff", "exp", "ready", "prod", "kept"))
        h_out, h_sq, h_sum, h_rms = sem("h_out"), sem("h_sq"), sem("h_sum"), sem("h_rms")
        f_abs, f_sp, f_cum, f_cumT, f_cumS = (sem(f"f_{n}") for n in ("abs", "sp", "cum", "cumT", "cumS"))
        f_tm, f_turn, f_logit = sem("f_tm"), sem("f_turn"), sem("f_logit")
        a_score, a_masked, a_max, a_prob, a_turn, a_pT, a_out = (
            sem(f"a_{n}") for n in ("score", "masked", "max", "prob", "turn", "pT", "out"))
        c_score, c_max, c_prob, c_turn, c_pT, c_out = (sem(f"c_{n}") for n in ("score", "max", "prob", "turn", "pT", "out"))
        r_rot, r_turn, r_kT, r_score, r_dec, r_out, r_sq, r_sum, r_rms, r_y, r_yT, r_hi, r_lo = (
            sem(f"r_{n}") for n in ("rot", "turn", "kT", "score", "dec", "out", "sq", "sum", "rms", "y", "yT", "hi", "lo"))
        s_score, s_sp, s_fail, s_after, s_sum, s_exp, s_w, s_out, s_hi, s_lo = (
            sem(f"s_{n}") for n in ("score", "sp", "fail", "after", "sum", "exp", "w", "out", "hi", "lo"))
        p_diff, p_dT, p_wl, p_out, p_hi, p_lo = (sem(f"p_{n}") for n in ("diff", "dT", "wl", "out", "hi", "lo"))
        br_done, br_used = sem("br_done"), sem("br_used")
        stored = sem("stored")

        def unit(b, l, off, c=0):
            return FIRST_UNIT[b] + l * LAYER_UNITS[b] + off + 3 * c

        def use(b, l, off, c=0):
            return FIRST_UNIT[b] // RING + l * (LAYER_UNITS[b] // RING) + off // RING + c + 1

        def turn_no(b, l, j):
            return FIRST_TURN[b] + l * TURNS[b] + j

        def norm_no(b, l, j):
            return FIRST_NORM[b] + l * NORMS[b] + j

        def add_no(b, l, j):
            return FIRST_ADD[b] + l * ADDS[b] + j

        def ffn_no(b, l, e):
            return 2 * DEPTH * b + 2 * l + e

        def acc_no(b, l, j):
            return (0, DEPTH * ADDS[0])[b] + l * ADDS[b] + j

        def row_no(b, l, j):
            return (0, DEPTH * ROWS[0])[b] + l * ROWS[b] + j

        def xn_no(b, T):
            return T + b

        def piece(m, i):
            return m[:, i % 2, i // 2 * 512:(i // 2 + 1) * 512]

        def taken_no(b, l, j, who):
            per_layer = [t.count(who) for t in TAKEN]
            return (0, DEPTH * per_layer[0])[b] + l * per_layer[b] + TAKEN[b][:j + 1].count(who)

        def wait_taken(eng, b, l, j):
            who = TAKEN[b][j]
            eng.wait_ge(chunk_out if who == "S" else feat_out, taken_no(b, l, j, who))

        def wait_unit(eng, b, l, off, c=0):
            eng.wait_ge(unit_done, unit(b, l, off, c) + 1 + CREDIT)

        def stepper(eng, done, base):
            count = [0]

            def step(ins):
                count[0] += 1
                ins.then_inc(done, 1)
                eng.wait_ge(done, base + count[0])

            return step, count

        block = ctx.enter_context(nc.Block())

        @block.sync
        def _(sp):
            sp.dma_start(xres[:, :, :], x[0].rearrange("(t p) d -> p t d", p=P)).then_inc(x_loaded, 16)

            def load(b, l, off, c, parts):
                s = off % RING
                sp.wait_ge(lo_ready, unit(b, l, off, c) + 1)
                for dst, src in reversed(parts(raw[:, s])):
                    sp.dma_start(dst, src).then_inc(raw_loaded[s], 16)

            def cols(a, b_):
                def parts(slot):
                    v = slot.rearrange("p k (t n) -> p k t n", t=2)
                    return [(v[:, :, t, :], src.rearrange("(k p) n -> p k n", p=P)) for t, src in enumerate((a, b_))]
                return parts

            def rows(w):
                def parts(slot):
                    v = slot.rearrange("p (k t) n -> p k (t n)", k=2)
                    return [(v[:, k, :], w[k * P:(k + 1) * P, :]) for k in range(2)]
                return parts

            def ffn(b, l, off, e):
                wg, wu, wd = W[b, e, "gate"], W[b, e, "up"], W[b, e, "down"]

                def gate_up(off, c, step):
                    for k in range(2):
                        load(b, l, off + k, c, cols(*(w[l, k * 512:(k + 1) * 512, bass.ds(step * 256, 256)] for w in (wg, wu))))

                def down(off, c, step):
                    load(b, l, off, c, rows(wd[l, bass.ds(step * 256, 256), :]))

                gate_up(off, 0, 0)
                with sp.Fori(0, FF_STEPS - 1) as c:
                    gate_up(off + 2, c, c + 1)
                    down(off + 4, c, c)
                down(off + FFN_UNITS - 1, 0, FF_STEPS - 1)

            def chunk(b, l, off, w, c0, c1):
                for k in range(2):
                    load(b, l, off + k, 0, cols(*(w[l, k * 512:(k + 1) * 512, a:a + 256] for a in (c0, c1))))

            def tall(b, l, off, n, w):
                for u in range(n):
                    load(b, l, off + u, 0, rows(w[l, u * 256:(u + 1) * 256, :]))

            with sp.Fori(0, DEPTH) as l:
                ffn(0, l, A_FFN1, 0)
                w = W["w_in"]
                for n, c0 in enumerate((1536, 512, 0, None, 2048, 2560, 3072, 1024)):
                    off = A_IN + 2 * n
                    if c0 is not None:
                        chunk(0, l, off, w, c0, c0 + 256)
                        continue
                    for k in range(2):
                        load(0, l, off + k, 0, lambda slot, k=k: [
                            (slot[:, 2 * i:2 * i + 2, 0:8],
                             w[l, k * 512 + i * 256:k * 512 + (i + 1) * 256, 3584:3592].rearrange("(k p) n -> p k n", p=P))
                            for i in range(2)])
                tall(0, l, A_OUT, 4, W["w_out"])
                for off, name in ((A_K, "cross_wk"), (A_V, "cross_wv"), (A_Q, "cross_wq")):
                    for i in range(2):
                        chunk(0, l, off + 2 * i, W[name], 512 * i, 512 * i + 256)
                tall(0, l, A_O, 4, W["cross_wo"])
                ffn(0, l, A_FFN2, 1)
            with sp.Fori(0, DEPTH) as l:
                ffn(1, l, B_FFN1, 0)
                for n, (c0, c1) in enumerate([(768, 1024), (0, 256), (512, 2304), (1280, 1536), (1792, 2048)]
                                             + [(2560 + 512 * i, 2816 + 512 * i) for i in range(6)]):
                    chunk(1, l, B_IN + 2 * n, W["w_in_2"], c0, c1)
                tall(1, l, B_BR, 1, W["w_branch_sb_2"])
                tall(1, l, B_BR + 1, 2, W["w_branch_ret_2"])
                tall(1, l, B_BR + 3, 1, W["w_branch_pool_2"])
                tall(1, l, B_OUT, 4, W["w_out_2"])
                ffn(1, l, B_FFN2, 1)
            o = out[0].rearrange("(t p) d -> p t d", p=P)
            for i in range(PIECES):
                sp.wait_ge(x_ready, PIECES * add_no(1, DEPTH, 0) + i + 1)
                sp.dma_start(piece(o, i), piece(xres, i)).then_inc(stored, 16)
            sp.wait_ge(stored, 16 * PIECES)

        @block.gpsimd
        def _(pool):
            pool.sem_inc(lo_ready, CREDIT)

            def split_lo(n, s):
                pool.wait_ge(hi_ready, n + 1)
                pool.tensor_tensor(wlo[:, s], raw[:, s], whi[:, s].bitcast(F32), ALU.subtract).then_inc(lo_ready, 1)

            def forget_unit(n, s):
                pool.wait_ge(hi_ready, n + 1)
                pool.tensor_tensor(wlo[:, s, :, 0:8], raw[:, s, :, 0:8], whi[:, s, :, 0:8].bitcast(F32),
                                   ALU.subtract).then_inc(lo_ready, 1)

            FORGET = A_IN + 6
            with pool.Fori(0, DEPTH) as l:
                with pool.Fori(0, FORGET // RING) as c:
                    for s in range(RING):
                        split_lo(unit(0, l, s, c), s)
                for u in range(FORGET, FORGET + 3):
                    (forget_unit if u < FORGET + 2 else split_lo)(unit(0, l, u), u % RING)
                with pool.Fori(0, (A_UNITS - FORGET) // RING - 1) as c:
                    for s in range(RING):
                        split_lo(unit(0, l, FORGET + 3 + s, c), s)
            with pool.Fori(0, DEPTH) as l:
                with pool.Fori(0, B_UNITS // RING) as c:
                    for s in range(RING):
                        split_lo(unit(1, l, s, c), s)

        @block.scalar
        def _(act):
            act.dma_start(ident[:, :], eye).then_inc(ident_loaded, 16)
            act.dma_start(gain[:, :], gains[0:1, :].broadcast_to([P, DM])).then_inc(gain_loaded, 16)
            act.dma_start(lbt[:, :, :], lb).then_inc(lb_loaded, 16)
            for dst, src in ((cst[:, :], table_a), (memx[:, :, :], mem[0].rearrange("(t p) d -> p t d", p=P)),
                             (onorm[:, :, :], out_norm.unsqueeze(0).broadcast_to([P, DEPTH, H_D])),
                             (fbias[:, :], f_bias), (wpool[:, :, :, :], w_pool), (pscale[:, :, :], pool_scale)):
                act.dma_start(dst, src).then_inc(loaded, 16)

            act.wait_ge(lb_abs, 1)
            act.activation(lbw[:, 1, :], lbw[:, 1, :], ACT.Exp, scale=-1.0).then_inc(lb_sp, 1)
            act.wait_ge(lb_sp, 1)
            act.activation(lbw[:, 1, :], lbw[:, 1, :], ACT.Ln, bias=1.0).then_inc(lb_sp, 1)

            def split_hi(b, l, off, c=0, cols=512):
                s = off % RING
                act.wait_ge(raw_loaded[s], 32 * use(b, l, off, c))
                act.wait_ge(unit_done, unit(b, l, off, c) + 1)
                act.activation(whi[:, s, :, 0:cols], raw[:, s, :, 0:cols], ACT.Copy).then_inc(hi_ready, 1)

            def squares(src, n, add=None):
                st = stat[:, 1 if add is None else 0]
                for t in range(TB):
                    if add is not None:
                        act.wait_ge(x_ready, PIECES * add + 2 + t + 1)
                    act.activation(sq_junk[:, t * DM:(t + 1) * DM], src[:, t, :], ACT.Square, accum_out=st[:, 0, t:t + 1]).then_inc(sq_sum, 1)
                act.wait_ge(sq_sum, 2 * n + 2)
                act.activation(st[:, 1, :], st[:, 0, :], ACT.Sqrt, scale=1.0 / DM, bias=EPS).then_inc(sq_done, 1)

            def next_gain(b, n, T):
                act.wait_ge(xn_ready, PIECES * (xn_no(b, T) + 1))
                act.dma_start(gain[:, :], gains[bass.ds(n + 1, 1), :].broadcast_to([P, DM])).then_inc(gain_loaded, 16)

            def turn_out(T, pieces, banks=(TR, TR + 1)):
                for i in pieces:
                    h, t = divmod(i, 2)
                    act.wait_ge(turned, PIECES * T + i + 1)
                    act.activation(hT_hi[:, t, 4 * h:4 * h + 4, :].rearrange("p k c -> p (k c)"), ps[:, banks[t], :],
                                   ACT.Copy).then_inc(turn_hi, 1)

            def row_out(r):
                act.wait_ge(row_made, r + 1)
                act.activation(rms_row, ps[:, TR, 0:SEQ], ACT.Copy).then_inc(row_ready, 1)

            def ffn(b, l, off, e, T, n, add):
                f = ffn_no(b, l, e)

                def silu(u, cc, step, banks=(G, G + 1)):
                    for t in range(TB):
                        if t == 0:
                            wait_unit(act, b, l, u, cc)
                        act.activation(silu_g[:, t, :], ps[:, banks[t], 0:256], ACT.Silu,
                                       scale=stat[:, 0, 2, t:t + 1]).then_inc(silu_done, 1)

                def evac(step):
                    act.wait_ge(act_turned, FF_STEPS * f + step + 1)
                    act.activation(aT_hi[:, :, :, :].rearrange("p k t c -> p (k t c)"), ps[:, TR, :],
                                   ACT.Copy).then_inc(act_hi, 1)

                turn_out(T, (0, 1))
                split_hi(b, l, off + 2)
                turn_out(T, (2, 3))
                next_gain(b, n, T)
                squares(xres, n, add)
                split_hi(b, l, off + 3)
                act.wait_ge(inv_ready, n + 1)
                silu(off + 1, 0, 0, (ACC, ACC + 2))
                split_hi(b, l, off + 4)
                with act.Fori(0, FF_STEPS - 2) as c:
                    evac(c)
                    split_hi(b, l, off + 5, c)
                    silu(off + 3, c, c + 1)
                    split_hi(b, l, off + 6, c)
                    split_hi(b, l, off + 7, c)
                evac(FF_STEPS - 2)
                split_hi(b, l, off + FFN_UNITS - 1)
                silu(off + FFN_UNITS - 3, 0, FF_STEPS - 1)
                evac(FF_STEPS - 1)

            def chunk_out_(b, l, u, pair, dst, func):
                wait_unit(act, b, l, u + 1)
                act.activation(dst, ps[:, pair:pair + 2, :].rearrange("p a c -> p (a c)"), func).then_inc(chunk_out, 1)

            def normed_out(b, l, u, pair, dst, func):
                wait_unit(act, b, l, u + 1)
                for t in range(TB):
                    last = act.activation(dst[:, t * 512:(t + 1) * 512], ps[:, pair + t, :], func, scale=stat[:, 0, 2, t:t + 1])
                last.then_inc(chunk_out, 1)

            with act.Fori(0, DEPTH) as l:
                step, count = stepper(act, sstep, l * S_A)
                split_hi(0, l, A_FFN1)
                split_hi(0, l, A_FFN1 + 1)
                ffn(0, l, A_FFN1, 0, turn_no(0, l, 0), norm_no(0, l, 0), add_no(0, l, -1))
                U = A_IN
                split_hi(0, l, U)
                split_hi(0, l, U + 1)
                turn_out(turn_no(0, l, 1), (0, 1))
                split_hi(0, l, U + 2)
                turn_out(turn_no(0, l, 1), (2, 3))
                next_gain(0, norm_no(0, l, 1), turn_no(0, l, 1))
                split_hi(0, l, U + 3)
                squares(xres, norm_no(0, l, 1), add_no(0, l, 0))
                plan = ((hg, ACT.Silu), "hf", "hq", "ff", "fq", "fk", (fv, ACT.Copy), (hv, ACT.Copy))
                for i, what in enumerate(plan):
                    for u in (2 * i + 3, 2 * i + 4):
                        if 3 < u < 19:
                            split_hi(0, l, U + u, cols=8 if u in (6, 7) else 512)
                    if i == 0:
                        act.wait_ge(inv_ready, norm_no(0, l, 1) + 1)
                    if isinstance(what, tuple):
                        normed_out(0, l, U + 2 * i, PAIRS[(i if i < 3 else i - 1) % 3], *what)
                    if what == "hf":
                        row_out(row_no(0, l, 0))
                        act.wait_ge(loaded, N_LOADS * 16)
                        squares(memx, norm_no(0, l, 2))
                    if what == "ff":
                        wait_unit(act, 0, l, U + 7)
                        for t in range(TB):
                            last = act.activation(flog[:, t, :], ps[:, TR, 8 * t:8 * t + 8], ACT.Copy, scale=stat[:, 0, 2, t:t + 1])
                        last.then_inc(f_tm, 1)
                        act.wait_ge(f_turn, l + 1)
                        act.activation(fcs_f, ps[0:8, TR + 1, 0:256], ACT.Identity, bias=fbias[:, bass.ds(l, 1)]).then_inc(f_logit, 1)
                        wait_taken(act, 0, l, 2)
                        act.activation(hq, hq, ACT.Silu)
                        act.wait_ge(h_abs, l + 1)
                        step(act.activation(tmp1, tmp1, ACT.Exp, scale=-1.0))
                        act.activation(tmp1, tmp1, ACT.Ln, bias=1.0).then_inc(h_sp, 1)
                    if what == "fq":
                        act.wait_ge(f_abs, l + 1)
                        step(act.activation(fcs_t, fcs_t, ACT.Exp, scale=-1.0))
                        act.activation(fcs_t, fcs_t, ACT.Ln, bias=1.0).then_inc(f_sp, 1)
                        act.wait_ge(h_gate, l + 1)
                        step(act.activation(lev2[:, 0:1024], lev2[:, 0:1024], ACT.Exp, scale=-1.0))
                        act.activation(lev2[:, 0:1024], lev2[:, 0:1024], ACT.Ln, bias=1.0).then_inc(h_sp2, 1)
                    if what == "fk":
                        for h in range(H_HEADS):
                            act.activation(hk[:, h * SEQ:(h + 1) * SEQ], hk[:, h * SEQ:(h + 1) * SEQ], ACT.Exp, scale=-1.0,
                                           bias=lb_l[:, 1, h:h + 1]).then_inc(h_key, 1)
                NL = len(LEVELS) + 1
                for n in range(NL):
                    e = lev2[:, (n % 2) * 1024:(n % 2) * 1024 + 1024]
                    act.wait_ge(lev_diff, l * NL + n + 1)
                    act.activation(e, e, ACT.Exp).then_inc(lev_exp, 1)
                act.wait_ge(h_out, l + 1)
                o2 = ps[:, ACC + 2:ACC + 4, :].rearrange("p a c -> p (a c)")
                act.activation(tmp1, o2, ACT.Square).then_inc(h_sq, 1)
                act.activation(tmp2, o2, ACT.Copy)
                act.wait_ge(h_sum, l + 1)
                act.activation(hst[:, 1, :], hst[:, 0, :], ACT.Sqrt, scale=1.0 / H_D, bias=EPS).then_inc(h_rms, 1)
                act.wait_ge(f_cumT, l + 1)
                act.activation(sst[:, 3, :], ps[:, TR, 0:16], ACT.Copy).then_inc(f_cumS, 1)
                NA = X_HEADS * TB

                def fox_exp(i):
                    w = P * (i % 2 + 1)
                    act.wait_ge(a_max, l * NA + i + 1)
                    if i >= 4:
                        act.wait_ge(a_turn, l * NA + i - 3)
                    act.activation(fp[:, (i % 4) * 256:(i % 4) * 256 + w], fsc[:, (i % 4) * 256:(i % 4) * 256 + w], ACT.Exp,
                                   bias=sst[:, 1, i:i + 1], accum_out=sst[:, 2, i:i + 1]).then_inc(a_prob, 1)

                def fox_pT(i):
                    w = P * (i % 2 + 1)
                    act.wait_ge(a_turn, l * NA + i + 1)
                    if i >= 2:
                        act.wait_ge(a_out, l * NA + i - 1)
                    act.activation(fpT[:, (i % 2) * 256:(i % 2) * 256 + w], ps[:, G + i % 2, 0:w], ACT.Copy).then_inc(a_pT, 1)

                for i in range(NA + 1):
                    if i < NA:
                        fox_exp(i)
                    if i:
                        fox_pT(i - 1)
                    if i == 1:
                        turn_out(turn_no(0, l, 2), (0, 1), (ACC, ACC + 2))
                turn_out(turn_no(0, l, 2), (2, 3))
                T3, T4 = turn_no(0, l, 3), turn_no(0, l, 4)
                split_hi(0, l, A_OUT + 3)
                split_hi(0, l, A_K)
                turn_out(T3, (0, 1))
                next_gain(0, norm_no(0, l, 2), T3)
                split_hi(0, l, A_K + 1)
                turn_out(T3, (2, 3))
                split_hi(0, l, A_K + 2)
                for i, dst in enumerate((zf, hq, hk, hv)):
                    split_hi(0, l, A_K + 2 * i + 3)
                    if i == 3:
                        turn_out(T4, (0, 1))
                    split_hi(0, l, A_K + 2 * i + 4)
                    chunk_out_(0, l, A_K + 2 * i, PAIRS[i % 3], dst, ACT.Copy)
                    if i == 0:
                        squares(xres, norm_no(0, l, 3), add_no(0, l, 1))
                turn_out(T4, (2, 3))
                next_gain(0, norm_no(0, l, 3), T4)
                split_hi(0, l, A_K + 11)
                split_hi(0, l, A_K + 12)
                row_out(row_no(0, l, 1))
                split_hi(0, l, A_K + 13)
                split_hi(0, l, A_K + 14)
                NC = C_HEADS * TB

                def cross_exp(i):
                    act.wait_ge(c_max, l * NC + i + 1)
                    if i >= 4:
                        act.wait_ge(c_turn, l * NC + i - 3)
                    act.activation(fp[:, (i % 4) * 256:(i % 4) * 256 + 256], ps[:, TR + i % 2, 0:256], ACT.Exp,
                                   bias=sst[:, 1, i:i + 1], accum_out=sst[:, 2, i:i + 1]).then_inc(c_prob, 1)

                def cross_pT(i):
                    act.wait_ge(c_turn, l * NC + i + 1)
                    if i >= 2:
                        act.wait_ge(c_out, l * NC + i - 1)
                    act.activation(fpT[:, (i % 2) * 256:(i % 2) * 256 + 256], ps[:, G + i % 2, 0:256], ACT.Copy).then_inc(c_pT, 1)

                for i in range(NC + 1):
                    if i < NC:
                        cross_exp(i)
                    if i == NC:
                        turn_out(turn_no(0, l, 5), (0, 1), (ACC, ACC + 2))
                    if i:
                        cross_pT(i - 1)
                turn_out(turn_no(0, l, 5), (2, 3))
                split_hi(0, l, A_O + 3)
                split_hi(0, l, A_FFN2)
                split_hi(0, l, A_FFN2 + 1)
                ffn(0, l, A_FFN2, 1, turn_no(0, l, 6), norm_no(0, l, 4), add_no(0, l, 2))
                assert count[0] == S_A, ("S_A", count[0])
            squares(xres, norm_no(0, DEPTH, 0), add_no(0, DEPTH, -1))
            next_gain(0, norm_no(0, DEPTH, 0), turn_no(0, DEPTH, 0))
            act.dma_start(cst[:, :], table_b).then_inc(loaded, 16)
            with act.Fori(0, DEPTH) as l:
                step, count = stepper(act, sstep, DEPTH * S_A + l * S_B)
                split_hi(1, l, B_FFN1)
                split_hi(1, l, B_FFN1 + 1)
                ffn(1, l, B_FFN1, 0, turn_no(1, l, 0), norm_no(1, l, 0), add_no(1, l, -1))
                U = B_IN
                split_hi(1, l, U)
                split_hi(1, l, U + 1)
                turn_out(turn_no(1, l, 1), (0, 1))
                split_hi(1, l, U + 2)
                turn_out(turn_no(1, l, 1), (2, 3))
                next_gain(1, norm_no(1, l, 1), turn_no(1, l, 1))
                split_hi(1, l, U + 3)
                squares(xres, norm_no(1, l, 1), add_no(1, l, 0))
                plan = [(qk_r, ACT.Copy), None, (vu, ACT.Copy), (v_r, ACT.Copy), (g_r, ACT.Silu)] + [
                    (gates[:, 1024 * i:1024 * i + 1024], ACT.Sigmoid) for i in range(6)]
                for i, what in enumerate(plan):
                    for u in (2 * i + 3, 2 * i + 4):
                        if 3 < u < 25:
                            split_hi(1, l, U + u)
                    if i == 0:
                        act.wait_ge(inv_ready, norm_no(1, l, 1) + 1)
                    if what:
                        normed_out(1, l, U + 2 * i, PAIRS[i % 3], *what)
                    else:
                        row_out(row_no(1, l, 0))
                for t in range(TB):
                    act.wait_ge(r_turn, l * TB + t + 1)
                    act.activation(qk_rT.rearrange("p (k t c) -> p k t c", k=4, t=TB)[:, :, t, :],
                                   ps[:, TR + t, :].rearrange("p (k c) -> p k c", k=4), ACT.Copy).then_inc(r_kT, 1)
                act.wait_ge(s_score, 2 * l + 2)
                step(act.activation(st1, ps[:, 3:6, :].rearrange("p a c -> p (a c)"), ACT.Abs))
                step(act.activation(st1, st1, ACT.Exp, scale=-1.0))
                act.activation(st1, st1, ACT.Ln, bias=1.0).then_inc(s_sp, 1)
                act.wait_ge(s_sum, l + 1)
                act.activation(st2, st2, ACT.Exp).then_inc(s_exp, 1)
                act.wait_ge(p_diff, l + 1)
                act.activation(pool_d[0:64, :], ps[0:64, G:G + 2, :].rearrange("p a c -> p (a c)"), ACT.Copy).then_inc(p_dT, 1)
                act.wait_ge(r_out, l + 1)
                o2 = ps[:, TR:TR + 2, :].rearrange("p a c -> p (a c)")
                act.activation(qk_sb, o2, ACT.Square).then_inc(r_sq, 1)
                act.activation(v_r, o2, ACT.Copy)
                act.wait_ge(r_sum, l + 1)
                act.activation(hst[:, 1, :], hst[:, 0, :], ACT.Sqrt, scale=1.0 / P, bias=EPS).then_inc(r_rms, 1)
                act.wait_ge(s_out, l + 1)
                act.activation(hT_hi[:, :, 0:2, :].rearrange("p t k c -> p k t c"),
                               ps[:, 3, :].rearrange("p (k t c) -> p k t c", k=2, t=TB), ACT.Copy).then_inc(s_hi, 1)
                act.wait_ge(p_out, l + 1)
                for k in range(2):
                    act.activation(hT_hi[:, :, 6 + k, :], ps[:, 4, k * 256:(k + 1) * 256].rearrange("p (t c) -> p t c", t=TB),
                                   ACT.Copy, scale=pscale_l[:, k:k + 1]).then_inc(p_hi, 1)
                for t in range(TB):
                    act.wait_ge(r_yT, l * TB + t + 1)
                    act.activation(hT_hi[:, t, 2:6, :].rearrange("p k c -> p (k c)"), ps[:, TR + t, :], ACT.Copy).then_inc(r_hi, 1)
                split_hi(1, l, B_BR + 3)
                split_hi(1, l, B_OUT)
                split_hi(1, l, B_OUT + 1)
                split_hi(1, l, B_OUT + 2)
                turn_out(turn_no(1, l, 2), range(PIECES))
                split_hi(1, l, B_OUT + 3)
                split_hi(1, l, B_FFN2)
                split_hi(1, l, B_FFN2 + 1)
                ffn(1, l, B_FFN2, 1, turn_no(1, l, 3), norm_no(1, l, 2), add_no(1, l, 1))
                assert count[0] == S_B, ("S_B", count[0])
            squares(xres, norm_no(1, DEPTH, 0), add_no(1, DEPTH, -1))

        @block.tensor
        def _(pe):
            pe.sem_inc(unit_done, CREDIT)
            pe.wait_ge(ident_loaded, 16)

            def split_product(out, l_hi, l_lo, r_hi, r_lo, first, last):
                pe.matmul(out, l_hi, r_hi, start=first, stop=False, skip_group_check=True)
                pe.matmul(out, l_hi, r_lo, start=False, stop=False, skip_group_check=True)
                return pe.matmul(out, l_lo, r_hi, start=False, stop=last, skip_group_check=True)

            def wait_weights(b, l, off, c=0):
                pe.wait_ge(lo_ready, unit(b, l, off, c) + 1 + CREDIT)

            def turn_piece(b, T, i, banks=(TR, TR + 1)):
                h, t = divmod(i, 2)
                pe.wait_ge(xn_ready, PIECES * xn_no(b, T) + i + 1)
                if h:
                    pe.wait_ge(turn_lo, PIECES * T + i - 1)
                for k in range(4):
                    mm = pe.transpose(ps[:, banks[t], k * P:(k + 1) * P], piece(xn, i)[:, k * P:(k + 1) * P], ident[:, :])
                mm.then_inc(turned, 1)

            def wait_piece(T, k0, t):
                pe.wait_ge(turn_lo, PIECES * T + k0 // 2 + t + 1)

            def tokens_unit(b, l, off, c, k0, banks, first, last, ready=None, T=None, then=()):
                s = off % RING
                wait_weights(b, l, off, c)
                for t in range(TB):
                    if ready is not None:
                        pe.wait_ge(prod_ready, ready + t + 1)
                    if T is not None:
                        wait_piece(T, k0, t)
                    for k in range(4):
                        mm = split_product(ps[:, banks[t], :], hT_hi[:, t, k0 + k, :], hT_lo[:, t, k0 + k, :],
                                           whi[:, s, k, :], wlo[:, s, k, :], first and k == 0, last and k == 3)
                    if t == TB - 1:
                        mm.then_inc(unit_done, 1)
                    if then:
                        turn_piece(b, T, then[t])

            def features_unit(b, l, off, k0, bank, first, last, T=None):
                s = off % RING
                wait_weights(b, l, off)
                if T is not None:
                    wait_piece(T, k0, TB - 1)
                for n in range(4):
                    cols = slice(n * P, (n + 1) * P)
                    for k in range(4):
                        mm = split_product(ps[:, bank + n // 2, n % 2 * SEQ:(n % 2 + 1) * SEQ],
                                           whi[:, s, k, cols], wlo[:, s, k, cols], hT_hi[:, :, k0 + k, :], hT_lo[:, :, k0 + k, :],
                                           first and k == 0 and n % 2 == 0, last and k == 3)
                mm.then_inc(unit_done, 1)

            def tall_unit(b, l, off, lhs, bank, first, last, c=0, T=None, k0=0, signal=False, then={}):
                s = off % RING
                wait_weights(b, l, off, c)
                for i in range(PIECES):
                    half, t = divmod(i, 2)
                    if T is not None and half == 0:
                        wait_piece(T, k0, t)
                    for k in range(2):
                        hi, lo = lhs(k)
                        mm = split_product(ps[:, bank + 2 * t + half, :], hi[:, t], lo[:, t],
                                           whi[:, s, 2 * k + half, :], wlo[:, s, 2 * k + half, :], first and k == 0, last and k == 1)
                    if i == PIECES - 1:
                        mm.then_inc(unit_done, 1)
                    elif signal:
                        mm.then_inc(acc_done, 1)
                    if i in then:
                        then[i]()

            def from_hT(k0):
                return lambda k: (hT_hi[:, :, k0 + k, :], hT_lo[:, :, k0 + k, :])

            def turn_ahead(b, T):
                return {} if T is None else {2: lambda: turn_piece(b, T, 0), 3: lambda: turn_piece(b, T, 1)}

            def output(b, l, off, T, T_next=None, T_mid=None):
                tall_unit(b, l, off, from_hT(0), ACC, True, False, 0, T, 0,
                          then={1: lambda: (turn_piece(b, T, 2), turn_piece(b, T, 3))})
                tall_unit(b, l, off + 1, from_hT(2), ACC, False, False)
                wait_piece(T, 4, 1)
                if T_mid is not None:
                    turn_piece(b, T_mid, 0)
                    turn_piece(b, T_mid, 1)
                tall_unit(b, l, off + 2, from_hT(4), ACC, False, False)
                tall_unit(b, l, off + 3, from_hT(6), ACC, False, True, signal=True, then=turn_ahead(b, T_next))
                if T_mid is not None:
                    turn_piece(b, T_mid, 2)
                    turn_piece(b, T_mid, 3)

            def row(r, ones):
                pe.wait_ge(row_diag, r + 1)
                pe.matmul(ps[:, TR, 0:SEQ], ones, norm_diag, start=True, stop=True).then_inc(row_made, 1)

            def ffn(b, l, off, e, T, T_next=None):
                f = ffn_no(b, l, e)

                def half_up(off, c, step, k):
                    if isinstance(step, int) and step == 0:
                        tokens_unit(b, l, off + k, c, 4 * k, (ACC, ACC + 2), k == 0, k == 1, None, T, (2, 3) if k == 0 else ())
                        return
                    ready = 2 * FF_STEPS * f + 2 * (step - 1) if k == 0 and not (isinstance(step, int) and step == 1) else None
                    tokens_unit(b, l, off + k, c, 4 * k, (G, G + 1), k == 0, k == 1, ready)

                def turn_act(step):
                    pe.wait_ge(prod_ready, 2 * FF_STEPS * f + 2 * step + 2)
                    for k in range(2):
                        for t in range(TB):
                            mm = pe.transpose(ps[:, TR, (2 * k + t) * P:(2 * k + t + 1) * P], prod[:, t, k * P:(k + 1) * P], ident[:, :])
                    mm.then_inc(act_turned, 1)

                def down(off, c, step, first, last):
                    pe.wait_ge(act_lo, FF_STEPS * f + step + 1)
                    tall_unit(b, l, off, lambda k: (aT_hi[:, k], aT_lo[:, k]), ACC, first, last, c, signal=last,
                              then=turn_ahead(b, T_next) if last else {})

                def step_(off, c, step, first):
                    half_up(off, c, step, 0)
                    turn_act(step - 1)
                    half_up(off, c, step, 1)
                    down(off + 2, c, step - 1, first, False)

                half_up(off, 0, 0, 0)
                half_up(off, 0, 0, 1)
                step_(off + 2, 0, 1, True)
                with pe.Fori(0, FF_STEPS - 2) as c:
                    step_(off + 5, c, c + 2, False)
                turn_act(FF_STEPS - 1)
                down(off + FFN_UNITS - 1, 0, FF_STEPS - 1, False, True)

            def chunk(b, l, off, pair, features, before=None, T=None, then=(), between=None):
                if before is not None:
                    wait_taken(pe, b, l, before)
                for k in range(2):
                    if features:
                        features_unit(b, l, off + k, 4 * k, pair, k == 0, k == 1, T)
                    else:
                        tokens_unit(b, l, off + k, 0, 4 * k, (pair, pair + 1), k == 0, k == 1, None, T, then if k == 0 else ())
                    if k == 0 and between:
                        between()

            with pe.Fori(0, DEPTH) as l:
                T0, T1, T2, T3, T4, T5, T6 = (turn_no(0, l, j) for j in range(7))
                turn_piece(0, T0, 0)
                turn_piece(0, T0, 1)
                ffn(0, l, A_FFN1, 0, T0, T1)
                for i, features in enumerate((False, True, True, None, True, True, False, False)):
                    off, j = A_IN + 2 * i, i if i < 3 else i - 1
                    if features is not None:
                        chunk(0, l, off, PAIRS[j % 3], features, j - 3 if j >= 3 else None, T1 if i == 0 else None, (2, 3) if i == 0 else ())
                        if i == 0:
                            pe.wait_ge(loaded, N_LOADS * 16)
                            row(row_no(0, l, 0), con("ones", 0, P))
                        continue
                    pe.wait_ge(row_ready, row_no(0, l, 0) + 1)
                    for k in range(2):
                        s = (off + k) % RING
                        wait_weights(0, l, off + k)
                        for t in range(TB):
                            for kk in range(4):
                                mm = split_product(ps[:, TR, 8 * t:8 * t + 8], hT_hi[:, t, 4 * k + kk, :], hT_lo[:, t, 4 * k + kk, :],
                                                   whi[:, s, kk, 0:8], wlo[:, s, kk, 0:8], k == 0 and kk == 0 and t == 0, k == 1 and kk == 3)
                        mm.then_inc(unit_done, 1)
                    pe.wait_ge(f_tm, l + 1)
                    for t in range(TB):
                        mm = pe.transpose(ps[0:8, TR + 1, t * P:(t + 1) * P], flog[:, t, :], ident[:, :])
                    mm.then_inc(f_turn, 1)
                wait_taken(pe, 0, l, 4)
                wait_taken(pe, 0, l, 6)
                NG = len(LEVELS) + 2
                for n in range(NG):
                    bank = ACC + 2 * (n % 2)
                    if n >= 2:
                        pe.wait_ge(lev_kept, l * NG + n - 1)
                    if n == 0:
                        pe.wait_ge(h_key, H_HEADS * (l + 1))
                        a, c = hk, hq
                    else:
                        pe.wait_ge(lev_ready, l * (NG - 1) + n)
                        a = c = lev2[:, (n - 1) % 2 * 1024:(n - 1) % 2 * 1024 + 1024]
                    if n < NG - 1:
                        for g in range(H_HEADS * TB):
                            mm = pe.matmul(ps[:, bank + g // 4, g % 4 * P:(g % 4 + 1) * P], a[:, g * P:(g + 1) * P],
                                           c[:, g * P:(g + 1) * P], start=True, stop=True)
                    else:
                        for h in range(H_HEADS):
                            mm = pe.matmul(ps[:, bank, h * P:(h + 1) * P], a[:, 2 * h * P:(2 * h + 1) * P],
                                           c[:, (2 * h + 1) * P:(2 * h + 2) * P], start=True, stop=True)
                    mm.then_inc(lev_prod, 1)
                pe.wait_ge(lev_kept, l * NG + NG)
                for h in range(H_HEADS):
                    v = [hv[:, t * 512 + h * P:t * 512 + (h + 1) * P] for t in range(TB)]
                    o = [ps[:, ACC + 2 + t, h * P:(h + 1) * P] for t in range(TB)]
                    pe.matmul(o[0], att[:, 2 * h * P:(2 * h + 1) * P], v[0], start=True, stop=True)
                    pe.matmul(o[1], attx[:, h * P:(h + 1) * P], v[0], start=True, stop=False)
                    mm = pe.matmul(o[1], att[:, (2 * h + 1) * P:(2 * h + 2) * P], v[1], start=False, stop=True)
                mm.then_inc(h_out, 1)
                pe.wait_ge(f_cum, l + 1)
                for t in range(TB):
                    mm = pe.matmul(ps[:, TR, 8 * t:8 * t + 8], fcs_c[:, t * P:(t + 1) * P], ident[0:8, 0:8], start=True, stop=True)
                mm.then_inc(f_cumT, 1)
                pe.wait_ge(f_cumS, l + 1)
                NA = X_HEADS * TB

                def fox_score(i):
                    h, t = divmod(i, 2)
                    w, r, j = P * (t + 1), h % 2 * 64, h // 2
                    if i >= 2:
                        pe.wait_ge(a_masked, l * NA + i - 1)
                    o = ps[:, TR + i % 2, 0:w]
                    pe.matmul(o, fq[r:r + 64, j * SEQ + t * P:j * SEQ + (t + 1) * P], fk[r:r + 64, j * SEQ:j * SEQ + w], start=True, stop=False)
                    pe.matmul(o, con("sel", h * P, P, 8), fcs_n[:, 0:w], start=False, stop=True).then_inc(a_score, 1)

                def fox_turn(i):
                    pe.wait_ge(a_prob, l * NA + i + 1)
                    if i >= 2:
                        pe.wait_ge(a_pT, l * NA + i - 1)
                    for k in range(i % 2 + 1):
                        mm = pe.transpose(ps[:, G + i % 2, k * P:(k + 1) * P], fp[:, i % 4 * 256 + k * P:i % 4 * 256 + (k + 1) * P], ident[:, :])
                    mm.then_inc(a_turn, 1)

                def fox_out(i):
                    h, t = divmod(i, 2)
                    pe.wait_ge(a_pT, l * NA + i + 1)
                    for k in range(t + 1):
                        mm = pe.matmul(ps[:, ACC + 2 * t + 1, h * 64:(h + 1) * 64], fpT[:, i % 2 * 256 + k * P:i % 2 * 256 + (k + 1) * P],
                                       fv[:, k * 512 + h * 64:k * 512 + (h + 1) * 64], start=(k == 0), stop=(k == t))
                    mm.then_inc(a_out, 1)

                for i in range(NA + 3):
                    if i == 2:
                        for k in range(2):
                            turn_piece(0, T2, k, (ACC, ACC + 2))
                    if i < NA:
                        fox_score(i)
                    if 2 <= i < NA + 2:
                        fox_turn(i - 2)
                    if i >= 3:
                        fox_out(i - 3)
                output(0, l, A_OUT, T2, T_mid=T3)
                for i in range(6):
                    if i < 4:
                        chunk(0, l, A_K + 2 * i, PAIRS[i % 3], i < 2, 7 + i - 3 if i >= 3 else None, T3 if i == 0 else None,
                              between=(lambda: (turn_piece(0, T4, 0), turn_piece(0, T4, 1))) if i == 3 else None)
                        continue
                    if i == 4:
                        turn_piece(0, T4, 2)
                        turn_piece(0, T4, 3)
                    chunk(0, l, A_K + 2 * i, PAIRS[i % 3], True, 7 + i - 3, T4 if i == 4 else None)
                    if i == 4:
                        row(row_no(0, l, 1), con("ones", 0, P))
                wait_taken(pe, 0, l, 10)
                wait_taken(pe, 0, l, 12)
                NC = C_HEADS * TB

                def cross_score(i):
                    h, t = divmod(i, 2)
                    if i >= 2:
                        pe.wait_ge(c_prob, l * NC + i - 1)
                    q, k_ = (hg, fq)[h // 2], (zf, hq)[h // 2]
                    for k in range(2):
                        at = (2 * (h % 2) + k) * SEQ
                        mm = pe.matmul(ps[:, TR + i % 2, 0:SEQ], q[:, at + t * P:at + (t + 1) * P], k_[:, at:at + SEQ], start=(k == 0), stop=(k == 1))
                    mm.then_inc(c_score, 1)

                def cross_turn(i):
                    pe.wait_ge(c_prob, l * NC + i + 1)
                    if i >= 2:
                        pe.wait_ge(c_pT, l * NC + i - 1)
                    for k in range(2):
                        mm = pe.transpose(ps[:, G + i % 2, k * P:(k + 1) * P], fp[:, i % 4 * 256 + k * P:i % 4 * 256 + (k + 1) * P], ident[:, :])
                    mm.then_inc(c_turn, 1)

                def cross_out(i):
                    h, t = divmod(i, 2)
                    v = (hk, hv)[h // 2]
                    pe.wait_ge(c_pT, l * NC + i + 1)
                    for k in range(2):
                        at = k * 512 + h % 2 * C_D
                        mm = pe.matmul(ps[:, ACC + 2 * t + h // 2, h % 2 * C_D:(h % 2 + 1) * C_D],
                                       fpT[:, i % 2 * 256 + k * P:i % 2 * 256 + (k + 1) * P], v[:, at:at + C_D], start=(k == 0), stop=(k == 1))
                    mm.then_inc(c_out, 1)

                for i in range(NC + 3):
                    if i == NC:
                        for k in range(2):
                            turn_piece(0, T5, k, (ACC, ACC + 2))
                    if i < NC:
                        cross_score(i)
                    if 2 <= i < NC + 2:
                        cross_turn(i - 2)
                    if i >= 3:
                        cross_out(i - 3)
                output(0, l, A_O, T5, T_next=T6)
                ffn(0, l, A_FFN2, 1, T6)

            pe.wait_ge(loaded, N_LOADS * 16 + 16)
            with pe.Fori(0, DEPTH) as l:
                T0, T1, T2, T3 = (turn_no(1, l, j) for j in range(4))
                turn_piece(1, T0, 0)
                turn_piece(1, T0, 1)
                ffn(1, l, B_FFN1, 0, T0, T1)
                for i in range(11):
                    chunk(1, l, B_IN + 2 * i, PAIRS[i % 3], i == 1, i - 3 if i >= 3 else None, T1 if i == 0 else None, (2, 3) if i == 0 else ())
                    if i == 0:
                        row(row_no(1, l, 0), con("neg_ones"))
                wait_taken(pe, 1, l, 10)
                for t in range(TB):
                    pe.wait_ge(r_rot, l * TB + t + 1)
                    for k in range(4):
                        mm = pe.transpose(ps[:, TR + t, k * P:(k + 1) * P], qk_rot[:, t * 512 + k * P:t * 512 + (k + 1) * P], ident[:, :])
                    mm.then_inc(r_turn, 1)

                def key_scores(qk, bank, done):
                    for n, h in enumerate(HEAD_ORDER):
                        r, j = h % 2 * 64, h // 2
                        if n == 2:
                            pe.wait_ge(done, 2 * l + 1)
                        q = qk[r:r + 64, j * SEQ:(j + 1) * SEQ]
                        k = qk[r:r + 64, (2 + j) * SEQ:(3 + j) * SEQ]
                        pe.matmul(ps[:, bank + n // 2, n % 2 * SEQ:(n % 2 + 1) * SEQ], k[:, 0:P], q, start=True, stop=True)
                        mm = pe.matmul(ps[:, bank + 2, n * P:(n + 1) * P], k[:, P:SEQ], q[:, P:SEQ], start=True, stop=True)
                        if n % 2:
                            mm.then_inc(done, 1)

                key_scores(qk_sb, 3, s_score)
                pe.wait_ge(r_kT, TB * (l + 1))
                key_scores(qk_rT, 0, r_score)
                pe.wait_ge(s_fail, l + 1)
                for g in range(4):
                    u = [vu[:, t * 512 + 256 + g * 64:t * 512 + 256 + (g + 1) * 64] for t in range(TB)]
                    o = ps[0:64, G + g // 2, g % 2 * SEQ:(g % 2 + 1) * SEQ]
                    m = [con("pool", (3 * g + n) * P, P) for n in range(3)]
                    pe.matmul(o[:, 0:P], u[0], m[0], start=True, stop=True)
                    pe.matmul(o[:, P:SEQ], u[0], m[1], start=True, stop=False)
                    mm = pe.matmul(o[:, P:SEQ], u[1], m[2], start=False, stop=True)
                mm.then_inc(p_diff, 1)
                pe.wait_ge(r_dec, l + 1)
                later, all_ = con("neg_later"), con("neg_ones")
                for n in range(2):
                    pe.matmul(ps[:, n, :], later, st3[:, n * 512:(n + 1) * 512], start=True, stop=False, skip_group_check=True)
                    pe.matmul(ps[:, n, :].rearrange("p (h b c) -> p h b c", h=2, b=2)[:, :, 1, :], all_,
                              st3[:, 1024 + n * 256:1024 + (n + 1) * 256], start=False, stop=True, skip_group_check=True)
                pe.matmul(ps[:, 2, :], later, st3[:, 1024:1536], start=True, stop=True).then_inc(s_after, 1)
                for n, h in enumerate(HEAD_ORDER):
                    v = [v_r[:, t * 512 + h * P:t * 512 + (h + 1) * P] for t in range(TB)]
                    o = [ps[:, TR + t, h * P:(h + 1) * P] for t in range(TB)]
                    pe.matmul(o[0], sc_r[:, 2 * n * P:(2 * n + 1) * P], v[0], start=True, stop=True)
                    pe.matmul(o[1], sc_r[:, (2 * n + 1) * P:(2 * n + 2) * P], v[0], start=True, stop=False)
                    mm = pe.matmul(o[1], sc_r[:, 1024 + n * P:1024 + (n + 1) * P], v[1], start=False, stop=True)
                mm.then_inc(r_out, 1)
                pe.wait_ge(p_dT, l + 1)
                pe.wait_ge(p_wl, l + 1)
                pe.wait_ge(s_w, l + 1)
                for n, h in enumerate(HEAD_ORDER):
                    r = h % 2 * 64
                    v = [vu[:, t * 512 + h * 64:t * 512 + (h + 1) * 64] for t in range(TB)]
                    o = ps[r:r + 64, 3, h // 2 * SEQ:(h // 2 + 1) * SEQ]
                    pe.matmul(o[:, 0:P], v[0], st2[:, 2 * n * P:(2 * n + 1) * P], start=True, stop=True)
                    pe.matmul(o[:, P:SEQ], v[0], st2[:, (2 * n + 1) * P:(2 * n + 2) * P], start=True, stop=False)
                    mm = pe.matmul(o[:, P:SEQ], v[1], st2[:, 1024 + n * P:1024 + (n + 1) * P], start=False, stop=True)
                mm.then_inc(s_out, 1)
                for g in range(4):
                    r = g % 2 * 64
                    mm = pe.matmul(ps[r:r + 64, 4, g // 2 * SEQ:(g // 2 + 1) * SEQ], wpool_l[:, g, :], pool_d[0:64, g * SEQ:(g + 1) * SEQ],
                                   start=True, stop=True)
                mm.then_inc(p_out, 1)
                for t in range(TB):
                    pe.wait_ge(r_y, l + 1)
                    for k in range(4):
                        mm = pe.transpose(ps[:, TR + t, k * P:(k + 1) * P], v_r[:, t * 512 + k * P:t * 512 + (k + 1) * P], ident[:, :])
                    mm.then_inc(r_yT, 1)
                pe.wait_ge(s_lo, l + 1)
                pe.wait_ge(p_lo, l + 1)
                tall_unit(1, l, B_BR, from_hT(0), 0, True, True)
                pe.wait_ge(r_lo, TB * (l + 1))
                tall_unit(1, l, B_BR + 1, from_hT(2), 4, True, False)
                tall_unit(1, l, B_BR + 2, from_hT(4), 4, False, True)
                pe.wait_ge(br_used, 2 * l + 1)
                tall_unit(1, l, B_BR + 3, from_hT(6), 0, True, True)
                turn_piece(1, T2, 0)
                turn_piece(1, T2, 1)
                output(1, l, B_OUT, T2, T_next=T3)
                ffn(1, l, B_FFN2, 1, T3)

        @block.vector
        def _(dve):
            dve.wait_ge(lb_loaded, 16)
            step, count = stepper(dve, vstep, 0)

            def absolute(o, z):
                return dve.scalar_tensor_tensor(out=o, in0=z, scalar=-1.0, in1=z, op0=ALU.mult, op1=ALU.max)

            dve.memset(ln_lb[:, 0, :], MASKED)
            dve.memset(ln_1mlb[:, 0, :], 0.0)
            step(dve.tensor_tensor(lbw[:, 0, :], lbt[:, 1, :], lbt[:, 0, :], ALU.subtract))
            absolute(lbw[:, 1, :], lbw[:, 0, :]).then_inc(lb_abs, 1)
            dve.wait_ge(lb_sp, 2)
            dve.scalar_tensor_tensor(out=ln_lb[:, 1, :], in0=lbw[:, 0, :], scalar=0.0, in1=lbw[:, 1, :], op0=ALU.min, op1=ALU.subtract)
            step(dve.scalar_tensor_tensor(out=lbw[:, 2, :], in0=lbw[:, 0, :], scalar=0.0, in1=lbw[:, 1, :], op0=ALU.max, op1=ALU.add))
            step(dve.tensor_scalar(ln_1mlb[:, 1, :], lbw[:, 2, :], -1.0, None, ALU.mult))
            assert count[0] == V_START, ("V_START", count[0])

            def inverse(n, which=0):
                dve.wait_ge(sq_done, n + 1)
                dve.reciprocal(stat[:, which, 2, :], stat[:, which, 1, :]).then_inc(inv_ready, 1)
                dve.wait_ge(inv_ready, n + 1)

            def gained(A, n, i):
                if i == 0:
                    dve.wait_ge(gain_loaded, 16 * n + 16)
                dve.wait_ge(x_ready, PIECES * A + i + 1)
                dve.tensor_tensor(piece(xn, i), piece(xres, i), gain[:, i // 2 * 512:(i // 2 + 1) * 512], ALU.mult).then_inc(xn_ready, 1)

            def turn_out(T, pieces, banks=(TR, TR + 1)):
                for i in pieces:
                    h, t = divmod(i, 2)
                    dve.wait_ge(turn_hi, PIECES * T + i + 1)
                    at = lambda m: m[:, t, 4 * h:4 * h + 4, :].rearrange("p k c -> p (k c)")
                    dve.tensor_tensor(at(hT_lo), ps[:, banks[t], :], at(hT_hi).bitcast(F32), ALU.subtract).then_inc(turn_lo, 1)

            def add(b, l, j, i, off, factor):
                h, t = divmod(i, 2)
                if i < PIECES - 1:
                    dve.wait_ge(acc_done, (PIECES - 1) * acc_no(b, l, j) + i + 1)
                else:
                    wait_unit(dve, b, l, off)
                dve.scalar_tensor_tensor(out=piece(xres, i), in0=ps[:, ACC + 2 * t + h, :], scalar=factor, in1=piece(xres, i),
                                         op0=ALU.mult, op1=ALU.add).then_inc(x_ready, 1)

            def add_and_norm(b, l, j, off, factor, n, T=None):
                for i in range(PIECES):
                    if T is not None and i == PIECES - 1:
                        turn_out(T, (0,))
                    add(b, l, j, i, off, factor)
                    if T is not None and i == PIECES - 1:
                        turn_out(T, (1,))
                    gained(add_no(b, l, j), n, i)

            def rms_diag(sign):
                for t in range(TB):
                    last = dve.tensor_scalar(norm_diag[:, t * P:(t + 1) * P], ident[:, :], stat[:, 0, 2, t:t + 1], sign, ALU.mult, ALU.mult)
                last.then_inc(row_diag, 1)

            def scaled_out(b, l, u, pair, r, parts):
                wait_unit(dve, b, l, u + 1)
                dve.wait_ge(row_ready, r + 1)
                src = ps[:, pair:pair + 2, :].rearrange("p a (f c) -> p (a f) c", c=SEQ)
                at = 0
                for dst, scale in parts:
                    d = dst.rearrange("p (f c) -> p f c", c=SEQ)
                    F = d.shape[1]
                    last = dve.scalar_tensor_tensor(out=d, in0=src[:, at:at + F, :], scalar=scale,
                                                    in1=rms_row.unsqueeze(1).broadcast_to([P, F, SEQ]), op0=ALU.mult, op1=ALU.mult)
                    at += F
                last.then_inc(feat_out, 1)

            def ffn(b, l, off, e, T, n):
                f = ffn_no(b, l, e)

                def product(stp, banks=(G, G + 1)):
                    for t in range(TB):
                        dve.wait_ge(silu_done, 2 * FF_STEPS * f + 2 * stp + t + 1)
                        dve.scalar_tensor_tensor(out=prod[:, t, :], in0=ps[:, banks[t], 256:512], scalar=stat[:, 0, 2, t:t + 1],
                                                 in1=silu_g[:, t, :], op0=ALU.mult, op1=ALU.mult).then_inc(prod_ready, 1)

                def rest(stp):
                    dve.wait_ge(act_hi, FF_STEPS * f + stp + 1)
                    flat = lambda m: m[:, :, :, :].rearrange("p k t c -> p (k t c)")
                    dve.tensor_tensor(flat(aT_lo), ps[:, TR, :], flat(aT_hi).bitcast(F32), ALU.subtract).then_inc(act_lo, 1)

                turn_out(T, range(PIECES) if e == 0 else (2, 3))
                inverse(n)
                product(0, (ACC, ACC + 2))
                with dve.Fori(0, FF_STEPS - 1) as c:
                    rest(c)
                    product(c + 1)
                rest(FF_STEPS - 1)
                add_and_norm(b, l, 0 if e == 0 else ADDS[b] - 1, off + FFN_UNITS - 1, 0.5, n + 1, T + 1 if e == 0 else None)

            def head_norm(squares, o, summed, rooted):
                dve.tensor_reduce(hst[:, 0, :], squares.rearrange("p (g c) -> p g c", g=8), AX, ALU.add).then_inc(summed, 1)
                dve.wait_ge(*rooted)
                step(dve.reciprocal(hst[:, 2, :], hst[:, 1, :]))
                o3 = o.rearrange("p (g c) -> p g c", g=8)
                step(dve.tensor_tensor(o3, o3, hst[:, 2, :].unsqueeze(2).broadcast_to([P, 8, P]), ALU.mult))

            dve.wait_ge(x_loaded, 16)
            dve.sem_inc(x_ready, PIECES)
            for i in range(PIECES):
                gained(0, 0, i)
            with dve.Fori(0, DEPTH) as l:
                step, count = stepper(dve, vstep, V_START + l * V_A)
                ffn(0, l, A_FFN1, 0, turn_no(0, l, 0), norm_no(0, l, 0))
                dve.wait_ge(loaded, N_LOADS * 16)
                dve.tensor_copy(lb_l[:, 0, :], ln_lb[:, bass.ds(l, 1), :].rearrange("p a h -> p (a h)"))
                dve.tensor_copy(lb_l[:, 1, :], ln_1mlb[:, bass.ds(l, 1), :].rearrange("p a h -> p (a h)"))
                step(dve.tensor_copy(onorm_l[:, :], onorm[:, bass.ds(l, 1), :].rearrange("p a h -> p (a h)")))
                turn_out(turn_no(0, l, 1), (2, 3))
                inverse(norm_no(0, l, 1))
                rms_diag(1.0)

                def projected(i, pair, dst, scale=1.0):
                    scaled_out(0, l, A_IN + 2 * i, pair, row_no(0, l, 0), [(dst, scale)])

                projected(1, PAIRS[1], zf)
                dve.wait_ge(feat_out, taken_no(0, l, 1, "V"))
                absolute(tmp1, zf).then_inc(h_abs, 1)
                inverse(norm_no(0, l, 2), 1)
                projected(2, PAIRS[2], hq)
                dve.wait_ge(f_logit, l + 1)
                absolute(fcs_t, fcs_f).then_inc(f_abs, 1)
                dve.wait_ge(h_sp, l + 1)
                dve.scalar_tensor_tensor(out=hk, in0=zf, scalar=0.0, in1=tmp1, op0=ALU.max, op1=ALU.add)
                step(dve.scalar_tensor_tensor(out=tmp2, in0=zf, scalar=0.0, in1=tmp1, op0=ALU.min, op1=ALU.subtract))

                def head(m, h):
                    return m[:, h * SEQ:(h + 1) * SEQ]

                for h in range(H_HEADS):
                    last = dve.tensor_scalar(head(tmp1, h), head(tmp2, h), lb_l[:, 1, h:h + 1], None, ALU.add)
                step(last)
                for h in range(H_HEADS):
                    dve.tensor_scalar(head(zf, h), head(tmp1, h), lb_l[:, 0, h:h + 1], None, ALU.max)
                    last = dve.tensor_scalar(head(lev2, h), head(tmp1, h), lb_l[:, 0, h:h + 1], None, ALU.subtract)
                step(last)
                absolute(lev2[:, 0:1024], lev2[:, 0:1024]).then_inc(h_gate, 1)
                projected(4, PAIRS[0], fq, X_D ** -0.5)
                dve.wait_ge(f_sp, l + 1)
                step(dve.scalar_tensor_tensor(out=fcs_f, in0=fcs_f, scalar=0.0, in1=fcs_t, op0=ALU.min, op1=ALU.subtract))
                step(dve.tensor_tensor_scan(fcs_c, con("ones", rows=8), fcs_f, 0.0, ALU.mult, ALU.add))
                dve.tensor_scalar(fcs_n, fcs_c, -1.0, None, ALU.mult).then_inc(f_cum, 1)
                dve.memset(att, 0.0)
                projected(5, PAIRS[1], fk)
                dve.wait_ge(h_sp2, l + 1)
                step(dve.tensor_tensor(zf, zf, lev2[:, 0:1024], ALU.add))
                for h in range(H_HEADS):
                    last = dve.tensor_tensor_scan(head(cum, h), con("reset"), head(zf, h), 0.0, ALU.mult, ALU.add)
                step(last)
                NL = len(LEVELS) + 1
                NG = NL + 1

                def level(n, m_):
                    m = LEVELS[n] if n < NL - 1 else P
                    return m, m_.rearrange("p (b c) -> p b c", c=2 * m)

                def lev(n):
                    return lev2[:, n % 2 * 1024:n % 2 * 1024 + 1024]

                def diff(n):
                    m, e = level(n, lev(n))
                    g = level(n, cum)[1]
                    B = 1024 // (2 * m)
                    end = g[:, :, m - 1:m].broadcast_to([P, B, m])
                    dve.tensor_tensor(e[:, :, 0:m], end, g[:, :, 0:m], ALU.subtract)
                    if n < NL - 1:
                        last = dve.tensor_tensor(e[:, :, m:2 * m], g[:, :, m:2 * m], end, ALU.subtract)
                    else:
                        last = dve.tensor_copy(e[:, :, m:2 * m], g[:, :, m:2 * m])
                    last.then_inc(lev_diff, 1)

                def decayed(n):
                    m, e = level(n, lev(n))
                    dve.wait_ge(lev_exp, l * NL + n + 1)
                    dve.tensor_tensor(e[:, :, 0:m], e[:, :, 0:m], level(n, hk)[1][:, :, 0:m], ALU.mult)
                    dve.tensor_tensor(e[:, :, m:2 * m], e[:, :, m:2 * m], level(n, hq)[1][:, :, m:2 * m], ALU.mult).then_inc(lev_ready, 1)

                def keep(n):
                    bank = ACC + 2 * (n % 2)
                    mask = ident[:, :] if n == 0 else con("level", (n - 1) * P, P)
                    dve.copy_predicated(att.rearrange("p (g c) -> p g c", c=P),
                                        mask.bitcast(I32).unsqueeze(1).broadcast_to([P, 8, P]),
                                        ps[:, bank:bank + 2, :].rearrange("p a (g c) -> p (a g) c", c=P)).then_inc(lev_kept, 1)

                diff(0)
                dve.wait_ge(h_key, H_HEADS * (l + 1))
                for n in range(NL):
                    decayed(n)
                    if n + 1 < NL:
                        dve.wait_ge(lev_prod, l * NG + n + 1)
                        if n:
                            dve.wait_ge(lev_kept, l * NG + n)
                        diff(n + 1)
                        keep(n)
                dve.wait_ge(lev_prod, l * NG + NG)
                dve.wait_ge(lev_kept, l * NG + NL - 1)
                dve.tensor_copy(attx, ps[:, ACC + 2 * ((NG - 1) % 2), :]).then_inc(lev_kept, 1)
                keep(NL - 1)
                dve.wait_ge(h_sq, l + 1)
                head_norm(tmp1, tmp2, h_sum, (h_rms, l + 1))
                o3 = tmp2.rearrange("p (g c) -> p g c", g=8)
                step(dve.tensor_tensor(o3, o3, onorm_l[:, :].unsqueeze(1).broadcast_to([P, 8, P]), ALU.mult))
                for t in range(TB):
                    dve.tensor_tensor(piece(xn, t), tmp2[:, t * 512:(t + 1) * 512], hg[:, t * 512:(t + 1) * 512], ALU.mult).then_inc(xn_ready, 1)
                dve.wait_ge(f_cumS, l + 1)
                NA = X_HEADS * TB
                for i in range(NA):
                    h, t = divmod(i, 2)
                    w, at = P * (t + 1), i % 4 * 256
                    dve.wait_ge(a_score, l * NA + i + 1)
                    if i >= 4:
                        dve.wait_ge(a_prob, l * NA + i - 3)
                    dve.scalar_tensor_tensor(out=fsc[:, at:at + w], in0=ps[:, TR + i % 2, 0:w], scalar=sst[:, 3, 8 * t + h:8 * t + h + 1],
                                             in1=con("zeros", P - t * P, w), op0=ALU.add, op1=ALU.add).then_inc(a_masked, 1)
                    dve.wait_ge(a_masked, l * NA + i + 1)
                    step(dve.tensor_reduce(sst[:, 0, i:i + 1], fsc[:, at:at + w], AX, ALU.max))
                    dve.tensor_scalar(sst[:, 1, i:i + 1], sst[:, 0, i:i + 1], -1.0, None, ALU.mult).then_inc(a_max, 1)
                    if i == 2:
                        turn_out(turn_no(0, l, 2), (0, 1), (ACC, ACC + 2))
                dve.wait_ge(a_out, l * NA + NA)
                step(dve.reciprocal(sst[:, 4, :], sst[:, 2, :]))
                for t in range(TB):
                    dve.tensor_tensor(xn[:, t, 512:1024].rearrange("p (h d) -> p h d", h=X_HEADS),
                                      ps[:, ACC + 2 * t + 1, :].rearrange("p (h d) -> p h d", h=X_HEADS),
                                      sst[:, 4, :].rearrange("p (h t) -> p t h", t=TB)[:, t, :].unsqueeze(2).broadcast_to([P, X_HEADS, X_D]),
                                      ALU.mult).then_inc(xn_ready, 1)
                turn_out(turn_no(0, l, 2), (2, 3))
                dve.wait_ge(gain_loaded, 16 * norm_no(0, l, 2) + 16)
                for i in range(PIECES):
                    dve.scalar_tensor_tensor(out=piece(xn, i), in0=piece(memx, i), scalar=stat[:, 1, 2, i % 2:i % 2 + 1],
                                             in1=gain[:, i // 2 * 512:(i // 2 + 1) * 512], op0=ALU.mult, op1=ALU.mult).then_inc(xn_ready, 1)
                T3, T4 = turn_no(0, l, 3), turn_no(0, l, 4)
                turn_out(T3, (0, 1))
                for i in range(PIECES):
                    add(0, l, 1, i, A_OUT + 3, 1.0)
                turn_out(T3, (2, 3))
                for i in range(PIECES):
                    gained(add_no(0, l, 1), norm_no(0, l, 3), i)
                inverse(norm_no(0, l, 3))
                rms_diag(1.0)
                turn_out(T4, range(PIECES))
                for i, dst in enumerate((hg, fq)):
                    scaled_out(0, l, A_Q + 2 * i, PAIRS[(4 + i) % 3], row_no(0, l, 1), [(dst, C_D ** -0.5)])
                NC = C_HEADS * TB

                def heads_out(half):
                    a = half * NC // 2
                    dve.wait_ge(c_out, l * NC + a + NC // 2)
                    step(dve.reciprocal(sst[:, 4, a:a + NC // 2], sst[:, 2, a:a + NC // 2]))
                    for t in range(TB):
                        dve.tensor_tensor(piece(xn, 2 * half + t).rearrange("p (h d) -> p h d", d=C_D),
                                          ps[:, ACC + 2 * t + half, :].rearrange("p (h d) -> p h d", d=C_D),
                                          sst[:, 4, a:a + NC // 2].rearrange("p (h t) -> p t h", t=TB)[:, t, :].unsqueeze(2).broadcast_to([P, 2, C_D]),
                                          ALU.mult).then_inc(xn_ready, 1)

                for i in range(NC):
                    dve.wait_ge(c_score, l * NC + i + 1)
                    step(dve.tensor_reduce(sst[:, 0, i:i + 1], ps[:, TR + i % 2, 0:256], AX, ALU.max))
                    dve.tensor_scalar(sst[:, 1, i:i + 1], sst[:, 0, i:i + 1], -1.0, None, ALU.mult).then_inc(c_max, 1)
                    if i == NC - 2:
                        heads_out(0)
                turn_out(turn_no(0, l, 5), (0, 1), (ACC, ACC + 2))
                heads_out(1)
                turn_out(turn_no(0, l, 5), (2, 3))
                add_and_norm(0, l, 2, A_O + 3, 1.0, norm_no(0, l, 4), turn_no(0, l, 6))
                ffn(0, l, A_FFN2, 1, turn_no(0, l, 6), norm_no(0, l, 4))
                assert count[0] == V_A, ("V_A", count[0])

            def final_norm(n):
                inverse(n)
                for i in range(PIECES):
                    dve.tensor_scalar(piece(xres, i), piece(xn, i), stat[:, 0, 2, i % 2:i % 2 + 1], None, ALU.mult).then_inc(x_ready, 1)

            final_norm(norm_no(0, DEPTH, 0))
            for i in range(PIECES):
                gained(add_no(0, DEPTH, 0), norm_no(1, 0, 0), i)
            dve.wait_ge(loaded, N_LOADS * 16 + 16)
            with dve.Fori(0, DEPTH) as l:
                step, count = stepper(dve, vstep, V_START + DEPTH * V_A + l * V_B)
                dve.tensor_copy(wpool_l[:, :, :].rearrange("p g c -> p (g c)"), wpool[:, bass.ds(l, 1), :, :].rearrange("p a g c -> p (a g c)"))
                step(dve.tensor_copy(pscale_l[:, :], pscale[:, bass.ds(l, 1), :].rearrange("p a k -> p (a k)")))
                dve.sem_inc(p_wl, 1)
                ffn(1, l, B_FFN1, 0, turn_no(1, l, 0), norm_no(1, l, 0))
                turn_out(turn_no(1, l, 1), (2, 3))
                inverse(norm_no(1, l, 1))
                rms_diag(-1.0)
                wait_taken(dve, 1, l, 0)
                parts = []
                for t, tmp in enumerate((st1, st3)):
                    xx = qk_r[:, t * 512:(t + 1) * 512].rearrange("p (h d) -> p h d", h=8)
                    x1, x2 = xx[:, :, 0:32], xx[:, :, 32:64]
                    cos, sin = (con(n, t * 32, 32).unsqueeze(1).broadcast_to([P, 8, 32]) for n in ("cos", "sin"))
                    q = [tmp[:, n * 256:(n + 1) * 256].rearrange("p (h d) -> p h d", h=8) for n in range(4)]
                    for o, a, c in zip(q, (x1, x2, x2, x1), (cos, sin, cos, sin)):
                        last = dve.tensor_tensor(o, a, c, ALU.mult)
                    parts.append(q)
                step(last)
                for t, q in enumerate(parts):
                    rot = qk_rot[:, t * 512:(t + 1) * 512].rearrange("p (h d) -> p h d", h=8)
                    dve.tensor_tensor(rot[:, :, 0:32], q[0], q[1], ALU.subtract)
                    dve.tensor_tensor(rot[:, :, 32:64], q[2], q[3], ALU.add).then_inc(r_rot, 1)
                scaled_out(1, l, B_IN + 2, PAIRS[1], row_no(1, l, 0), [(qk_sb[:, 0:512], 64 ** -0.5), (qk_sb[:, 512:1024], 1.0)])
                zs = ps[:, 3:6, :].rearrange("p a c -> p (a c)")
                dve.wait_ge(r_score, 2 * l + 2)
                dve.tensor_tensor(sc_r[:, 0:1024], ps[:, 0:2, :].rearrange("p a c -> p (a c)"), con("decay"), ALU.mult)
                dve.tensor_tensor(sc_r[:, 1024:1536].rearrange("p (h c) -> p h c", h=4), ps[:, 2, :].rearrange("p (h c) -> p h c", h=4),
                                  con("decay").rearrange("p (h o c) -> p h o c", h=4, o=2)[:, :, 0, :], ALU.mult).then_inc(r_dec, 1)
                dve.wait_ge(r_turn, TB * (l + 1))
                dve.wait_ge(s_sp, l + 1)
                dve.scalar_tensor_tensor(out=st2, in0=zs, scalar=0.0, in1=st1, op0=ALU.min, op1=ALU.subtract)
                step(dve.scalar_tensor_tensor(out=st3, in0=zs, scalar=0.0, in1=st1, op0=ALU.max, op1=ALU.add))

                def masked(m):
                    strict = con("strict").unsqueeze(1).broadcast_to([P, 4, P])
                    a = m[:, 0:1024].rearrange("p (h o c) -> p h o c", h=4, o=2)[:, :, 0, :]
                    c = m[:, 1024:1536].rearrange("p (h c) -> p h c", h=4)
                    dve.tensor_tensor(a, a, strict, ALU.mult)
                    return dve.tensor_tensor(c, c, strict, ALU.mult)

                masked(st3).then_inc(s_fail, 1)
                dve.wait_ge(s_after, l + 1)
                dve.tensor_tensor(st2, st2, ps[:, 0:3, :].rearrange("p a c -> p (a c)"), ALU.add).then_inc(s_sum, 1)
                dve.wait_ge(s_exp, l + 1)
                masked(st2).then_inc(s_w, 1)
                dve.wait_ge(r_sq, l + 1)
                head_norm(qk_sb, v_r, r_sum, (r_rms, l + 1))
                dve.tensor_tensor(v_r, v_r, g_r, ALU.mult).then_inc(r_y, 1)
                dve.wait_ge(s_hi, l + 1)
                dve.tensor_tensor(hT_lo[:, :, 0:2, :].rearrange("p t k c -> p k t c"), ps[:, 3, :].rearrange("p (k t c) -> p k t c", k=2, t=TB),
                                  hT_hi[:, :, 0:2, :].rearrange("p t k c -> p k t c").bitcast(F32), ALU.subtract).then_inc(s_lo, 1)
                dve.wait_ge(p_hi, 2 * l + 2)
                for k in range(2):
                    last = dve.scalar_tensor_tensor(out=hT_lo[:, :, 6 + k, :], in0=ps[:, 4, k * 256:(k + 1) * 256].rearrange("p (t c) -> p t c", t=TB),
                                                    scalar=pscale_l[:, k:k + 1], in1=hT_hi[:, :, 6 + k, :].bitcast(F32),
                                                    op0=ALU.mult, op1=ALU.subtract)
                last.then_inc(p_lo, 1)
                for t in range(TB):
                    dve.wait_ge(r_hi, l * TB + t + 1)
                    dve.tensor_tensor(hT_lo[:, t, 2:6, :].rearrange("p k c -> p (k c)"), ps[:, TR + t, :],
                                      hT_hi[:, t, 2:6, :].rearrange("p k c -> p (k c)").bitcast(F32), ALU.subtract).then_inc(r_lo, 1)

                def gated(out, n, bank, t):
                    return dve.tensor_tensor(out.rearrange("p (h c) -> p h c", h=2), ps[:, bank + 2 * t:bank + 2 * t + 2, :],
                                             gates[:, n * 2048:(n + 1) * 2048].rearrange("p (h t c) -> p t h c", h=2, t=TB)[:, t], ALU.mult)

                def tmp(t):
                    return br_tmp[:, t * DM:(t + 1) * DM]

                wait_unit(dve, 1, l, B_BR)
                for t in range(TB):
                    last = gated(xn[:, t, :], 0, 0, t)
                last.then_inc(br_used, 1)
                wait_unit(dve, 1, l, B_BR + 2)
                for t in range(TB):
                    last = gated(tmp(t), 1, 4, t)
                step(last)
                dve.wait_ge(br_used, 2 * l + 1)
                for t in range(TB):
                    last = dve.tensor_tensor(xn[:, t, :], xn[:, t, :], tmp(t), ALU.add)
                last.then_inc(br_used, 1)
                dve.wait_ge(br_used, 2 * l + 2)
                wait_unit(dve, 1, l, B_BR + 3)
                for i in range(PIECES):
                    h, t = divmod(i, 2)
                    step(dve.tensor_tensor(piece(br_tmp.rearrange("p (t d) -> p t d", t=TB), i), ps[:, 2 * t + h, :],
                                           gates[:, 4096 + i * 512:4096 + (i + 1) * 512], ALU.mult))
                    dve.tensor_tensor(piece(xn, i), piece(xn, i), piece(br_tmp.rearrange("p (t d) -> p t d", t=TB), i), ALU.add).then_inc(xn_ready, 1)
                turn_out(turn_no(1, l, 2), range(PIECES))
                add_and_norm(1, l, 1, B_OUT + 3, 1.0, norm_no(1, l, 2), turn_no(1, l, 3))
                ffn(1, l, B_FFN2, 1, turn_no(1, l, 3), norm_no(1, l, 2))
                assert count[0] == V_B, ("V_B", count[0])
            final_norm(norm_no(1, DEPTH, 0))


FFN_NAMES = {(0, 0): ("ffn1_w_gate", "ffn1_w_up", "ffn1_w_down"), (0, 1): ("ffn2_w_gate", "ffn2_w_up", "ffn2_w_down"),
             (1, 0): ("w1_ffn1_2", "w3_ffn1_2", "w2_ffn1_2"), (1, 1): ("w1_ffn2_2", "w3_ffn2_2", "w2_ffn2_2")}
WEIGHTS = ("w_in", "w_out", "cross_wq", "cross_wk", "cross_wv", "cross_wo", "w_in_2", "w_branch_sb_2", "w_branch_ret_2",
           "w_branch_pool_2", "w_out_2")
NORM_ORDER = (("ffn1_norm", "mix_norm", "mem_norm", "cross_norm", "ffn2_norm"), ("g_ffn1_2", "g_mix_2", "g_ffn2_2"))


def kernel(**inputs):
    import concourse.bacc as bacc
    from concourse.bass_utils import run_bass_kernel_spmd

    a = {k: np.asarray(v) for k, v in inputs.items()}
    gains = []
    for names, last in zip(NORM_ORDER, ("final_norm", "g_final_2")):
        gains += [a[n][l] for l in range(DEPTH) for n in names] + [a[last]]
    table_a, table_b, eye = constants()
    small = dict(
        x=a["x"], mem=a["mem"], gains=np.stack(gains), table_a=table_a, table_b=table_b, eye=eye,
        lb=a["hgrn_lb"].reshape(DEPTH, H_HEADS, P).transpose(2, 0, 1), out_norm=a["hgrn_out_norm"],
        f_bias=a["fox_f_bias"].T, w_pool=a["w_pool_2"].transpose(2, 0, 1, 3),
        pool_scale=a["pool_scale_2"].reshape(DEPTH, 2, P).transpose(2, 0, 1))
    big = {n: a[n] for n in WEIGHTS} | {n: a[n] for names in FFN_NAMES.values() for n in names}
    nc = bacc.Bacc("TRN2", target_bir_lowering=False, num_devices=1)
    arrays, aps = {}, {}
    for name, v in (small | big).items():
        arrays["in_" + name] = np.ascontiguousarray(v)
        aps[name] = nc.dram_tensor("in_" + name, v.shape, mybir.dt.from_np(v.dtype), kind="ExternalInput").ap()
    out = nc.dram_tensor("out_0", (1, SEQ, DM), F32, kind="ExternalOutput").ap()
    W = {n: aps[n] for n in WEIGHTS}
    for (b, e), names in FFN_NAMES.items():
        for what, n in zip(("gate", "up", "down"), names):
            W[b, e, what] = aps[n]
    build(nc, *(aps[n] for n in small), W, out)
    r = run_bass_kernel_spmd(nc, [arrays], core_ids=[0])
    return r.results[0]["out_0"]
```

```python
from contextlib import ExitStack

import numpy as np
import concourse.bass as bass
from concourse import mybir

F32 = mybir.dt.float32
F32R = mybir.dt.float32r
I32 = mybir.dt.int32
ALU = mybir.AluOpType
ACT = mybir.ActivationFunctionType
AX = mybir.AxisListType.X

P = 128
SEQ, DM, DFF, DEPTH = 256, 1024, 2816, 2
TB = SEQ // P
KT = DM // P
EPS = 1e-6
FF_STEPS = DFF // 256
RING = 3
CREDIT = RING
FFN_UNITS = 3 * FF_STEPS
MASKED = -1e30
N_LOADS = 7
S_A, S_B = 3, 2
V_A, V_B = 38, 10

A_FFN1 = 0
A_IN = FFN_UNITS
A_OUT = A_IN + 16
A_K = A_OUT + 4
A_V = A_K + 4
A_Q = A_V + 4
A_O = A_Q + 4
A_FFN2 = A_O + 4
A_UNITS = A_FFN2 + FFN_UNITS
B_FFN1 = 0
B_IN = FFN_UNITS
B_BR = B_IN + 22
B_OUT = B_BR + 4
B_FFN2 = B_OUT + 4
B_UNITS = B_FFN2 + FFN_UNITS
assert A_UNITS % RING == 0 and B_UNITS % RING == 0 and A_FFN2 % RING == 0 and B_FFN2 % RING == 0
LAYER_UNITS = (A_UNITS, B_UNITS)
FIRST_UNIT = (0, DEPTH * A_UNITS)

TURNS = (7, 4)
FIRST_TURN = (0, DEPTH * 7)
ROWS = (2, 1)
NORMS = (5, 3)
FIRST_NORM = (0, DEPTH * 5 + 1)
ADDS = (4, 3)
FIRST_ADD = (1, DEPTH * 4 + 2)

H_HEADS, H_D = 4, 128
X_HEADS, X_D = 8, 64
C_HEADS, C_D = 4, 256
PIECES = 2 * TB
HEAD_ORDER = (0, 2, 1, 3)
TAKEN = ("SVVVVSS" "SSSSVV", "SVSSSSSSSSS")
LEVELS = (64, 32, 16, 8, 4, 2, 1)
POOL_WINDOWS = (2, 4, 8, 16)

TABLES = (dict(level=128 * len(LEVELS), reset=256, zeros=128, causal=128, sel=1024, ones=256),
          dict(neg_later=128, neg_ones=128, strict=128, cos=64, sin=64, decay=1024, pool=1536))
CONST_AT = {name: (sum(list(t.values())[:n]), cols) for t in TABLES for n, (name, cols) in enumerate(t.items())}
N_CONST = max(sum(t.values()) for t in TABLES)


def constants():
    c = np.zeros((2, P, N_CONST), np.float32)

    def part(name):
        at, cols = CONST_AT[name]
        return c[0 if name in TABLES[0] else 1][:, at:at + cols]

    i = np.arange(P)
    s, t = i[:, None], i[None, :]
    for n, m in enumerate(LEVELS):
        part("level")[:, n * P:(n + 1) * P] = (s // (2 * m) == t // (2 * m)) & (s % (2 * m) < m) & (t % (2 * m) >= m)
    part("reset")[:] = (np.arange(SEQ) % P != 0)[None, :]
    part("causal")[:] = np.where(t <= s, 0.0, MASKED)
    for h in range(8):
        part("sel")[h, h * P:(h + 1) * P] = 1.0
    part("ones")[:] = 1.0
    part("neg_later")[:] = -(s > t).astype(np.float32)
    part("neg_ones")[:] = -1.0
    part("strict")[:] = s < t
    half = 32
    freq = np.float32(10000.0) ** (-np.arange(half, dtype=np.float32) / half)
    ang = np.arange(SEQ, dtype=np.float32)[:, None] * freq[None, :]
    for name, f in (("cos", np.cos), ("sin", np.sin)):
        part(name)[:] = f(ang).reshape(TB, P, half).transpose(1, 0, 2).reshape(P, TB * half)
    for h, head in enumerate(HEAD_ORDER):
        g = np.log(1.0 - 2.0 ** (-5.0 - head))
        for o in range(2):
            d = t + o * P - s
            w = np.where(d >= 0, np.exp(np.maximum(d, 0) * g), 0.0) * 64 ** -0.5
            part("decay")[:, (h * 2 + o) * P:(h * 2 + o + 1) * P] = w
    for n, win in enumerate(POOL_WINDOWS):
        for m, (sb, tb) in enumerate(((0, 0), (0, 1), (1, 1))):
            S, T = s + sb * P, t + tb * P
            count = np.minimum(T + 1, win)
            w = ((S <= T) & (S > T - win)) / count - (S == T)
            part("pool")[:, (n * 3 + m) * P:(n * 3 + m + 1) * P] = w
    return c[0], c[1], np.eye(P, dtype=np.float32)


def build(nc, x, mem, gains, table_a, table_b, eye, lb, out_norm, f_bias, w_pool, pool_scale, W, out):
    with ExitStack() as ctx:
        def sb(name, shape, dt=F32):
            return ctx.enter_context(nc.sbuf_tensor(name, shape, dt))

        def sem(name):
            return ctx.enter_context(nc.semaphore(name))

        raw = sb("raw", [P, RING, 4, 512])
        whi = sb("whi", [P, RING, 4, 512], F32R)
        wlo = sb("wlo", [P, RING, 4, 512], F32R)
        xres = sb("xres", [P, TB, DM])
        xn = sb("xn", [P, TB, DM])
        hT_hi = sb("hT_hi", [P, TB, KT, P], F32R)
        hT_lo = sb("hT_lo", [P, TB, KT, P], F32R)
        gain = sb("gain", [P, DM])
        silu_g = sb("silu_g", [P, TB, 256])
        prod = sb("prod", [P, TB, 256])
        aT_hi = sb("aT_hi", [P, 2, TB, P], F32R)
        aT_lo = sb("aT_lo", [P, 2, TB, P], F32R)
        ident = sb("ident", [P, P])
        cst = sb("cst", [P, N_CONST])
        stat = sb("stat", [P, 2, 3, TB])
        lbt = sb("lbt", [P, DEPTH, H_HEADS])
        lbw = sb("lbw", [P, 3, H_HEADS])
        lb_l = sb("lb_l", [P, 2, H_HEADS])
        onorm_l = sb("onorm_l", [P, H_D])
        pscale_l = sb("pscale_l", [P, 2])
        flog = sb("flog", [P, TB, 8])
        ln_lb = sb("ln_lb", [P, DEPTH, H_HEADS])
        ln_1mlb = sb("ln_1mlb", [P, DEPTH, H_HEADS])
        onorm = sb("onorm", [P, DEPTH, H_D])
        fbias = sb("fbias", [8, DEPTH])
        wpool = sb("wpool", [64, DEPTH, 4, 64])
        wpool_l = sb("wpool_l", [64, 4, 64])
        pscale = sb("pscale", [P, DEPTH, 2])
        sst = sb("sst", [P, 5, 16])
        hst = sb("hst", [P, 3, 8])
        arena = sb("arena", [P, 18432])

        def take(*spans):
            at, got = 0, []
            for n in spans:
                got.append(arena[:, at:at + n])
                at += n
            assert at <= 18432, at
            return got

        (memx_, zf, hq, hk, hv, hg, fq, fk, fv, cum, tmp1, tmp2, lev2, att, attx, fpT, fcs) = take(
            2048, *[1024] * 11, 2048, 1024, 512, 512, 1024)
        memx = memx_.rearrange("p (t d) -> p t d", t=TB)
        fsc, fp = lev2[:, 0:1024], lev2[:, 1024:2048]
        norm_diag, rms_row = fpT[:, 0:256], fpT[:, 256:512]
        sq_junk = lev2
        fcs_f, fcs_c, fcs_n, fcs_t = (fcs[0:8, 256 * n:256 * n + 256] for n in range(4))
        (qk_sb, qk_r, vu, v_r, g_r, pool_d, gates, st1, st2, st3, sc_r) = take(*[1024] * 6, 6144, *[1536] * 4)
        qk_rot = st2[:, 0:1024]
        qk_rT = qk_r
        br_tmp = arena[:, 12288:12288 + 2048]
        ps = ctx.enter_context(nc.psum_tensor("ps", [P, 8, 512], F32))
        ACC, G, TR = 0, 4, 6
        PAIRS = (4, 0, 2)

        GATED_PAIRS = (4, 0, 2, 4, 0) + (4, 6) * 3

        HYBRID_PAIRS = (4, 0, 2, None, 4, 6, 4, 6)

        def last_aT(hT):
            return hT[:, :, 4:6, :].rearrange("p t k c -> p k t c")

        def con(name, a=0, n=None, rows=P):
            at, cols = CONST_AT[name]
            return cst[0:rows, at + a:at + a + (cols if n is None else n)]

        loaded = sem("loaded")
        ident_loaded = sem("ident_loaded")
        x_loaded = sem("x_loaded")
        gain_loaded = sem("gain_loaded")
        raw_loaded = [sem(f"raw_loaded{s}") for s in range(RING)]
        hi_ready = sem("hi_ready")
        lo_ready = sem("lo_ready")
        unit_done = sem("unit_done")
        acc_done = sem("acc_done")
        x_ready = sem("x_ready")
        sq_sum = sem("sq_sum")
        sq_done = sem("sq_done")
        inv_ready = sem("inv_ready")
        row_diag = sem("row_diag")
        row_made = sem("row_made")
        row_ready = sem("row_ready")
        xn_ready = sem("xn_ready")
        turned = sem("turned")
        turn_hi = sem("turn_hi")
        turn_lo = sem("turn_lo")
        silu_done = sem("silu_done")
        prod_ready = sem("prod_ready")
        act_turned = sem("act_turned")
        act_hi = sem("act_hi")
        act_lo = sem("act_lo")
        chunk_out = sem("chunk_out")
        feat_out = sem("feat_out")
        vstep = sem("vstep")
        pstep = sem("pstep")
        sstep = sem("sstep")
        lb_abs, lb_sp = sem("lb_abs"), sem("lb_sp")
        h_abs, h_sp, h_gate, h_sp2 = sem("h_abs"), sem("h_sp"), sem("h_gate"), sem("h_sp2")
        h_key, h_query, h_inv = sem("h_key"), sem("h_query"), sem("h_inv")
        lev_diff, lev_exp, lev_ready, lev_prod, lev_kept = (sem(f"lev_{n}") for n in ("diff", "exp", "ready", "prod", "kept"))
        h_out, h_sq, h_sum, h_rms = sem("h_out"), sem("h_sq"), sem("h_sum"), sem("h_rms")
        f_abs, f_sp, f_cum, f_cumT, f_cumS = (sem(f"f_{n}") for n in ("abs", "sp", "cum", "cumT", "cumS"))
        f_tm, f_turn, f_logit = sem("f_tm"), sem("f_turn"), sem("f_logit")
        a_score, a_masked, a_max, a_prob, a_turn, a_pT, a_out = (
            sem(f"a_{n}") for n in ("score", "masked", "max", "prob", "turn", "pT", "out"))
        c_score, c_max, c_prob, c_turn, c_pT, c_out = (sem(f"c_{n}") for n in ("score", "max", "prob", "turn", "pT", "out"))
        r_rot, r_turn, r_kT, r_score, r_dec, r_out, r_sq, r_sum, r_rms, r_y, r_yT, r_hi, r_lo = (
            sem(f"r_{n}") for n in ("rot", "turn", "kT", "score", "dec", "out", "sq", "sum", "rms", "y", "yT", "hi", "lo"))
        s_score, s_sp, s_fail, s_after, s_sum, s_exp, s_w, s_out, s_hi, s_lo = (
            sem(f"s_{n}") for n in ("score", "sp", "fail", "after", "sum", "exp", "w", "out", "hi", "lo"))
        p_diff, p_dT, p_wl, p_out, p_hi, p_lo = (sem(f"p_{n}") for n in ("diff", "dT", "wl", "out", "hi", "lo"))
        br_piece, br_used = sem("br_piece"), sem("br_used")
        stored = sem("stored")

        def unit(b, l, off, c=0):
            return FIRST_UNIT[b] + l * LAYER_UNITS[b] + off + 3 * c

        def use(b, l, off, c=0):
            return FIRST_UNIT[b] // RING + l * (LAYER_UNITS[b] // RING) + off // RING + c + 1

        def turn_no(b, l, j):
            return FIRST_TURN[b] + l * TURNS[b] + j

        def norm_no(b, l, j):
            return FIRST_NORM[b] + l * NORMS[b] + j

        def add_no(b, l, j):
            return FIRST_ADD[b] + l * ADDS[b] + j

        def ffn_no(b, l, e):
            return 2 * DEPTH * b + 2 * l + e

        def acc_no(b, l, j):
            return (0, DEPTH * ADDS[0])[b] + l * ADDS[b] + j

        def row_no(b, l, j):
            return (0, DEPTH * ROWS[0])[b] + l * ROWS[b] + j

        def xn_no(b, T):
            return T + b

        def piece(m, i):
            return m[:, i % 2, i // 2 * 512:(i // 2 + 1) * 512]

        def taken_no(b, l, j, who):
            per_layer = [t.count(who) for t in TAKEN]
            return (0, DEPTH * per_layer[0])[b] + l * per_layer[b] + TAKEN[b][:j + 1].count(who)

        def wait_taken(eng, b, l, j):
            who = TAKEN[b][j]
            eng.wait_ge(chunk_out if who == "S" else feat_out, taken_no(b, l, j, who))

        def wait_unit(eng, b, l, off, c=0):
            eng.wait_ge(unit_done, unit(b, l, off, c) + 1 + CREDIT)

        def stepper(eng, done, base):
            count = [0]

            def step(ins):
                count[0] += 1
                ins.then_inc(done, 1)
                eng.wait_ge(done, base + count[0])

            return step, count

        block = ctx.enter_context(nc.Block())

        @block.sync
        def _(sp):
            def load(b, l, off, c, parts):
                s = off % RING
                sp.wait_ge(lo_ready, unit(b, l, off, c) + 1)
                for dst, src in reversed(parts(raw[:, s])):
                    sp.dma_start(dst, src).then_inc(raw_loaded[s], 16)

            def cols(a, b_):
                def parts(slot):
                    v = slot.rearrange("p k (t n) -> p k t n", t=2)
                    return [(v[:, :, t, :], src.rearrange("(k p) n -> p k n", p=P)) for t, src in enumerate((a, b_))]
                return parts

            def rows(w):
                def parts(slot):
                    v = slot.rearrange("p (k t) n -> p k (t n)", k=2)
                    return [(v[:, k, :], w[k * P:(k + 1) * P, :]) for k in range(2)]
                return parts

            def ffn(b, l, off, e):
                wg, wu, wd = W[b, e, "gate"], W[b, e, "up"], W[b, e, "down"]

                def gate_up(off, c, step):
                    for k in range(2):
                        load(b, l, off + k, c, cols(*(w[l, k * 512:(k + 1) * 512, bass.ds(step * 256, 256)] for w in (wg, wu))))

                def down(off, c, step):
                    load(b, l, off, c, rows(wd[l, bass.ds(step * 256, 256), :]))

                gate_up(off, 0, 0)
                with sp.Fori(0, FF_STEPS - 1) as c:
                    gate_up(off + 2, c, c + 1)
                    down(off + 4, c, c)
                down(off + FFN_UNITS - 1, 0, FF_STEPS - 1)

            def chunk(b, l, off, w, c0, c1):
                for k in range(2):
                    load(b, l, off + k, 0, cols(*(w[l, k * 512:(k + 1) * 512, a:a + 256] for a in (c0, c1))))

            def tall(b, l, off, n, w):
                for u in range(n):
                    load(b, l, off + u, 0, rows(w[l, u * 256:(u + 1) * 256, :]))

            with sp.Fori(0, DEPTH) as l:
                ffn(0, l, A_FFN1, 0)
                w = W["w_in"]
                for n, c0 in enumerate((1536, 512, 0, None, 2048, 2560, 3072, 1024)):
                    off = A_IN + 2 * n
                    if c0 is not None:
                        chunk(0, l, off, w, c0, c0 + 256)
                        continue
                    for k in range(2):
                        load(0, l, off + k, 0, lambda slot, k=k: [
                            (slot[:, 2 * i:2 * i + 2, 0:8],
                             w[l, k * 512 + i * 256:k * 512 + (i + 1) * 256, 3584:3592].rearrange("(k p) n -> p k n", p=P))
                            for i in range(2)])
                tall(0, l, A_OUT, 4, W["w_out"])
                for off, name in ((A_K, "cross_wk"), (A_V, "cross_wv"), (A_Q, "cross_wq")):
                    for i in range(2):
                        chunk(0, l, off + 2 * i, W[name], 512 * i, 512 * i + 256)
                tall(0, l, A_O, 4, W["cross_wo"])
                ffn(0, l, A_FFN2, 1)
            with sp.Fori(0, DEPTH) as l:
                ffn(1, l, B_FFN1, 0)
                for n, (c0, c1) in enumerate([(768, 1024), (0, 256), (512, 2304), (1280, 1536), (1792, 2048)]
                                             + [(2560 + 512 * i, 2816 + 512 * i) for i in range(6)]):
                    chunk(1, l, B_IN + 2 * n, W["w_in_2"], c0, c1)
                tall(1, l, B_BR, 1, W["w_branch_sb_2"])
                tall(1, l, B_BR + 1, 1, W["w_branch_pool_2"])
                tall(1, l, B_BR + 2, 2, W["w_branch_ret_2"])
                tall(1, l, B_OUT, 4, W["w_out_2"])
                ffn(1, l, B_FFN2, 1)
            o = out[0].rearrange("(t p) d -> p t d", p=P)
            for i in range(PIECES):
                sp.wait_ge(x_ready, PIECES * add_no(1, DEPTH, 0) + i + 1)
                sp.dma_start(piece(o, i), piece(xres, i)).then_inc(stored, 16)
            sp.wait_ge(stored, 16 * PIECES)

        @block.gpsimd
        def _(pool):
            pool.sem_inc(lo_ready, CREDIT)

            def split_lo(n, s):
                pool.wait_ge(hi_ready, n + 1)
                pool.tensor_tensor(wlo[:, s], raw[:, s], whi[:, s].bitcast(F32), ALU.subtract).then_inc(lo_ready, 1)

            def forget_unit(n, s):
                pool.wait_ge(hi_ready, n + 1)
                pool.tensor_tensor(wlo[:, s, :, 0:8], raw[:, s, :, 0:8], whi[:, s, :, 0:8].bitcast(F32),
                                   ALU.subtract).then_inc(lo_ready, 1)

            def hgrn_norm():
                pool.wait_ge(h_inv, l + 1)
                o3 = tmp2.rearrange("p (g c) -> p g c", g=8)
                pool.tensor_tensor(o3, o3, hst[:, 2, :].unsqueeze(2).broadcast_to([P, 8, P]), ALU.mult).then_inc(pstep, 1)
                pool.wait_ge(pstep, 2 * l + 1)
                pool.tensor_tensor(o3, o3, onorm_l[:, :].unsqueeze(1).broadcast_to([P, 8, P]), ALU.mult).then_inc(pstep, 1)
                pool.wait_ge(pstep, 2 * l + 2)
                for t in range(TB):
                    pool.tensor_tensor(piece(xn, t), tmp2[:, t * 512:(t + 1) * 512], hg[:, t * 512:(t + 1) * 512], ALU.mult).then_inc(xn_ready, 1)

            FORGET = A_IN + 6
            with pool.Fori(0, DEPTH) as l:
                with pool.Fori(0, FORGET // RING) as c:
                    for s in range(RING):
                        split_lo(unit(0, l, s, c), s)
                for u in range(FORGET, FORGET + 3):
                    (forget_unit if u < FORGET + 2 else split_lo)(unit(0, l, u), u % RING)
                with pool.Fori(0, (A_OUT - FORGET) // RING - 1) as c:
                    for s in range(RING):
                        split_lo(unit(0, l, FORGET + 3 + s, c), s)
                HELD = FORGET + (A_OUT - FORGET) // RING * RING
                while_held = range(HELD, A_OUT + RING)
                for u in while_held:
                    split_lo(unit(0, l, u), u % RING)
                hgrn_norm()
                REST = HELD + (len(while_held) + RING - 1) // RING * RING
                for u in range(A_OUT + RING, REST):
                    split_lo(unit(0, l, u), u % RING)
                with pool.Fori(0, (A_UNITS - REST) // RING) as c:
                    for s in range(RING):
                        split_lo(unit(0, l, REST + s, c), s)
            with pool.Fori(0, DEPTH) as l:
                with pool.Fori(0, B_UNITS // RING) as c:
                    for s in range(RING):
                        split_lo(unit(1, l, s, c), s)

        @block.scalar
        def _(act):
            act.dma_start(gain[:, :], gains[0:1, :].broadcast_to([P, DM])).then_inc(gain_loaded, 16)
            act.dma_start(xres[:, :, :], x[0].rearrange("(t p) d -> p t d", p=P)).then_inc(x_loaded, 16)
            act.dma_start(ident[:, :], eye).then_inc(ident_loaded, 16)
            for dst, src in ((lbt[:, :, :], lb), (onorm[:, :, :], out_norm.unsqueeze(0).broadcast_to([P, DEPTH, H_D])),
                             (fbias[:, :], f_bias), (wpool[:, :, :, :], w_pool), (pscale[:, :, :], pool_scale)):
                act.dma_start(dst, src).then_inc(loaded, 16)
            act.wait_ge(raw_loaded[0], 32)
            for dst, src in ((cst[:, :], table_a), (memx[:, :, :], mem[0].rearrange("(t p) d -> p t d", p=P))):
                act.dma_start(dst, src).then_inc(loaded, 16)

            def split_hi(b, l, off, c=0, cols=512):
                s = off % RING
                act.wait_ge(raw_loaded[s], 32 * use(b, l, off, c))
                act.wait_ge(unit_done, unit(b, l, off, c) + 1)
                act.activation(whi[:, s, :, 0:cols], raw[:, s, :, 0:cols], ACT.Copy).then_inc(hi_ready, 1)

            def squares(src, n, add=None, junk=(sq_junk[:, 0:DM], sq_junk[:, DM:2 * DM])):
                st = stat[:, 1 if add is None else 0]
                for t in range(TB):
                    if add is not None:
                        act.wait_ge(x_ready, PIECES * add + 2 + t + 1)
                    act.activation(junk[t], src[:, t, :], ACT.Square, accum_out=st[:, 0, t:t + 1]).then_inc(sq_sum, 1)
                act.wait_ge(sq_sum, 2 * n + 2)
                act.activation(st[:, 1, :], st[:, 0, :], ACT.Sqrt, scale=1.0 / DM, bias=EPS).then_inc(sq_done, 1)

            def next_gain(b, n, T):
                act.wait_ge(xn_ready, PIECES * (xn_no(b, T) + 1))
                act.dma_start(gain[:, :], gains[bass.ds(n + 1, 1), :].broadcast_to([P, DM])).then_inc(gain_loaded, 16)

            def turn_out(T, pieces, banks=(TR, TR + 1)):
                for i in pieces:
                    h, t = divmod(i, 2)
                    act.wait_ge(turned, PIECES * T + i + 1)
                    act.activation(hT_hi[:, t, 4 * h:4 * h + 4, :].rearrange("p k c -> p (k c)"), ps[:, banks[t], :],
                                   ACT.Copy).then_inc(turn_hi, 1)

            def row_out(r):
                act.wait_ge(row_made, r + 1)
                act.activation(rms_row, ps[:, TR, 0:SEQ], ACT.Copy).then_inc(row_ready, 1)

            def ffn(b, l, off, e, T, n, add):
                f = ffn_no(b, l, e)

                def silu(u, cc, step, banks=(G, G + 1)):
                    for t in range(TB):
                        if t == 0:
                            wait_unit(act, b, l, u, cc)
                        act.activation(silu_g[:, t, :], ps[:, banks[t], 0:256], ACT.Silu,
                                       scale=stat[:, 0, 2, t:t + 1]).then_inc(silu_done, 1)

                def evac(step, out=aT_hi):
                    act.wait_ge(act_turned, FF_STEPS * f + step + 1)
                    act.activation(out[:, :, :, :], ps[:, TR, :].rearrange("p (k t c) -> p k t c", k=2, t=TB),
                                   ACT.Copy).then_inc(act_hi, 1)

                turn_out(T, (0, 1))
                split_hi(b, l, off + 2)
                turn_out(T, (2, 3))
                next_gain(b, n, T)
                squares(xres, n, add)
                split_hi(b, l, off + 3)
                act.wait_ge(inv_ready, n + 1)
                silu(off + 1, 0, 0, (ACC, ACC + 2))
                split_hi(b, l, off + 4)
                with act.Fori(0, FF_STEPS - 2) as c:
                    evac(c)
                    split_hi(b, l, off + 5, c)
                    silu(off + 3, c, c + 1)
                    split_hi(b, l, off + 6, c)
                    split_hi(b, l, off + 7, c)
                evac(FF_STEPS - 2)
                split_hi(b, l, off + FFN_UNITS - 1)
                silu(off + FFN_UNITS - 3, 0, FF_STEPS - 1)
                evac(FF_STEPS - 1, last_aT(hT_hi))

            def chunk_out_(b, l, u, pair, dst, func):
                wait_unit(act, b, l, u + 1)
                act.activation(dst, ps[:, pair:pair + 2, :].rearrange("p a c -> p (a c)"), func).then_inc(chunk_out, 1)

            def normed_out(b, l, u, pair, dst, func):
                wait_unit(act, b, l, u + 1)
                for t in range(TB):
                    last = act.activation(dst[:, t * 512:(t + 1) * 512], ps[:, pair + t, :], func, scale=stat[:, 0, 2, t:t + 1])
                last.then_inc(chunk_out, 1)

            with act.Fori(0, DEPTH) as l:
                step, count = stepper(act, sstep, l * S_A)
                split_hi(0, l, A_FFN1)
                split_hi(0, l, A_FFN1 + 1)
                ffn(0, l, A_FFN1, 0, turn_no(0, l, 0), norm_no(0, l, 0), add_no(0, l, -1))
                U = A_IN
                split_hi(0, l, U)
                split_hi(0, l, U + 1)
                turn_out(turn_no(0, l, 1), (0, 1))
                split_hi(0, l, U + 2)
                turn_out(turn_no(0, l, 1), (2, 3))
                next_gain(0, norm_no(0, l, 1), turn_no(0, l, 1))
                split_hi(0, l, U + 3)
                squares(xres, norm_no(0, l, 1), add_no(0, l, 0))
                NL = len(LEVELS) + 1

                def level_exp(n):
                    e = lev2[:, (n % 2) * 1024:(n % 2) * 1024 + 1024]
                    act.wait_ge(lev_diff, l * NL + n + 1)
                    act.activation(e, e, ACT.Exp).then_inc(lev_exp, 1)

                split_hi(0, l, U + 4)
                act.wait_ge(inv_ready, norm_no(0, l, 1) + 1)
                normed_out(0, l, U, HYBRID_PAIRS[0], hg, ACT.Silu)
                act.wait_ge(loaded, N_LOADS * 16)
                squares(memx, norm_no(0, l, 2), junk=(hv, fv))
                split_hi(0, l, U + 5)
                row_out(row_no(0, l, 0))
                split_hi(0, l, U + 6, cols=8)
                act.wait_ge(lb_abs, l + 1)
                act.activation(lbw[:, 1, :], lbw[:, 1, :], ACT.Exp, scale=-1.0)
                act.wait_ge(h_abs, l + 1)
                step(act.activation(tmp1, tmp1, ACT.Exp, scale=-1.0))
                act.activation(lbw[:, 1, :], lbw[:, 1, :], ACT.Ln, bias=1.0).then_inc(lb_sp, 1)
                act.activation(tmp1, tmp1, ACT.Ln, bias=1.0).then_inc(h_sp, 1)
                split_hi(0, l, U + 7, cols=8)
                split_hi(0, l, U + 8)
                split_hi(0, l, U + 9)
                split_hi(0, l, U + 10)
                wait_unit(act, 0, l, U + 7)
                for t in range(TB):
                    last = act.activation(flog[:, t, :], ps[:, TR, 8 * t:8 * t + 8], ACT.Copy, scale=stat[:, 0, 2, t:t + 1])
                last.then_inc(f_tm, 1)
                act.wait_ge(h_gate, l + 1)
                step(act.activation(lev2[:, 0:1024], lev2[:, 0:1024], ACT.Exp, scale=-1.0))
                act.activation(lev2[:, 0:1024], lev2[:, 0:1024], ACT.Ln, bias=1.0).then_inc(h_sp2, 1)
                wait_taken(act, 0, l, 2)
                act.activation(hq, hq, ACT.Silu).then_inc(h_query, 1)
                split_hi(0, l, U + 11)
                act.wait_ge(f_turn, l + 1)
                act.activation(fcs_f, ps[0:8, TR + 1, 0:256], ACT.Identity, bias=fbias[:, bass.ds(l, 1)]).then_inc(f_logit, 1)
                for h in range(H_HEADS):
                    act.activation(hk[:, h * SEQ:(h + 1) * SEQ], hk[:, h * SEQ:(h + 1) * SEQ], ACT.Exp, scale=-1.0,
                                   bias=lb_l[:, 1, h:h + 1]).then_inc(h_key, 1)
                act.wait_ge(f_abs, l + 1)
                step(act.activation(fcs_t, fcs_t, ACT.Exp, scale=-1.0))
                act.activation(fcs_t, fcs_t, ACT.Ln, bias=1.0).then_inc(f_sp, 1)
                split_hi(0, l, U + 12)
                level_exp(0)
                split_hi(0, l, U + 13)
                level_exp(1)
                split_hi(0, l, U + 14)
                level_exp(2)
                level_exp(3)
                split_hi(0, l, U + 15)
                level_exp(4)
                level_exp(5)
                split_hi(0, l, U + 16)
                normed_out(0, l, U + 12, HYBRID_PAIRS[6], fv, ACT.Copy)
                level_exp(6)
                level_exp(7)
                split_hi(0, l, U + 17)
                normed_out(0, l, U + 14, HYBRID_PAIRS[7], hv, ACT.Copy)
                split_hi(0, l, U + 18)
                assert NL == 8
                act.wait_ge(f_cumT, l + 1)
                act.activation(sst[:, 3, :], ps[:, G, 0:16], ACT.Copy).then_inc(f_cumS, 1)
                NA = X_HEADS * TB

                def fox_exp(i):
                    w = P * (i % 2 + 1)
                    act.wait_ge(a_max, l * NA + i + 1)
                    if i >= 4:
                        act.wait_ge(a_turn, l * NA + i - 3)
                    act.activation(fp[:, (i % 4) * 256:(i % 4) * 256 + w], fsc[:, (i % 4) * 256:(i % 4) * 256 + w], ACT.Exp,
                                   bias=sst[:, 1, i:i + 1], accum_out=sst[:, 2, i:i + 1]).then_inc(a_prob, 1)

                def fox_pT(i):
                    w = P * (i % 2 + 1)
                    act.wait_ge(a_turn, l * NA + i + 1)
                    if i >= 2:
                        act.wait_ge(a_out, l * NA + i - 1)
                    act.activation(fpT[:, (i % 2) * 256:(i % 2) * 256 + w], ps[:, G + i % 2, 0:w], ACT.Copy).then_inc(a_pT, 1)

                fox_exp(0)
                fox_exp(1)
                act.wait_ge(h_out, l + 1)
                o2 = ps[:, ACC + 2:ACC + 4, :].rearrange("p a c -> p (a c)")
                act.activation(tmp1, o2, ACT.Square).then_inc(h_sq, 1)
                act.activation(tmp2, o2, ACT.Copy)
                act.wait_ge(h_sum, l + 1)
                act.activation(hst[:, 1, :], hst[:, 0, :], ACT.Sqrt, scale=1.0 / H_D, bias=EPS).then_inc(h_rms, 1)
                for i in range(1, NA + 1):
                    if 1 < i < NA:
                        fox_exp(i)
                    fox_pT(i - 1)
                    if i == 13:
                        turn_out(turn_no(0, l, 2), (0, 1), (ACC, ACC + 2))
                turn_out(turn_no(0, l, 2), (2, 3))
                T3, T4 = turn_no(0, l, 3), turn_no(0, l, 4)
                split_hi(0, l, A_OUT + 3)
                split_hi(0, l, A_K)
                turn_out(T3, (0, 1))
                next_gain(0, norm_no(0, l, 2), T3)
                split_hi(0, l, A_K + 1)
                turn_out(T3, (2, 3))
                split_hi(0, l, A_K + 2)
                for i, dst in enumerate((zf, hq, hk, hv)):
                    split_hi(0, l, A_K + 2 * i + 3)
                    if i == 3:
                        turn_out(T4, (0, 1))
                    split_hi(0, l, A_K + 2 * i + 4)
                    chunk_out_(0, l, A_K + 2 * i, PAIRS[i % 3], dst, ACT.Copy)
                    if i == 0:
                        squares(xres, norm_no(0, l, 3), add_no(0, l, 1))
                turn_out(T4, (2, 3))
                next_gain(0, norm_no(0, l, 3), T4)
                split_hi(0, l, A_K + 11)
                split_hi(0, l, A_K + 12)
                row_out(row_no(0, l, 1))
                split_hi(0, l, A_K + 13)
                split_hi(0, l, A_K + 14)
                NC = C_HEADS * TB

                def cross_exp(i):
                    act.wait_ge(c_max, l * NC + i + 1)
                    if i >= 4:
                        act.wait_ge(c_turn, l * NC + i - 3)
                    act.activation(fp[:, (i % 4) * 256:(i % 4) * 256 + 256], ps[:, TR + i % 2, 0:256], ACT.Exp,
                                   bias=sst[:, 1, i:i + 1], accum_out=sst[:, 2, i:i + 1]).then_inc(c_prob, 1)

                def cross_pT(i):
                    act.wait_ge(c_turn, l * NC + i + 1)
                    if i >= 2:
                        act.wait_ge(c_out, l * NC + i - 1)
                    act.activation(fpT[:, (i % 2) * 256:(i % 2) * 256 + 256], ps[:, G + i % 2, 0:256], ACT.Copy).then_inc(c_pT, 1)

                for i in range(NC + 1):
                    if i < NC:
                        cross_exp(i)
                    if i == NC:
                        turn_out(turn_no(0, l, 5), (0, 1), (ACC, ACC + 2))
                    if i:
                        cross_pT(i - 1)
                turn_out(turn_no(0, l, 5), (2, 3))
                split_hi(0, l, A_O + 3)
                split_hi(0, l, A_FFN2)
                split_hi(0, l, A_FFN2 + 1)
                ffn(0, l, A_FFN2, 1, turn_no(0, l, 6), norm_no(0, l, 4), add_no(0, l, 2))
                assert count[0] == S_A, ("S_A", count[0])
            squares(xres, norm_no(0, DEPTH, 0), add_no(0, DEPTH, -1))
            next_gain(0, norm_no(0, DEPTH, 0), turn_no(0, DEPTH, 0))
            act.dma_start(cst[:, :], table_b).then_inc(loaded, 16)
            with act.Fori(0, DEPTH) as l:
                step, count = stepper(act, sstep, DEPTH * S_A + l * S_B)
                split_hi(1, l, B_FFN1)
                split_hi(1, l, B_FFN1 + 1)
                ffn(1, l, B_FFN1, 0, turn_no(1, l, 0), norm_no(1, l, 0), add_no(1, l, -1))
                U = B_IN
                split_hi(1, l, U)
                split_hi(1, l, U + 1)
                turn_out(turn_no(1, l, 1), (0, 1))
                split_hi(1, l, U + 2)
                turn_out(turn_no(1, l, 1), (2, 3))
                next_gain(1, norm_no(1, l, 1), turn_no(1, l, 1))
                split_hi(1, l, U + 3)
                squares(xres, norm_no(1, l, 1), add_no(1, l, 0))
                plan = [(qk_r, ACT.Copy), None, (vu, ACT.Copy), (v_r, ACT.Copy), (g_r, ACT.Silu)] + [
                    (gates[:, 1024 * i:1024 * i + 1024], ACT.Sigmoid) for i in range(6)]
                def branches():
                    act.wait_ge(s_out, l + 1)
                    act.activation(hT_hi[:, :, 0:2, :].rearrange("p t k c -> p k t c"),
                                   ps[:, 3, :].rearrange("p (k t c) -> p k t c", k=2, t=TB), ACT.Copy).then_inc(s_hi, 1)
                    act.wait_ge(p_diff, l + 1)
                    act.activation(pool_d[0:64, :], ps[0:64, 0:2, :].rearrange("p a c -> p (a c)"), ACT.Copy).then_inc(p_dT, 1)
                    for t in range(TB):
                        act.wait_ge(r_yT, l * TB + t + 1)
                        act.activation(hT_hi[:, t, 2:6, :].rearrange("p k c -> p (k c)"), ps[:, G + t, :], ACT.Copy).then_inc(r_hi, 1)
                        if t == 0:
                            act.wait_ge(p_out, l + 1)
                            for k in range(2):
                                act.activation(hT_hi[:, :, 6 + k, :], ps[:, 2, k * 256:(k + 1) * 256].rearrange("p (t c) -> p t c", t=TB),
                                               ACT.Copy, scale=pscale_l[:, k:k + 1]).then_inc(p_hi, 1)

                scores = ps[:, 0:3, :].rearrange("p a c -> p (a c)")
                o2 = ps[:, 0:2, :].rearrange("p a c -> p (a c)")
                for i, what in enumerate(plan):
                    for u in (2 * i + 3, 2 * i + 4):
                        if 3 < u < 25:
                            split_hi(1, l, U + u)
                        if u == 23:
                            branches()
                    if i == 0:
                        act.wait_ge(inv_ready, norm_no(1, l, 1) + 1)
                    if what:
                        normed_out(1, l, U + 2 * i, GATED_PAIRS[i], *what)
                    else:
                        row_out(row_no(1, l, 0))
                    if i == 3:
                        for t in range(TB):
                            act.wait_ge(r_turn, l * TB + t + 1)
                            act.activation(qk_rT.rearrange("p (k t c) -> p k t c", k=4, t=TB)[:, :, t, :],
                                           ps[:, TR + t, :].rearrange("p (k c) -> p k c", k=4), ACT.Copy).then_inc(r_kT, 1)
                    if i == 5:
                        act.wait_ge(s_score, 2 * l + 2)
                        step(act.activation(st1, scores, ACT.Abs))
                        step(act.activation(st1, st1, ACT.Exp, scale=-1.0))
                        act.activation(st1, st1, ACT.Ln, bias=1.0).then_inc(s_sp, 1)
                    if i == 8:
                        act.wait_ge(s_sum, l + 1)
                        act.activation(st2, st2, ACT.Exp).then_inc(s_exp, 1)
                    if i == 9:
                        act.wait_ge(r_out, l + 1)
                        act.activation(qk_sb, o2, ACT.Square).then_inc(r_sq, 1)
                        act.activation(v_r, o2, ACT.Copy)
                        act.wait_ge(r_sum, l + 1)
                        act.activation(hst[:, 1, :], hst[:, 0, :], ACT.Sqrt, scale=1.0 / P, bias=EPS).then_inc(r_rms, 1)
                split_hi(1, l, B_BR + 3)
                split_hi(1, l, B_OUT)
                split_hi(1, l, B_OUT + 1)
                turn_out(turn_no(1, l, 2), (0, 1))
                split_hi(1, l, B_OUT + 2)
                turn_out(turn_no(1, l, 2), (2, 3))
                split_hi(1, l, B_OUT + 3)
                split_hi(1, l, B_FFN2)
                split_hi(1, l, B_FFN2 + 1)
                ffn(1, l, B_FFN2, 1, turn_no(1, l, 3), norm_no(1, l, 2), add_no(1, l, 1))
                assert count[0] == S_B, ("S_B", count[0])
            squares(xres, norm_no(1, DEPTH, 0), add_no(1, DEPTH, -1))

        @block.tensor
        def _(pe):
            pe.sem_inc(unit_done, CREDIT)
            pe.wait_ge(ident_loaded, 16)

            def split_product(out, l_hi, l_lo, r_hi, r_lo, first, last):
                pe.matmul(out, l_hi, r_hi, start=first, stop=False, skip_group_check=True)
                pe.matmul(out, l_hi, r_lo, start=False, stop=False, skip_group_check=True)
                return pe.matmul(out, l_lo, r_hi, start=False, stop=last, skip_group_check=True)

            def wait_weights(b, l, off, c=0):
                pe.wait_ge(lo_ready, unit(b, l, off, c) + 1 + CREDIT)

            def turn_piece(b, T, i, banks=(TR, TR + 1)):
                h, t = divmod(i, 2)
                pe.wait_ge(xn_ready, PIECES * xn_no(b, T) + i + 1)
                if h:
                    pe.wait_ge(turn_lo, PIECES * T + i - 1)
                for k in range(4):
                    mm = pe.transpose(ps[:, banks[t], k * P:(k + 1) * P], piece(xn, i)[:, k * P:(k + 1) * P], ident[:, :])
                mm.then_inc(turned, 1)

            def wait_piece(T, k0, t):
                pe.wait_ge(turn_lo, PIECES * T + k0 // 2 + t + 1)

            def tokens_unit(b, l, off, c, k0, banks, first, last, ready=None, T=None, then=()):
                s = off % RING
                wait_weights(b, l, off, c)
                for t in range(TB):
                    if ready is not None:
                        pe.wait_ge(prod_ready, ready + t + 1)
                    if T is not None:
                        wait_piece(T, k0, t)
                    for k in range(4):
                        mm = split_product(ps[:, banks[t], :], hT_hi[:, t, k0 + k, :], hT_lo[:, t, k0 + k, :],
                                           whi[:, s, k, :], wlo[:, s, k, :], first and k == 0, last and k == 3)
                    if t == TB - 1:
                        mm.then_inc(unit_done, 1)
                    if then and then[t]:
                        then[t]()

            def features_unit(b, l, off, k0, bank, first, last, T=None):
                s = off % RING
                wait_weights(b, l, off)
                if T is not None:
                    wait_piece(T, k0, TB - 1)
                for n in range(4):
                    cols = slice(n * P, (n + 1) * P)
                    for k in range(4):
                        mm = split_product(ps[:, bank + n // 2, n % 2 * SEQ:(n % 2 + 1) * SEQ],
                                           whi[:, s, k, cols], wlo[:, s, k, cols], hT_hi[:, :, k0 + k, :], hT_lo[:, :, k0 + k, :],
                                           first and k == 0 and n % 2 == 0, last and k == 3)
                mm.then_inc(unit_done, 1)

            def tall_unit(b, l, off, lhs, bank, first, last, c=0, T=None, k0=0, signal=None, then={}):
                s = off % RING
                wait_weights(b, l, off, c)
                for i in range(PIECES):
                    half, t = divmod(i, 2)
                    if T is not None and half == 0:
                        wait_piece(T, k0, t)
                    for k in range(2):
                        hi, lo = lhs(k)
                        mm = split_product(ps[:, bank + 2 * t + half, :], hi[:, t], lo[:, t],
                                           whi[:, s, 2 * k + half, :], wlo[:, s, 2 * k + half, :], first and k == 0, last and k == 1)
                    if i == PIECES - 1:
                        mm.then_inc(unit_done, 1)
                    elif signal is not None:
                        mm.then_inc(signal, 1)
                    if i in then:
                        then[i]()

            def from_hT(k0):
                return lambda k: (hT_hi[:, :, k0 + k, :], hT_lo[:, :, k0 + k, :])

            def rest_of(b, T):
                return tuple((lambda i=i: turn_piece(b, T, i)) for i in (2, 3))

            def turn_ahead(b, T):
                return {} if T is None else {2: lambda: turn_piece(b, T, 0), 3: lambda: turn_piece(b, T, 1)}

            def output(b, l, off, T, T_next=None, T_mid=None):
                tall_unit(b, l, off, from_hT(0), ACC, True, False, 0, T, 0,
                          then={1: lambda: (turn_piece(b, T, 2), turn_piece(b, T, 3))})
                tall_unit(b, l, off + 1, from_hT(2), ACC, False, False)
                wait_piece(T, 4, 1)
                if T_mid is not None:
                    turn_piece(b, T_mid, 0)
                    turn_piece(b, T_mid, 1)
                tall_unit(b, l, off + 2, from_hT(4), ACC, False, False)
                tall_unit(b, l, off + 3, from_hT(6), ACC, False, True, signal=acc_done, then=turn_ahead(b, T_next))
                if T_mid is not None:
                    turn_piece(b, T_mid, 2)
                    turn_piece(b, T_mid, 3)

            def row(r, ones):
                pe.wait_ge(row_diag, r + 1)
                pe.matmul(ps[:, TR, 0:SEQ], ones, norm_diag, start=True, stop=True).then_inc(row_made, 1)

            def ffn(b, l, off, e, T, T_next=None):
                f = ffn_no(b, l, e)

                def half_up(off, c, step, k):
                    if isinstance(step, int) and step == 0:
                        tokens_unit(b, l, off + k, c, 4 * k, (ACC, ACC + 2), k == 0, k == 1, None, T, rest_of(b, T) if k == 0 else ())
                        return
                    ready = 2 * FF_STEPS * f + 2 * (step - 1) if k == 0 and not (isinstance(step, int) and step == 1) else None
                    tokens_unit(b, l, off + k, c, 4 * k, (G, G + 1), k == 0, k == 1, ready)

                def turn_act(step):
                    pe.wait_ge(prod_ready, 2 * FF_STEPS * f + 2 * step + 2)
                    for k in range(2):
                        for t in range(TB):
                            mm = pe.transpose(ps[:, TR, (2 * k + t) * P:(2 * k + t + 1) * P], prod[:, t, k * P:(k + 1) * P], ident[:, :])
                    mm.then_inc(act_turned, 1)

                def down(off, c, step, first, last, then=None):
                    lhs = from_hT(4) if last else lambda k: (aT_hi[:, k], aT_lo[:, k])
                    pe.wait_ge(act_lo, FF_STEPS * f + step + 1)
                    tall_unit(b, l, off, lhs, ACC, first, last, c, signal=acc_done if last else None,
                              then=then or (turn_ahead(b, T_next) if last else {}))

                def step_(off, c, step, first, then=None):
                    half_up(off, c, step, 0)
                    turn_act(step - 1)
                    half_up(off, c, step, 1)
                    down(off + 2, c, step - 1, first, False, then)

                half_up(off, 0, 0, 0)
                half_up(off, 0, 0, 1)
                step_(off + 2, 0, 1, True)
                with pe.Fori(0, FF_STEPS - 3) as c:
                    step_(off + 5, c, c + 2, False)
                step_(off + FFN_UNITS - 4, 0, FF_STEPS - 1, False, {2: lambda: turn_act(FF_STEPS - 1)})
                down(off + FFN_UNITS - 1, 0, FF_STEPS - 1, False, True)

            def chunk(b, l, off, pair, features, before=None, T=None, then=(), between=None):
                if before is not None:
                    wait_taken(pe, b, l, before)
                for k in range(2):
                    if features:
                        features_unit(b, l, off + k, 4 * k, pair, k == 0, k == 1, T)
                    else:
                        tokens_unit(b, l, off + k, 0, 4 * k, (pair, pair + 1), k == 0, k == 1, None, T, then[2 * k:2 * k + 2])
                    if k == 0 and between:
                        between()

            with pe.Fori(0, DEPTH) as l:
                T0, T1, T2, T3, T4, T5, T6 = (turn_no(0, l, j) for j in range(7))
                turn_piece(0, T0, 0)
                turn_piece(0, T0, 1)
                ffn(0, l, A_FFN1, 0, T0, T1)

                def turn_forget():
                    pe.wait_ge(f_tm, l + 1)
                    for t in range(TB):
                        mm = pe.transpose(ps[0:8, TR + 1, t * P:(t + 1) * P], flog[:, t, :], ident[:, :])
                    mm.then_inc(f_turn, 1)

                NG = len(LEVELS) + 2

                def level_products(n):
                    bank = ACC + 2 * (n % 2)
                    if n < 2:
                        wait_taken(pe, 0, l, n + 1)
                    else:
                        pe.wait_ge(lev_kept, l * NG + n - 1)
                    if n == 0:
                        pe.wait_ge(h_key, H_HEADS * (l + 1))
                        pe.wait_ge(h_query, l + 1)
                        a, c = hk, hq
                    else:
                        pe.wait_ge(lev_ready, l * (NG - 1) + n)
                        a = c = lev2[:, (n - 1) % 2 * 1024:(n - 1) % 2 * 1024 + 1024]
                    if n < NG - 1:
                        for g in range(H_HEADS * TB):
                            mm = pe.matmul(ps[:, bank + g // 4, g % 4 * P:(g % 4 + 1) * P], a[:, g * P:(g + 1) * P],
                                           c[:, g * P:(g + 1) * P], start=True, stop=True)
                    else:
                        for h in range(H_HEADS):
                            mm = pe.matmul(ps[:, bank, h * P:(h + 1) * P], a[:, 2 * h * P:(2 * h + 1) * P],
                                           c[:, (2 * h + 1) * P:(2 * h + 2) * P], start=True, stop=True)
                    mm.then_inc(lev_prod, 1)

                def levels(*ns):
                    return tuple(n if n is None else (lambda n=n: level_products(n)) for n in ns)

                between = {1: lambda: row(row_no(0, l, 0), con("ones", 0, P)), 4: turn_forget, 5: lambda: level_products(0)}
                then = {0: rest_of(0, T1), 6: levels(2, 3, 4, 5), 7: levels(6, 7, 8, None)}
                before = {4: 0, 6: 3, 7: 4}
                for i, features in enumerate((False, True, True, None, True, True, False, False)):
                    off = A_IN + 2 * i
                    if features is not None:
                        if i == 1:
                            pe.wait_ge(loaded, N_LOADS * 16)
                        if i == 5:
                            pe.wait_ge(f_logit, l + 1)
                        chunk(0, l, off, HYBRID_PAIRS[i], features, before.get(i), T1 if i == 0 else None, then.get(i, ()), between.get(i))
                        if i == 5:
                            level_products(1)
                        continue
                    pe.wait_ge(row_ready, row_no(0, l, 0) + 1)
                    for k in range(2):
                        s = (off + k) % RING
                        wait_weights(0, l, off + k)
                        for t in range(TB):
                            for kk in range(4):
                                mm = split_product(ps[:, TR, 8 * t:8 * t + 8], hT_hi[:, t, 4 * k + kk, :], hT_lo[:, t, 4 * k + kk, :],
                                                   whi[:, s, kk, 0:8], wlo[:, s, kk, 0:8], k == 0 and kk == 0 and t == 0, k == 1 and kk == 3)
                        mm.then_inc(unit_done, 1)
                wait_taken(pe, 0, l, 5)
                pe.wait_ge(f_cum, l + 1)
                for t in range(TB):
                    mm = pe.matmul(ps[:, G, 8 * t:8 * t + 8], fcs_c[:, t * P:(t + 1) * P], ident[0:8, 0:8], start=True, stop=True)
                mm.then_inc(f_cumT, 1)
                NA = X_HEADS * TB

                def fox_score(i):
                    h, t = divmod(i, 2)
                    w, r, j = P * (t + 1), h % 2 * 64, h // 2
                    if i >= 2:
                        pe.wait_ge(a_masked, l * NA + i - 1)
                    o = ps[:, TR + i % 2, 0:w]
                    pe.matmul(o, fq[r:r + 64, j * SEQ + t * P:j * SEQ + (t + 1) * P], fk[r:r + 64, j * SEQ:j * SEQ + w], start=True, stop=False)
                    pe.matmul(o, con("sel", h * P, P, 8), fcs_n[:, 0:w], start=False, stop=True).then_inc(a_score, 1)

                def fox_turn(i):
                    pe.wait_ge(a_prob, l * NA + i + 1)
                    if i >= 2:
                        pe.wait_ge(a_pT, l * NA + i - 1)
                    for k in range(i % 2 + 1):
                        mm = pe.transpose(ps[:, G + i % 2, k * P:(k + 1) * P], fp[:, i % 4 * 256 + k * P:i % 4 * 256 + (k + 1) * P], ident[:, :])
                    mm.then_inc(a_turn, 1)

                def fox_out(i):
                    h, t = divmod(i, 2)
                    pe.wait_ge(a_pT, l * NA + i + 1)
                    for k in range(t + 1):
                        mm = pe.matmul(ps[:, ACC + 2 * t + 1, h * 64:(h + 1) * 64], fpT[:, i % 2 * 256 + k * P:i % 2 * 256 + (k + 1) * P],
                                       fv[:, k * 512 + h * 64:k * 512 + (h + 1) * 64], start=(k == 0), stop=(k == t))
                    mm.then_inc(a_out, 1)

                wait_taken(pe, 0, l, 4)
                wait_taken(pe, 0, l, 6)
                fox_score(0)
                fox_score(1)
                pe.wait_ge(lev_kept, l * NG + NG)
                wait_taken(pe, 0, l, 6)
                for h in range(H_HEADS):
                    v = [hv[:, t * 512 + h * P:t * 512 + (h + 1) * P] for t in range(TB)]
                    o = [ps[:, ACC + 2 + t, h * P:(h + 1) * P] for t in range(TB)]
                    pe.matmul(o[0], att[:, 2 * h * P:(2 * h + 1) * P], v[0], start=True, stop=True)
                    pe.matmul(o[1], attx[:, h * P:(h + 1) * P], v[0], start=True, stop=False)
                    mm = pe.matmul(o[1], att[:, (2 * h + 1) * P:(2 * h + 2) * P], v[1], start=False, stop=True)
                mm.then_inc(h_out, 1)
                pe.wait_ge(f_cumS, l + 1)
                for i in range(2, NA + 3):
                    if i == 14:
                        for k in range(2):
                            turn_piece(0, T2, k, (ACC, ACC + 2))
                    if i < NA:
                        fox_score(i)
                    if 2 <= i < NA + 2:
                        fox_turn(i - 2)
                    if i >= 3:
                        fox_out(i - 3)
                output(0, l, A_OUT, T2, T_mid=T3)
                for i in range(6):
                    if i < 4:
                        chunk(0, l, A_K + 2 * i, PAIRS[i % 3], i < 2, 7 + i - 3 if i >= 3 else None, T3 if i == 0 else None,
                              between=(lambda: (turn_piece(0, T4, 0), turn_piece(0, T4, 1))) if i == 3 else None)
                        continue
                    if i == 4:
                        turn_piece(0, T4, 2)
                        turn_piece(0, T4, 3)
                    chunk(0, l, A_K + 2 * i, PAIRS[i % 3], True, 7 + i - 3, T4 if i == 4 else None)
                    if i == 4:
                        row(row_no(0, l, 1), con("ones", 0, P))
                wait_taken(pe, 0, l, 10)
                wait_taken(pe, 0, l, 12)
                NC = C_HEADS * TB

                def cross_score(i):
                    h, t = divmod(i, 2)
                    if i >= 2:
                        pe.wait_ge(c_prob, l * NC + i - 1)
                    q, k_ = (hg, fq)[h // 2], (zf, hq)[h // 2]
                    for k in range(2):
                        at = (2 * (h % 2) + k) * SEQ
                        mm = pe.matmul(ps[:, TR + i % 2, 0:SEQ], q[:, at + t * P:at + (t + 1) * P], k_[:, at:at + SEQ], start=(k == 0), stop=(k == 1))
                    mm.then_inc(c_score, 1)

                def cross_turn(i):
                    pe.wait_ge(c_prob, l * NC + i + 1)
                    if i >= 2:
                        pe.wait_ge(c_pT, l * NC + i - 1)
                    for k in range(2):
                        mm = pe.transpose(ps[:, G + i % 2, k * P:(k + 1) * P], fp[:, i % 4 * 256 + k * P:i % 4 * 256 + (k + 1) * P], ident[:, :])
                    mm.then_inc(c_turn, 1)

                def cross_out(i):
                    h, t = divmod(i, 2)
                    v = (hk, hv)[h // 2]
                    pe.wait_ge(c_pT, l * NC + i + 1)
                    for k in range(2):
                        at = k * 512 + h % 2 * C_D
                        mm = pe.matmul(ps[:, ACC + 2 * t + h // 2, h % 2 * C_D:(h % 2 + 1) * C_D],
                                       fpT[:, i % 2 * 256 + k * P:i % 2 * 256 + (k + 1) * P], v[:, at:at + C_D], start=(k == 0), stop=(k == 1))
                    mm.then_inc(c_out, 1)

                for i in range(NC + 3):
                    if i == NC:
                        for k in range(2):
                            turn_piece(0, T5, k, (ACC, ACC + 2))
                    if i < NC:
                        cross_score(i)
                    if 2 <= i < NC + 2:
                        cross_turn(i - 2)
                    if i >= 3:
                        cross_out(i - 3)
                output(0, l, A_O, T5, T_next=T6)
                ffn(0, l, A_FFN2, 1, T6)

            with pe.Fori(0, DEPTH) as l:
                T0, T1, T2, T3 = (turn_no(1, l, j) for j in range(4))
                turn_piece(1, T0, 0)
                turn_piece(1, T0, 1)
                ffn(1, l, B_FFN1, 0, T0, T1)
                def rotated_turn():
                    for t in range(TB):
                        pe.wait_ge(r_rot, l * TB + t + 1)
                        for k in range(4):
                            mm = pe.transpose(ps[:, TR + t, k * P:(k + 1) * P], qk_rot[:, t * 512 + k * P:t * 512 + (k + 1) * P], ident[:, :])
                        mm.then_inc(r_turn, 1)

                def key_scores(qk, done):
                    for n, h in enumerate(HEAD_ORDER):
                        r, j = h % 2 * 64, h // 2
                        if n == 2:
                            pe.wait_ge(done, 2 * l + 1)
                        q = qk[r:r + 64, j * SEQ:(j + 1) * SEQ]
                        k = qk[r:r + 64, (2 + j) * SEQ:(3 + j) * SEQ]
                        pe.matmul(ps[:, n // 2, n % 2 * SEQ:(n % 2 + 1) * SEQ], k[:, 0:P], q, start=True, stop=True)
                        mm = pe.matmul(ps[:, 2, n * P:(n + 1) * P], k[:, P:SEQ], q[:, P:SEQ], start=True, stop=True)
                        if n % 2:
                            mm.then_inc(done, 1)

                def stick_scores():
                    wait_taken(pe, 1, l, 4)
                    wait_taken(pe, 1, l, 1)
                    key_scores(qk_sb, s_score)

                def retention_scores():
                    pe.wait_ge(r_kT, TB * (l + 1))
                    pe.wait_ge(s_fail, l + 1)
                    key_scores(qk_rT, r_score)

                def stick_after():
                    pe.wait_ge(r_dec, l + 1)
                    later, all_ = con("neg_later"), con("neg_ones")
                    for n in range(2):
                        pe.matmul(ps[:, n, :], later, st3[:, n * 512:(n + 1) * 512], start=True, stop=False, skip_group_check=True)
                        pe.matmul(ps[:, n, :].rearrange("p (h b c) -> p h b c", h=2, b=2)[:, :, 1, :], all_,
                                  st3[:, 1024 + n * 256:1024 + (n + 1) * 256], start=False, stop=True, skip_group_check=True)
                    pe.matmul(ps[:, 2, :], later, st3[:, 1024:1536], start=True, stop=True).then_inc(s_after, 1)

                def retention_out():
                    pe.wait_ge(s_sum, l + 1)
                    for n, h in enumerate(HEAD_ORDER):
                        v = [v_r[:, t * 512 + h * P:t * 512 + (h + 1) * P] for t in range(TB)]
                        o = [ps[:, t, h * P:(h + 1) * P] for t in range(TB)]
                        pe.matmul(o[0], sc_r[:, 2 * n * P:(2 * n + 1) * P], v[0], start=True, stop=True)
                        pe.matmul(o[1], sc_r[:, (2 * n + 1) * P:(2 * n + 2) * P], v[0], start=True, stop=False)
                        mm = pe.matmul(o[1], sc_r[:, 1024 + n * P:1024 + (n + 1) * P], v[1], start=False, stop=True)
                    mm.then_inc(r_out, 1)

                def stick_out():
                    pe.wait_ge(s_w, l + 1)
                    for n, h in enumerate(HEAD_ORDER):
                        r = h % 2 * 64
                        v = [vu[:, t * 512 + h * 64:t * 512 + (h + 1) * 64] for t in range(TB)]
                        o = ps[r:r + 64, 3, h // 2 * SEQ:(h // 2 + 1) * SEQ]
                        pe.matmul(o[:, 0:P], v[0], st2[:, 2 * n * P:(2 * n + 1) * P], start=True, stop=True)
                        pe.matmul(o[:, P:SEQ], v[0], st2[:, (2 * n + 1) * P:(2 * n + 2) * P], start=True, stop=False)
                        mm = pe.matmul(o[:, P:SEQ], v[1], st2[:, 1024 + n * P:1024 + (n + 1) * P], start=False, stop=True)
                    mm.then_inc(s_out, 1)

                def pool_means():
                    pe.wait_ge(r_rms, l + 1)
                    for g in range(4):
                        u = [vu[:, t * 512 + 256 + g * 64:t * 512 + 256 + (g + 1) * 64] for t in range(TB)]
                        o = ps[0:64, g // 2, g % 2 * SEQ:(g % 2 + 1) * SEQ]
                        m = [con("pool", (3 * g + n) * P, P) for n in range(3)]
                        pe.matmul(o[:, 0:P], u[0], m[0], start=True, stop=True)
                        pe.matmul(o[:, P:SEQ], u[0], m[1], start=True, stop=False)
                        mm = pe.matmul(o[:, P:SEQ], u[1], m[2], start=False, stop=True)
                    mm.then_inc(p_diff, 1)

                after = {3: rotated_turn, 5: stick_scores, 7: retention_scores, 8: stick_after, 9: retention_out}
                before = {3: 0, 4: 1, 5: 3, 6: None, 7: 5, 8: 6, 9: 7, 10: 8}
                for i in range(11):
                    if i == 1:
                        pe.wait_ge(loaded, N_LOADS * 16 + 16)
                    if i == 6:
                        pe.wait_ge(r_kT, TB * (l + 1))
                    chunk(1, l, B_IN + 2 * i, GATED_PAIRS[i], i == 1, before.get(i), T1 if i == 0 else None,
                          {0: rest_of(1, T1), 10: (None, None, pool_means, None)}.get(i, ()),
                          {1: lambda: row(row_no(1, l, 0), con("neg_ones")), 10: stick_out}.get(i))
                    if i in after:
                        after[i]()
                def pool_groups():
                    for g in range(4):
                        r = g % 2 * 64
                        mm = pe.matmul(ps[r:r + 64, 2, g // 2 * SEQ:(g // 2 + 1) * SEQ], wpool_l[:, g, :], pool_d[0:64, g * SEQ:(g + 1) * SEQ],
                                       start=True, stop=True)
                    mm.then_inc(p_out, 1)

                wait_taken(pe, 1, l, 9)
                for t in range(TB):
                    pe.wait_ge(r_y, l + 1)
                    if t == 0:
                        pe.wait_ge(p_dT, l + 1)
                        pe.wait_ge(p_wl, l + 1)
                    for k in range(4):
                        mm = pe.transpose(ps[:, G + t, k * P:(k + 1) * P], v_r[:, t * 512 + k * P:t * 512 + (k + 1) * P], ident[:, :])
                    mm.then_inc(r_yT, 1)
                    if t == 0:
                        pool_groups()
                pe.wait_ge(s_lo, l + 1)
                pe.wait_ge(p_lo, l + 1)
                tall_unit(1, l, B_BR, from_hT(0), 0, True, True)
                pe.wait_ge(r_lo, TB * (l + 1))
                wait_taken(pe, 1, l, 10)
                tall_unit(1, l, B_BR + 1, from_hT(6), 4, True, True)
                pe.wait_ge(br_used, 2 * l + 1)
                tall_unit(1, l, B_BR + 2, from_hT(2), 0, True, False)
                tall_unit(1, l, B_BR + 3, from_hT(4), 0, False, True, signal=br_piece, then=turn_ahead(1, T2))
                output(1, l, B_OUT, T2, T_next=T3)
                ffn(1, l, B_FFN2, 1, T3)

        @block.vector
        def _(dve):
            def absolute(o, z):
                return dve.scalar_tensor_tensor(out=o, in0=z, scalar=-1.0, in1=z, op0=ALU.mult, op1=ALU.max)

            def inverse(n, which=0):
                dve.wait_ge(sq_done, n + 1)
                dve.reciprocal(stat[:, which, 2, :], stat[:, which, 1, :]).then_inc(inv_ready, 1)
                dve.wait_ge(inv_ready, n + 1)

            def gained(A, n, i):
                if i == 0:
                    dve.wait_ge(gain_loaded, 16 * n + 16)
                dve.wait_ge(x_ready, PIECES * A + i + 1)
                dve.tensor_tensor(piece(xn, i), piece(xres, i), gain[:, i // 2 * 512:(i // 2 + 1) * 512], ALU.mult).then_inc(xn_ready, 1)

            def turn_out(T, pieces, banks=(TR, TR + 1)):
                for i in pieces:
                    h, t = divmod(i, 2)
                    dve.wait_ge(turn_hi, PIECES * T + i + 1)
                    at = lambda m: m[:, t, 4 * h:4 * h + 4, :].rearrange("p k c -> p (k c)")
                    dve.tensor_tensor(at(hT_lo), ps[:, banks[t], :], at(hT_hi).bitcast(F32), ALU.subtract).then_inc(turn_lo, 1)

            def add(b, l, j, i, off, factor):
                h, t = divmod(i, 2)
                if i < PIECES - 1:
                    dve.wait_ge(acc_done, (PIECES - 1) * acc_no(b, l, j) + i + 1)
                else:
                    wait_unit(dve, b, l, off)
                dve.scalar_tensor_tensor(out=piece(xres, i), in0=ps[:, ACC + 2 * t + h, :], scalar=factor, in1=piece(xres, i),
                                         op0=ALU.mult, op1=ALU.add).then_inc(x_ready, 1)

            def add_and_norm(b, l, j, off, factor, n, T=None):
                for i in range(PIECES):
                    if T is not None and i == PIECES - 1:
                        turn_out(T, (0,))
                    add(b, l, j, i, off, factor)
                    if T is not None and i == PIECES - 1:
                        turn_out(T, (1,))
                    gained(add_no(b, l, j), n, i)

            def rms_diag(sign):
                for t in range(TB):
                    last = dve.tensor_scalar(norm_diag[:, t * P:(t + 1) * P], ident[:, :], stat[:, 0, 2, t:t + 1], sign, ALU.mult, ALU.mult)
                last.then_inc(row_diag, 1)

            def scaled_out(b, l, u, pair, r, parts):
                wait_unit(dve, b, l, u + 1)
                dve.wait_ge(row_ready, r + 1)
                src = ps[:, pair:pair + 2, :].rearrange("p a (f c) -> p (a f) c", c=SEQ)
                at = 0
                for dst, scale in parts:
                    d = dst.rearrange("p (f c) -> p f c", c=SEQ)
                    F = d.shape[1]
                    last = dve.scalar_tensor_tensor(out=d, in0=src[:, at:at + F, :], scalar=scale,
                                                    in1=rms_row.unsqueeze(1).broadcast_to([P, F, SEQ]), op0=ALU.mult, op1=ALU.mult)
                    at += F
                last.then_inc(feat_out, 1)

            def ffn(b, l, off, e, T, n):
                f = ffn_no(b, l, e)

                def product(stp, banks=(G, G + 1)):
                    for t in range(TB):
                        dve.wait_ge(silu_done, 2 * FF_STEPS * f + 2 * stp + t + 1)
                        dve.scalar_tensor_tensor(out=prod[:, t, :], in0=ps[:, banks[t], 256:512], scalar=stat[:, 0, 2, t:t + 1],
                                                 in1=silu_g[:, t, :], op0=ALU.mult, op1=ALU.mult).then_inc(prod_ready, 1)

                def rest(stp, hi=aT_hi, lo=aT_lo):
                    dve.wait_ge(act_hi, FF_STEPS * f + stp + 1)
                    dve.tensor_tensor(lo[:, :, :, :], ps[:, TR, :].rearrange("p (k t c) -> p k t c", k=2, t=TB),
                                      hi[:, :, :, :].bitcast(F32), ALU.subtract).then_inc(act_lo, 1)

                turn_out(T, range(PIECES) if e == 0 else (2, 3))
                inverse(n)
                product(0, (ACC, ACC + 2))
                with dve.Fori(0, FF_STEPS - 1) as c:
                    rest(c)
                    product(c + 1)
                rest(FF_STEPS - 1, last_aT(hT_hi), last_aT(hT_lo))
                add_and_norm(b, l, 0 if e == 0 else ADDS[b] - 1, off + FFN_UNITS - 1, 0.5, n + 1, T + 1 if e == 0 else None)

            def head_norm(squares, o, summed, rooted):
                dve.tensor_reduce(hst[:, 0, :], squares.rearrange("p (g c) -> p g c", g=8), AX, ALU.add).then_inc(summed, 1)
                dve.wait_ge(*rooted)
                step(dve.reciprocal(hst[:, 2, :], hst[:, 1, :]))
                o3 = o.rearrange("p (g c) -> p g c", g=8)
                step(dve.tensor_tensor(o3, o3, hst[:, 2, :].unsqueeze(2).broadcast_to([P, 8, P]), ALU.mult))

            dve.wait_ge(x_loaded, 16)
            dve.sem_inc(x_ready, PIECES)
            for i in range(PIECES):
                gained(0, 0, i)
            with dve.Fori(0, DEPTH) as l:
                step, count = stepper(dve, vstep, l * V_A)
                ffn(0, l, A_FFN1, 0, turn_no(0, l, 0), norm_no(0, l, 0))
                turn_out(turn_no(0, l, 1), (2, 3))
                inverse(norm_no(0, l, 1))
                rms_diag(1.0)

                def projected(i, dst, scale=1.0):
                    scaled_out(0, l, A_IN + 2 * i, HYBRID_PAIRS[i], row_no(0, l, 0), [(dst, scale)])

                dve.wait_ge(loaded, N_LOADS * 16)
                dve.memset(ln_lb[:, 0, :], MASKED)
                dve.memset(ln_1mlb[:, 0, :], 0.0)
                step(dve.tensor_tensor(lbw[:, 0, :], lbt[:, 1, :], lbt[:, 0, :], ALU.subtract))
                absolute(lbw[:, 1, :], lbw[:, 0, :]).then_inc(lb_abs, 1)
                inverse(norm_no(0, l, 2), 1)
                projected(1, zf)
                dve.wait_ge(feat_out, taken_no(0, l, 1, "V"))
                absolute(tmp1, zf).then_inc(h_abs, 1)
                dve.wait_ge(lb_sp, l + 1)
                dve.scalar_tensor_tensor(out=ln_lb[:, 1, :], in0=lbw[:, 0, :], scalar=0.0, in1=lbw[:, 1, :], op0=ALU.min, op1=ALU.subtract)
                step(dve.scalar_tensor_tensor(out=lbw[:, 2, :], in0=lbw[:, 0, :], scalar=0.0, in1=lbw[:, 1, :], op0=ALU.max, op1=ALU.add))
                step(dve.tensor_scalar(ln_1mlb[:, 1, :], lbw[:, 2, :], -1.0, None, ALU.mult))
                dve.tensor_copy(lb_l[:, 0, :], ln_lb[:, bass.ds(l, 1), :].rearrange("p a h -> p (a h)"))
                dve.tensor_copy(lb_l[:, 1, :], ln_1mlb[:, bass.ds(l, 1), :].rearrange("p a h -> p (a h)"))
                step(dve.tensor_copy(onorm_l[:, :], onorm[:, bass.ds(l, 1), :].rearrange("p a h -> p (a h)")))

                dve.wait_ge(h_sp, l + 1)
                dve.scalar_tensor_tensor(out=hk, in0=zf, scalar=0.0, in1=tmp1, op0=ALU.max, op1=ALU.add)
                step(dve.scalar_tensor_tensor(out=tmp2, in0=zf, scalar=0.0, in1=tmp1, op0=ALU.min, op1=ALU.subtract))

                def head(m, h):
                    return m[:, h * SEQ:(h + 1) * SEQ]

                for h in range(H_HEADS):
                    last = dve.tensor_scalar(head(tmp1, h), head(tmp2, h), lb_l[:, 1, h:h + 1], None, ALU.add)
                step(last)
                for h in range(H_HEADS):
                    dve.tensor_scalar(head(zf, h), head(tmp1, h), lb_l[:, 0, h:h + 1], None, ALU.max)
                    last = dve.tensor_scalar(head(lev2, h), head(tmp1, h), lb_l[:, 0, h:h + 1], None, ALU.subtract)
                step(last)
                absolute(lev2[:, 0:1024], lev2[:, 0:1024]).then_inc(h_gate, 1)
                projected(2, hq)
                dve.memset(att, 0.0)
                dve.wait_ge(h_sp2, l + 1)
                step(dve.tensor_tensor(zf, zf, lev2[:, 0:1024], ALU.add))
                for h in range(H_HEADS):
                    last = dve.tensor_tensor_scan(head(cum, h), con("reset"), head(zf, h), 0.0, ALU.mult, ALU.add)
                step(last)
                NL = len(LEVELS) + 1
                NG = NL + 1

                def level(n, m_):
                    m = LEVELS[n] if n < NL - 1 else P
                    return m, m_.rearrange("p (b c) -> p b c", c=2 * m)

                def lev(n):
                    return lev2[:, n % 2 * 1024:n % 2 * 1024 + 1024]

                def diff(n):
                    m, e = level(n, lev(n))
                    g = level(n, cum)[1]
                    B = 1024 // (2 * m)
                    end = g[:, :, m - 1:m].broadcast_to([P, B, m])
                    dve.tensor_tensor(e[:, :, 0:m], end, g[:, :, 0:m], ALU.subtract)
                    if n < NL - 1:
                        last = dve.tensor_tensor(e[:, :, m:2 * m], g[:, :, m:2 * m], end, ALU.subtract)
                    else:
                        last = dve.tensor_copy(e[:, :, m:2 * m], g[:, :, m:2 * m])
                    last.then_inc(lev_diff, 1)

                def decayed(n):
                    m, e = level(n, lev(n))
                    dve.wait_ge(lev_exp, l * NL + n + 1)
                    dve.tensor_tensor(e[:, :, 0:m], e[:, :, 0:m], level(n, hk)[1][:, :, 0:m], ALU.mult)
                    dve.tensor_tensor(e[:, :, m:2 * m], e[:, :, m:2 * m], level(n, hq)[1][:, :, m:2 * m], ALU.mult).then_inc(lev_ready, 1)

                def keep(n):
                    bank = ACC + 2 * (n % 2)
                    mask = ident[:, :] if n == 0 else con("level", (n - 1) * P, P)
                    dve.copy_predicated(att.rearrange("p (g c) -> p g c", c=P),
                                        mask.bitcast(I32).unsqueeze(1).broadcast_to([P, 8, P]),
                                        ps[:, bank:bank + 2, :].rearrange("p a (g c) -> p (a g) c", c=P)).then_inc(lev_kept, 1)

                diff(0)
                dve.wait_ge(f_logit, l + 1)
                absolute(fcs_t, fcs_f).then_inc(f_abs, 1)
                projected(4, fq, X_D ** -0.5)
                dve.wait_ge(f_sp, l + 1)
                step(dve.scalar_tensor_tensor(out=fcs_f, in0=fcs_f, scalar=0.0, in1=fcs_t, op0=ALU.min, op1=ALU.subtract))
                step(dve.tensor_tensor_scan(fcs_c, con("ones", rows=8), fcs_f, 0.0, ALU.mult, ALU.add))
                dve.tensor_scalar(fcs_n, fcs_c, -1.0, None, ALU.mult).then_inc(f_cum, 1)
                dve.wait_ge(h_key, H_HEADS * (l + 1))
                for n in range(NL):
                    decayed(n)
                    if n + 1 < NL:
                        dve.wait_ge(lev_prod, l * NG + n + 1)
                        if n:
                            dve.wait_ge(lev_kept, l * NG + n)
                        diff(n + 1)
                        keep(n)
                    if n == 1:
                        projected(5, fk)
                dve.wait_ge(lev_prod, l * NG + NG)
                dve.wait_ge(lev_kept, l * NG + NL - 1)
                dve.tensor_copy(attx, ps[:, ACC + 2 * ((NG - 1) % 2), :]).then_inc(lev_kept, 1)
                keep(NL - 1)
                dve.wait_ge(f_cumS, l + 1)
                NA = X_HEADS * TB
                for i in range(NA):
                    h, t = divmod(i, 2)
                    w, at = P * (t + 1), i % 4 * 256
                    dve.wait_ge(a_score, l * NA + i + 1)
                    if i >= 4:
                        dve.wait_ge(a_prob, l * NA + i - 3)
                    dve.scalar_tensor_tensor(out=fsc[:, at:at + w], in0=ps[:, TR + i % 2, 0:w], scalar=sst[:, 3, 8 * t + h:8 * t + h + 1],
                                             in1=con("zeros", P - t * P, w), op0=ALU.add, op1=ALU.add).then_inc(a_masked, 1)
                    dve.wait_ge(a_masked, l * NA + i + 1)
                    step(dve.tensor_reduce(sst[:, 0, i:i + 1], fsc[:, at:at + w], AX, ALU.max))
                    dve.tensor_scalar(sst[:, 1, i:i + 1], sst[:, 0, i:i + 1], -1.0, None, ALU.mult).then_inc(a_max, 1)
                    if i == 1:
                        dve.wait_ge(h_sq, l + 1)
                        dve.tensor_reduce(hst[:, 0, :], tmp1.rearrange("p (g c) -> p g c", g=8), AX, ALU.add).then_inc(h_sum, 1)
                    if i == 3:
                        dve.wait_ge(h_rms, l + 1)
                        dve.reciprocal(hst[:, 2, :], hst[:, 1, :]).then_inc(h_inv, 1)
                    if i == 14:
                        turn_out(turn_no(0, l, 2), (0, 1), (ACC, ACC + 2))
                dve.wait_ge(a_out, l * NA + NA)
                step(dve.reciprocal(sst[:, 4, :], sst[:, 2, :]))
                for t in range(TB):
                    dve.tensor_tensor(xn[:, t, 512:1024].rearrange("p (h d) -> p h d", h=X_HEADS),
                                      ps[:, ACC + 2 * t + 1, :].rearrange("p (h d) -> p h d", h=X_HEADS),
                                      sst[:, 4, :].rearrange("p (h t) -> p t h", t=TB)[:, t, :].unsqueeze(2).broadcast_to([P, X_HEADS, X_D]),
                                      ALU.mult).then_inc(xn_ready, 1)
                turn_out(turn_no(0, l, 2), (2, 3))
                dve.wait_ge(gain_loaded, 16 * norm_no(0, l, 2) + 16)
                for i in range(PIECES):
                    dve.scalar_tensor_tensor(out=piece(xn, i), in0=piece(memx, i), scalar=stat[:, 1, 2, i % 2:i % 2 + 1],
                                             in1=gain[:, i // 2 * 512:(i // 2 + 1) * 512], op0=ALU.mult, op1=ALU.mult).then_inc(xn_ready, 1)
                T3, T4 = turn_no(0, l, 3), turn_no(0, l, 4)
                turn_out(T3, (0, 1))
                for i in range(PIECES):
                    add(0, l, 1, i, A_OUT + 3, 1.0)
                turn_out(T3, (2, 3))
                for i in range(PIECES):
                    gained(add_no(0, l, 1), norm_no(0, l, 3), i)
                inverse(norm_no(0, l, 3))
                rms_diag(1.0)
                turn_out(T4, range(PIECES))
                for i, dst in enumerate((hg, fq)):
                    scaled_out(0, l, A_Q + 2 * i, PAIRS[(4 + i) % 3], row_no(0, l, 1), [(dst, C_D ** -0.5)])
                NC = C_HEADS * TB

                def heads_out(half):
                    a = half * NC // 2
                    dve.wait_ge(c_out, l * NC + a + NC // 2)
                    step(dve.reciprocal(sst[:, 4, a:a + NC // 2], sst[:, 2, a:a + NC // 2]))
                    for t in range(TB):
                        dve.tensor_tensor(piece(xn, 2 * half + t).rearrange("p (h d) -> p h d", d=C_D),
                                          ps[:, ACC + 2 * t + half, :].rearrange("p (h d) -> p h d", d=C_D),
                                          sst[:, 4, a:a + NC // 2].rearrange("p (h t) -> p t h", t=TB)[:, t, :].unsqueeze(2).broadcast_to([P, 2, C_D]),
                                          ALU.mult).then_inc(xn_ready, 1)

                for i in range(NC):
                    dve.wait_ge(c_score, l * NC + i + 1)
                    step(dve.tensor_reduce(sst[:, 0, i:i + 1], ps[:, TR + i % 2, 0:256], AX, ALU.max))
                    dve.tensor_scalar(sst[:, 1, i:i + 1], sst[:, 0, i:i + 1], -1.0, None, ALU.mult).then_inc(c_max, 1)
                    if i == NC - 2:
                        heads_out(0)
                turn_out(turn_no(0, l, 5), (0, 1), (ACC, ACC + 2))
                heads_out(1)
                turn_out(turn_no(0, l, 5), (2, 3))
                add_and_norm(0, l, 2, A_O + 3, 1.0, norm_no(0, l, 4), turn_no(0, l, 6))
                ffn(0, l, A_FFN2, 1, turn_no(0, l, 6), norm_no(0, l, 4))
                assert count[0] == V_A, ("V_A", count[0])

            def final_norm(n, then=None):
                inverse(n)
                for i in range(PIECES):
                    dve.tensor_scalar(piece(xres, i), piece(xn, i), stat[:, 0, 2, i % 2:i % 2 + 1], None, ALU.mult).then_inc(x_ready, 1)
                    if then:
                        then(i)

            final_norm(norm_no(0, DEPTH, 0), lambda i: gained(add_no(0, DEPTH, 0), norm_no(1, 0, 0), i))
            with dve.Fori(0, DEPTH) as l:
                step, count = stepper(dve, vstep, DEPTH * V_A + l * V_B)
                dve.tensor_copy(wpool_l[:, :, :].rearrange("p g c -> p (g c)"), wpool[:, bass.ds(l, 1), :, :].rearrange("p a g c -> p (a g c)"))
                step(dve.tensor_copy(pscale_l[:, :], pscale[:, bass.ds(l, 1), :].rearrange("p a k -> p (a k)")))
                dve.sem_inc(p_wl, 1)
                ffn(1, l, B_FFN1, 0, turn_no(1, l, 0), norm_no(1, l, 0))
                turn_out(turn_no(1, l, 1), (2, 3))
                inverse(norm_no(1, l, 1))
                rms_diag(-1.0)
                dve.wait_ge(loaded, N_LOADS * 16 + 16)
                wait_taken(dve, 1, l, 0)
                parts = []
                for t, tmp in enumerate((st1, st3)):
                    xx = qk_r[:, t * 512:(t + 1) * 512].rearrange("p (h d) -> p h d", h=8)
                    x1, x2 = xx[:, :, 0:32], xx[:, :, 32:64]
                    cos, sin = (con(n, t * 32, 32).unsqueeze(1).broadcast_to([P, 8, 32]) for n in ("cos", "sin"))
                    q = [tmp[:, n * 256:(n + 1) * 256].rearrange("p (h d) -> p h d", h=8) for n in range(4)]
                    for o, a, c in zip(q, (x1, x2, x2, x1), (cos, sin, cos, sin)):
                        last = dve.tensor_tensor(o, a, c, ALU.mult)
                    parts.append(q)
                step(last)
                for t, q in enumerate(parts):
                    rot = qk_rot[:, t * 512:(t + 1) * 512].rearrange("p (h d) -> p h d", h=8)
                    dve.tensor_tensor(rot[:, :, 0:32], q[0], q[1], ALU.subtract)
                    dve.tensor_tensor(rot[:, :, 32:64], q[2], q[3], ALU.add).then_inc(r_rot, 1)
                scaled_out(1, l, B_IN + 2, PAIRS[1], row_no(1, l, 0), [(qk_sb[:, 0:512], 64 ** -0.5), (qk_sb[:, 512:1024], 1.0)])
                zs = ps[:, 0:3, :].rearrange("p a c -> p (a c)")
                dve.wait_ge(r_turn, TB * (l + 1))
                dve.wait_ge(s_sp, l + 1)
                dve.scalar_tensor_tensor(out=st2, in0=zs, scalar=0.0, in1=st1, op0=ALU.min, op1=ALU.subtract)
                step(dve.scalar_tensor_tensor(out=st3, in0=zs, scalar=0.0, in1=st1, op0=ALU.max, op1=ALU.add))

                def masked(m):
                    strict = con("strict").unsqueeze(1).broadcast_to([P, 4, P])
                    a = m[:, 0:1024].rearrange("p (h o c) -> p h o c", h=4, o=2)[:, :, 0, :]
                    c = m[:, 1024:1536].rearrange("p (h c) -> p h c", h=4)
                    dve.tensor_tensor(a, a, strict, ALU.mult)
                    return dve.tensor_tensor(c, c, strict, ALU.mult)

                masked(st3).then_inc(s_fail, 1)
                dve.wait_ge(r_score, 2 * l + 2)
                dve.tensor_tensor(sc_r[:, 0:1024], ps[:, 0:2, :].rearrange("p a c -> p (a c)"), con("decay"), ALU.mult)
                dve.tensor_tensor(sc_r[:, 1024:1536].rearrange("p (h c) -> p h c", h=4), ps[:, 2, :].rearrange("p (h c) -> p h c", h=4),
                                  con("decay").rearrange("p (h o c) -> p h o c", h=4, o=2)[:, :, 0, :], ALU.mult).then_inc(r_dec, 1)
                dve.wait_ge(s_after, l + 1)
                dve.tensor_tensor(st2, st2, ps[:, 0:3, :].rearrange("p a c -> p (a c)"), ALU.add).then_inc(s_sum, 1)
                dve.wait_ge(s_exp, l + 1)
                masked(st2).then_inc(s_w, 1)
                dve.wait_ge(r_sq, l + 1)
                head_norm(qk_sb, v_r, r_sum, (r_rms, l + 1))
                dve.tensor_tensor(v_r, v_r, g_r, ALU.mult).then_inc(r_y, 1)
                dve.wait_ge(s_hi, l + 1)
                dve.tensor_tensor(hT_lo[:, :, 0:2, :].rearrange("p t k c -> p k t c"), ps[:, 3, :].rearrange("p (k t c) -> p k t c", k=2, t=TB),
                                  hT_hi[:, :, 0:2, :].rearrange("p t k c -> p k t c").bitcast(F32), ALU.subtract).then_inc(s_lo, 1)
                for t in range(TB):
                    dve.wait_ge(r_hi, l * TB + t + 1)
                    dve.tensor_tensor(hT_lo[:, t, 2:6, :].rearrange("p k c -> p (k c)"), ps[:, G + t, :],
                                      hT_hi[:, t, 2:6, :].rearrange("p k c -> p (k c)").bitcast(F32), ALU.subtract).then_inc(r_lo, 1)
                    if t == 0:
                        dve.wait_ge(p_hi, 2 * l + 2)
                        for k in range(2):
                            last = dve.scalar_tensor_tensor(out=hT_lo[:, :, 6 + k, :], in0=ps[:, 2, k * 256:(k + 1) * 256].rearrange("p (t c) -> p t c", t=TB),
                                                            scalar=pscale_l[:, k:k + 1], in1=hT_hi[:, :, 6 + k, :].bitcast(F32),
                                                            op0=ALU.mult, op1=ALU.subtract)
                        last.then_inc(p_lo, 1)

                def gated(out, n, bank, t):
                    return dve.tensor_tensor(out.rearrange("p (h c) -> p h c", h=2), ps[:, bank + 2 * t:bank + 2 * t + 2, :],
                                             gates[:, n * 2048:(n + 1) * 2048].rearrange("p (h t c) -> p t h c", h=2, t=TB)[:, t], ALU.mult)

                def tmp(t):
                    return br_tmp[:, t * DM:(t + 1) * DM]

                wait_unit(dve, 1, l, B_BR)
                for t in range(TB):
                    last = gated(xn[:, t, :], 0, 0, t)
                last.then_inc(br_used, 1)
                wait_unit(dve, 1, l, B_BR + 1)
                for t in range(TB):
                    last = gated(tmp(t), 2, 4, t)
                step(last)
                dve.wait_ge(br_used, 2 * l + 1)
                for t in range(TB):
                    last = dve.tensor_tensor(xn[:, t, :], xn[:, t, :], tmp(t), ALU.add)
                last.then_inc(br_used, 1)
                dve.wait_ge(br_used, 2 * l + 2)
                for i in range(PIECES):
                    h, t = divmod(i, 2)
                    if i < PIECES - 1:
                        dve.wait_ge(br_piece, (PIECES - 1) * l + i + 1)
                    else:
                        turn_out(turn_no(1, l, 2), (0, 1))
                        wait_unit(dve, 1, l, B_BR + 3)
                    step(dve.tensor_tensor(piece(br_tmp.rearrange("p (t d) -> p t d", t=TB), i), ps[:, 2 * t + h, :],
                                           gates[:, 2048 + i * 512:2048 + (i + 1) * 512], ALU.mult))
                    dve.tensor_tensor(piece(xn, i), piece(xn, i), piece(br_tmp.rearrange("p (t d) -> p t d", t=TB), i), ALU.add).then_inc(xn_ready, 1)
                turn_out(turn_no(1, l, 2), (2, 3))
                add_and_norm(1, l, 1, B_OUT + 3, 1.0, norm_no(1, l, 2), turn_no(1, l, 3))
                ffn(1, l, B_FFN2, 1, turn_no(1, l, 3), norm_no(1, l, 2))
                assert count[0] == V_B, ("V_B", count[0])
            final_norm(norm_no(1, DEPTH, 0))


FFN_NAMES = {(0, 0): ("ffn1_w_gate", "ffn1_w_up", "ffn1_w_down"), (0, 1): ("ffn2_w_gate", "ffn2_w_up", "ffn2_w_down"),
             (1, 0): ("w1_ffn1_2", "w3_ffn1_2", "w2_ffn1_2"), (1, 1): ("w1_ffn2_2", "w3_ffn2_2", "w2_ffn2_2")}
WEIGHTS = ("w_in", "w_out", "cross_wq", "cross_wk", "cross_wv", "cross_wo", "w_in_2", "w_branch_sb_2", "w_branch_ret_2",
           "w_branch_pool_2", "w_out_2")
NORM_ORDER = (("ffn1_norm", "mix_norm", "mem_norm", "cross_norm", "ffn2_norm"), ("g_ffn1_2", "g_mix_2", "g_ffn2_2"))


def kernel(**inputs):
    import concourse.bacc as bacc
    from concourse.bass_utils import run_bass_kernel_spmd

    a = {k: np.asarray(v) for k, v in inputs.items()}
    gains = []
    for names, last in zip(NORM_ORDER, ("final_norm", "g_final_2")):
        gains += [a[n][l] for l in range(DEPTH) for n in names] + [a[last]]
    table_a, table_b, eye = constants()
    small = dict(
        x=a["x"], mem=a["mem"], gains=np.stack(gains), table_a=table_a, table_b=table_b, eye=eye,
        lb=a["hgrn_lb"].reshape(DEPTH, H_HEADS, P).transpose(2, 0, 1), out_norm=a["hgrn_out_norm"],
        f_bias=a["fox_f_bias"].T, w_pool=a["w_pool_2"].transpose(2, 0, 1, 3),
        pool_scale=a["pool_scale_2"].reshape(DEPTH, 2, P).transpose(2, 0, 1))
    big = {n: a[n] for n in WEIGHTS} | {n: a[n] for names in FFN_NAMES.values() for n in names}
    nc = bacc.Bacc("TRN2", target_bir_lowering=False, num_devices=1)
    arrays, aps = {}, {}
    for name, v in (small | big).items():
        arrays["in_" + name] = np.ascontiguousarray(v)
        aps[name] = nc.dram_tensor("in_" + name, v.shape, mybir.dt.from_np(v.dtype), kind="ExternalInput").ap()
    out = nc.dram_tensor("out_0", (1, SEQ, DM), F32, kind="ExternalOutput").ap()
    W = {n: aps[n] for n in WEIGHTS}
    for (b, e), names in FFN_NAMES.items():
        for what, n in zip(("gate", "up", "down"), names):
            W[b, e, what] = aps[n]
    build(nc, *(aps[n] for n in small), W, out)
    r = run_bass_kernel_spmd(nc, [arrays], core_ids=[0])
    return r.results[0]["out_0"]
```
